# Optimizing a Trainium2 kernel written in Bass

```python
import math
import jax, jax.numpy as jnp
from jax import lax
import numpy as np

D_MODEL = 1024
BATCH = 1
SEQ = 1024
DEPTH = 2

MEM_LEN = 256
N_EVEN = (DEPTH + 1) // 2
N_ODD = DEPTH // 2
EPS = 1e-6
NEG = -1e30
Q_BLOCK = 128

HY_WIDTH = D_MODEL // 2
HY_ORDER = 2
HY_EMB = 33
HY_BANDS = (HY_EMB - 1) // 2
HY_FILT_HIDDEN = 64
HY_CONV = 3
HY_DECAY_TARGET = 1e-2
HY_FAST_PCT = 0.3
HY_SLOW_PCT = 1.5
HY_FILT_STD = 0.02
DIFF_WIDTH = D_MODEL // 2
DIFF_HEADS = 4
DIFF_HEAD_DIM = DIFF_WIDTH // DIFF_HEADS // 2
E_IN = 3 * HY_WIDTH + 3 * DIFF_WIDTH
E_MIX = HY_WIDTH + DIFF_WIDTH

WIN = 128
GQA_HEADS = 16
GQA_KV = 4
GQA_HD = 64
GQA_GROUP = GQA_HEADS // GQA_KV
O_Q = GQA_HEADS * GQA_HD
O_KV = GQA_KV * GQA_HD
O_IN = O_Q + 2 * O_KV

X_HEADS = 4
X_HD = 128
X_W = X_HEADS * X_HD

N_GROUPS = 4
EXP_PER_GROUP = 8
N_EXPERTS = N_GROUPS * EXP_PER_GROUP
TOP_K = 2
EXP_HIDDEN = 512
MOE_BLOCK = 128

kernel_name = 'hybrid_hyena_diffattn_swa_hmoe_encoder'

F32 = jnp.float32

def rmsnorm(x, g):
    x32 = x.astype(F32)
    y = x32 * lax.rsqrt(jnp.mean(x32 * x32, axis=-1, keepdims=True) + EPS)
    return (y * g.astype(F32)).astype(x.dtype)

def alibi_slopes(n):
    return 2.0 ** (-8.0 * jnp.arange(1, n + 1, dtype=F32) / n)

def short_conv3(u, w, b):
    up = jnp.pad(u, ((0, 0), (1, 1), (0, 0)))
    return up[:, :-2] * w[0] + up[:, 1:-1] * w[1] + up[:, 2:] * w[2] + b

def hyena_filters(L, w1, b1, w2, b2, w3, freq):
    pos = jnp.arange(L, dtype=F32)
    t = jnp.linspace(0.0, 1.0, L, dtype=F32)[:, None]
    bands = jnp.linspace(1e-4, HY_BANDS - 1, HY_BANDS, dtype=F32)[None]
    ang = bands * (2.0 * math.pi * pos[:, None] / L)
    z = jnp.concatenate([t, jnp.cos(ang), -jnp.sin(ang)], axis=-1)
    f = freq.astype(F32)
    a = jnp.sin(f * (z @ w1.astype(F32) + b1.astype(F32)))
    a = jnp.sin(f * (a @ w2.astype(F32) + b2.astype(F32)))
    h = (a @ w3.astype(F32)).reshape(L, HY_ORDER, 2, HY_WIDTH)
    max_decay = math.log(HY_DECAY_TARGET) / HY_FAST_PCT
    min_decay = math.log(HY_DECAY_TARGET) / HY_SLOW_PCT
    deltas = jnp.linspace(min_decay, max_decay, HY_WIDTH, dtype=F32)
    decay = jnp.exp(-t * jnp.abs(deltas))
    h = h * decay[:, None, None, :]
    k = jnp.concatenate([h[:, :, 0], jnp.zeros((1, HY_ORDER, HY_WIDTH), F32), h[:0:-1, :, 1]], axis=0)
    return jnp.fft.rfft(k, n=2 * L, axis=0)

def fft_conv(z, kf, bias):
    L = z.shape[1]
    z32 = z.astype(F32)
    zf = jnp.fft.rfft(z32, n=2 * L, axis=1)
    y = jnp.fft.irfft(zf * kf[None], n=2 * L, axis=1)[:, :L]
    return (y + z32 * bias.astype(F32)).astype(z.dtype)

def hyena_mixer(u, conv_w, conv_b, w1, b1, w2, b2, w3, freq, hy_bias):
    L = u.shape[1]
    u = short_conv3(u, conv_w, conv_b)
    v, g1, g2 = jnp.split(u, 3, axis=-1)
    kf = hyena_filters(L, w1, b1, w2, b2, w3, freq)
    z = g1 * fft_conv(v, kf[:, 0], hy_bias[0])
    z = g2 * fft_conv(z, kf[:, 1], hy_bias[1])
    return z

def diff_attention(q, k, v, lam, subln, layer_idx):
    B, S, _ = q.shape
    H, d = DIFF_HEADS, DIFF_HEAD_DIM
    nb = S // Q_BLOCK
    lam_init = 0.8 - 0.6 * math.exp(-0.3 * layer_idx)
    l32 = lam.astype(F32)
    lam_full = jnp.exp(jnp.sum(l32[0] * l32[1])) - jnp.exp(jnp.sum(l32[2] * l32[3])) + lam_init
    qb_all = q.reshape(B, nb, Q_BLOCK, 2 * H, d).transpose(1, 0, 2, 3, 4)
    k = k.reshape(B, S, 2 * H, d)
    v = v.reshape(B, S, H, 2 * d)
    slopes = jnp.repeat(alibi_slopes(H), 2)
    kpos = jnp.arange(S)
    scale = d ** -0.5

    def block(args):
        qb, j = args
        qpos = j * Q_BLOCK + jnp.arange(Q_BLOCK)
        dist = jnp.abs(qpos[:, None] - kpos[None]).astype(F32)
        s = jnp.einsum('bqhd,bkhd->bhqk', qb, k).astype(F32) * scale - slopes[:, None, None] * dist
        p = jax.nn.softmax(s, axis=-1).reshape(B, H, 2, Q_BLOCK, S)
        a = p[:, :, 0] - lam_full * p[:, :, 1]
        return jnp.einsum('bhqk,bkhe->bqhe', a.astype(v.dtype), v)

    o = lax.map(block, (qb_all, jnp.arange(nb)))
    o = o.transpose(1, 0, 2, 3, 4).reshape(B, S, H, 2 * d)
    o = rmsnorm(o, subln) * (1.0 - lam_init)
    return o.reshape(B, S, H * 2 * d)

def window_gqa(q, k, v, sink):
    B, S, _ = q.shape
    nb = S // Q_BLOCK
    span = Q_BLOCK + 2 * WIN
    qb_all = q.reshape(B, nb, Q_BLOCK, GQA_KV, GQA_GROUP, GQA_HD).transpose(1, 0, 2, 3, 4, 5)
    pad = ((0, 0), (WIN, WIN), (0, 0), (0, 0))
    kp = jnp.pad(k.reshape(B, S, GQA_KV, GQA_HD), pad)
    vp = jnp.pad(v.reshape(B, S, GQA_KV, GQA_HD), pad)
    slopes = alibi_slopes(GQA_HEADS).reshape(GQA_KV, GQA_GROUP)
    sink32 = sink.astype(F32).reshape(GQA_KV, GQA_GROUP)
    scale = GQA_HD ** -0.5

    def block(args):
        qb, j = args
        start = j * Q_BLOCK
        kb = lax.dynamic_slice_in_dim(kp, start, span, axis=1)
        vb = lax.dynamic_slice_in_dim(vp, start, span, axis=1)
        qpos = start + jnp.arange(Q_BLOCK)
        kpos = start - WIN + jnp.arange(span)
        rel = jnp.abs(qpos[:, None] - kpos[None])
        valid = (rel <= WIN) & (kpos >= 0)[None] & (kpos < S)[None]
        s = jnp.einsum('bqkgd,bckd->bkgqc', qb, kb).astype(F32) * scale - slopes[..., None, None] * rel.astype(F32)
        s = jnp.where(valid, s, NEG)
        sk = jnp.broadcast_to(sink32[None, :, :, None, None], s.shape[:-1] + (1,))
        p = jax.nn.softmax(jnp.concatenate([s, sk], axis=-1), axis=-1)[..., :-1]
        return jnp.einsum('bkgqc,bckd->bqkgd', p.astype(vb.dtype), vb)

    o = lax.map(block, (qb_all, jnp.arange(nb)))
    return o.transpose(1, 0, 2, 3, 4, 5).reshape(B, S, O_Q)

def cross_attention(h, memn, wq, wkv, wo):
    B, S, _ = h.shape
    M = memn.shape[1]
    q = (h @ wq).reshape(B, S, X_HEADS, X_HD)
    kv = (memn @ wkv).reshape(B, M, 2, X_HEADS, X_HD)
    s = jnp.einsum('bqhd,bkhd->bhqk', q, kv[:, :, 0]).astype(F32) * (X_HD ** -0.5)
    p = jax.nn.softmax(s, axis=-1)
    o = jnp.einsum('bhqk,bkhd->bqhd', p.astype(kv.dtype), kv[:, :, 1]).reshape(B, S, X_W)
    return o @ wo

def hier_moe(h, w_grp, b_grp, w_exp, b_exp, w_gate, w_up, w_down):
    B, S, D = h.shape
    N = B * S
    xf = h.reshape(N, D)
    g_logits = (xf @ w_grp + b_grp).astype(F32)
    g_prob = jax.nn.softmax(g_logits, axis=-1)
    g_sel = jnp.argmax(g_logits, axis=-1).astype(jnp.int32)
    g_gate = jnp.take_along_axis(g_prob, g_sel[:, None], axis=-1)
    e_logits = (xf @ w_exp + b_exp).astype(F32).reshape(N, N_GROUPS, EXP_PER_GROUP)
    e_logits = jnp.take_along_axis(e_logits, g_sel[:, None, None], axis=1)[:, 0]
    top_v, top_i = lax.top_k(e_logits, TOP_K)
    weights = g_gate * jax.nn.softmax(top_v, axis=-1)
    eid = (g_sel[:, None] * EXP_PER_GROUP + top_i).reshape(-1)
    tok = jnp.repeat(jnp.arange(N, dtype=jnp.int32), TOP_K)
    wt = weights.reshape(-1)
    P = N * TOP_K
    order = jnp.argsort(eid)
    s_eid, s_tok, s_wt = eid[order], tok[order], wt[order]
    counts = jnp.bincount(eid, length=N_EXPERTS)
    starts = jnp.cumsum(counts) - counts
    padded = (counts + MOE_BLOCK - 1) // MOE_BLOCK * MOE_BLOCK
    p_ends = jnp.cumsum(padded)
    p_starts = p_ends - padded
    dest = p_starts[s_eid] + (jnp.arange(P) - starts[s_eid])
    cap = P + N_EXPERTS * MOE_BLOCK
    nblk = cap // MOE_BLOCK
    buf_tok = jnp.full((cap,), N, jnp.int32).at[dest].set(s_tok)
    buf_wt = jnp.zeros((cap,), F32).at[dest].set(s_wt)
    blk_e = jnp.minimum(jnp.searchsorted(p_ends, jnp.arange(nblk) * MOE_BLOCK, side='right'), N_EXPERTS - 1)
    xpad = jnp.concatenate([xf, jnp.zeros((1, D), xf.dtype)], axis=0)
    xb = xpad[buf_tok].reshape(nblk, MOE_BLOCK, D)

    def expert_block(args):
        xblk, e = args
        a = xblk @ w_gate[e]
        b = xblk @ w_up[e]
        return (jax.nn.silu(a) * b) @ w_down[e]

    yb = lax.map(expert_block, (xb, blk_e)).reshape(cap, D)
    y = jnp.zeros((N + 1, D), F32).at[buf_tok].add(yb.astype(F32) * buf_wt[:, None])[:N]
    return y.astype(h.dtype).reshape(B, S, D)

def setup_inputs(seed: int = 0) -> dict:
    key = jax.random.key(seed)
    ks = iter(jax.random.split(key, 48))

    def nrm(shape, scale):
        return jax.random.normal(next(ks), shape, F32) * scale

    def gain(shape):
        return 1.0 + nrm(shape, 0.02)

    D = D_MODEL
    return {
        'x': nrm((BATCH, SEQ, D), 1.0),
        'mem': nrm((BATCH, MEM_LEN, D), 1.0),
        'e_norm': gain((N_EVEN, D)),
        'e_w_in': nrm((N_EVEN, D, E_IN), D ** -0.5),
        'e_conv_w': nrm((N_EVEN, HY_CONV, 3 * HY_WIDTH), HY_CONV ** -0.5),
        'e_conv_b': nrm((N_EVEN, 3 * HY_WIDTH), 0.02),
        'e_filt_w1': nrm((N_EVEN, HY_EMB, HY_FILT_HIDDEN), HY_EMB ** -0.5),
        'e_filt_b1': nrm((N_EVEN, HY_FILT_HIDDEN), 0.02),
        'e_filt_w2': nrm((N_EVEN, HY_FILT_HIDDEN, HY_FILT_HIDDEN), HY_FILT_HIDDEN ** -0.5),
        'e_filt_b2': nrm((N_EVEN, HY_FILT_HIDDEN), 0.02),
        'e_filt_w3': nrm((N_EVEN, HY_FILT_HIDDEN, HY_ORDER * 2 * HY_WIDTH), HY_FILT_STD),
        'e_filt_freq': gain((N_EVEN, HY_FILT_HIDDEN)),
        'e_hy_bias': nrm((N_EVEN, HY_ORDER, HY_WIDTH), 1.0),
        'e_lam': nrm((N_EVEN, 4, DIFF_HEAD_DIM), 0.1),
        'e_subln': gain((N_EVEN, 2 * DIFF_HEAD_DIM)),
        'e_w_out': nrm((N_EVEN, E_MIX, D), E_MIX ** -0.5),
        'o_norm': gain((N_ODD, D)),
        'o_w_in': nrm((N_ODD, D, O_IN), D ** -0.5),
        'o_sink': nrm((N_ODD, GQA_HEADS), 0.5),
        'o_w_out': nrm((N_ODD, O_Q, D), O_Q ** -0.5),
        'c_norm': gain((DEPTH, D)),
        'c_wq': nrm((DEPTH, D, X_W), D ** -0.5),
        'c_wkv': nrm((DEPTH, D, 2 * X_W), D ** -0.5),
        'c_wo': nrm((DEPTH, X_W, D), X_W ** -0.5),
        'f_norm': gain((DEPTH, D)),
        'f_w_grp': nrm((DEPTH, D, N_GROUPS), D ** -0.5),
        'f_b_grp': nrm((DEPTH, N_GROUPS), 0.01),
        'f_w_exp': nrm((DEPTH, D, N_EXPERTS), D ** -0.5),
        'f_b_exp': nrm((DEPTH, N_EXPERTS), 0.01),
        'f_w_gate': nrm((DEPTH, N_EXPERTS, D, EXP_HIDDEN), D ** -0.5),
        'f_w_up': nrm((DEPTH, N_EXPERTS, D, EXP_HIDDEN), D ** -0.5),
        'f_w_down': nrm((DEPTH, N_EXPERTS, EXP_HIDDEN, D), EXP_HIDDEN ** -0.5),
        'g_mem': gain((D,)),
        'g_final': gain((D,)),
    }

def reference(x, mem, e_norm, e_w_in, e_conv_w, e_conv_b, e_filt_w1, e_filt_b1, e_filt_w2, e_filt_b2,
              e_filt_w3, e_filt_freq, e_hy_bias, e_lam, e_subln, e_w_out, o_norm, o_w_in, o_sink, o_w_out,
              c_norm, c_wq, c_wkv, c_wo, f_norm, f_w_grp, f_b_grp, f_w_exp, f_b_exp, f_w_gate, f_w_up,
              f_w_down, g_mem, g_final):
    memn = rmsnorm(mem, g_mem)
    for i in range(DEPTH):
        j = i // 2
        if i % 2 == 0:
            h = rmsnorm(x, e_norm[j])
            proj = h @ e_w_in[j]
            hy_u, q, k, v = jnp.split(proj, [3 * HY_WIDTH, 3 * HY_WIDTH + DIFF_WIDTH,
                                             3 * HY_WIDTH + 2 * DIFF_WIDTH], axis=-1)
            y_hy = hyena_mixer(hy_u, e_conv_w[j], e_conv_b[j], e_filt_w1[j], e_filt_b1[j], e_filt_w2[j],
                               e_filt_b2[j], e_filt_w3[j], e_filt_freq[j], e_hy_bias[j])
            y_df = diff_attention(q, k, v, e_lam[j], e_subln[j], i)
            x = x + jnp.concatenate([y_hy, y_df], axis=-1) @ e_w_out[j]
        else:
            h = rmsnorm(x, o_norm[j])
            proj = h @ o_w_in[j]
            q, k, v = jnp.split(proj, [O_Q, O_Q + O_KV], axis=-1)
            x = x + window_gqa(q, k, v, o_sink[j]) @ o_w_out[j]
        h = rmsnorm(x, c_norm[i])
        x = x + cross_attention(h, memn, c_wq[i], c_wkv[i], c_wo[i])
        h = rmsnorm(x, f_norm[i])
        x = x + hier_moe(h, f_w_grp[i], f_b_grp[i], f_w_exp[i], f_b_exp[i], f_w_gate[i], f_w_up[i], f_w_down[i])
    return rmsnorm(x, g_final)


_drawn_inputs = setup_inputs


def setup_inputs(seed=0):
    import zlib

    import numpy as np

    out = dict(_drawn_inputs(seed))
    spreads = {}
    factors = {'e_lam': 3.001,
     'e_subln': 2.962,
     'o_norm': 5.515,
     'o_sink': 3.236,
     'c_norm': 5.828,
     'f_b_grp': 4.173,
     'f_b_exp': 3.563,
     'g_mem': 6.36,
     'g_final': 2.831}
    for name, (base, spread) in spreads.items():
        noise = np.random.default_rng([zlib.crc32(name.encode()), seed]).standard_normal(out[name].shape)
        drawn = base * np.exp(spread * noise) if base else spread * noise
        out[name] = __import__('jax').numpy.asarray(drawn.astype(out[name].dtype))
    for name, factor in factors.items():
        out[name] = (out[name] * factor).astype(out[name].dtype)
    return out
```

```python
from contextlib import ExitStack

import numpy as np
import concourse.bass as bass
from concourse import mybir
from concourse.alu_op_type import AluOpType as ALU

ACT = mybir.ActivationFunctionType
F32 = mybir.dt.float32
I32 = mybir.dt.int32
U32 = mybir.dt.uint32
AX_X = mybir.AxisListType.X

P = 128
S = 1024
D = 1024
NB = S // P
KC = D // P
BANK = 512
EPS = 1e-6
HW = 512
QT_N = 4
M_LEN = 256
XH = 4
NE = 32
NG = 4
EG = NE // NG
EH = 512
NBLK = 2 * S // P + NE
NSLOT = NBLK * P

X0 = 0
HT0 = X0 + NB * D
MT0 = HT0 + KC * S
ID0 = MT0 + KC * S
ST0 = ID0 + P
GB0 = ST0 + 256
ME0 = GB0 + D
W0 = ME0 + KC * M_LEN
TOTAL = 53200
WN = TOTAL - W0


class Steps:

    def __init__(self, sem):
        self.sem, self.k, self.i, self.per = sem, 0, None, 0

    def enter(self, i, per):
        self.i, self.per, self.k0 = i, per, self.k

    def leave(self, trips):
        assert self.k - self.k0 == self.per, (self.k - self.k0, self.per)
        self.k, self.i = self.k0 + trips * self.per, None

    def tick(self):
        self.k += 1
        return 1

    @property
    def n(self):
        return self.k if self.i is None else self.i * self.per + self.k


class Core:

    def __init__(self, nc, stack):
        self.nc = nc
        self.A = stack.enter_context(nc.sbuf_tensor("sbuf", [P, TOTAL], F32))
        self.PS = stack.enter_context(nc.psum_tensor("psum", [P, 8 * BANK], F32))
        self.pool_dma = iter([stack.enter_context(nc.semaphore(f"pool_dma{n}")) for n in range(23)])

    def a(self, at, n, p0=0, p1=P):
        return self.A[p0:p1, at:at + n]

    def dyn(self, at, n, p0=0, p1=P):
        return self.A[p0:p1, bass.ds(at, n)]

    def bank(self, b, n=BANK, p0=0, p1=P, at=0):
        return self.PS[p0:p1, b * BANK + at:b * BANK + at + n]

    def ident(self, n=P):
        return self.A[0:n, ID0:ID0 + n]


class Phase:

    def __init__(self, nc, name):
        self.nc, self.name = nc, name

    def __enter__(self):
        self.stack, self.sems = ExitStack(), []
        return self

    def sem(self, name):
        s = self.stack.enter_context(self.nc.semaphore(f"{self.name}_{name}"))
        self.sems.append(s)
        return s

    def pool_dma(self, m):
        return next(m.pool_dma)

    def block(self):
        return self.nc.Block()

    def __exit__(self, *exc):
        if exc[0] is None:
            for s in self.sems:
                self.nc.sync.sem_clear(s)
            self.nc.all_engine_barrier()
        self.stack.close()


def row(ap):
    n = ap.shape[0]
    return ap.rearrange("(a n) -> a n", a=1).to_broadcast([P, n])


def load_start(nc, m, d):
    with Phase(nc, "start") as ph:
        loaded = ph.sem("loaded")
        with ph.block() as block:
            @block.sync
            def _(sp):
                sp.dma_start(m.ident(), d["c_ident"]).then_inc(loaded, 16)
                sp.dma_start(m.a(X0, NB * D).rearrange("p (b n) -> p b n", b=NB),
                             d["x"][0].rearrange("(b p) n -> p b n", p=P)).then_inc(loaded, 16)
                sp.wait_ge(loaded, 32)


def norm_transpose(nc, m, name, gain, src, dst, nblk, stats=True, h_dram=None):
    ntok = nblk * P
    sums, rstd = m.a(ST0, nblk), m.a(ST0 + 8, nblk)
    h0 = W0
    sq0 = W0 + 2 * D
    with Phase(nc, name) as ph:
        loaded, squared, var_ok = ph.sem("loaded"), ph.sem("squared"), ph.sem("var_ok")
        rooted, dve, h_ready = ph.sem("rooted"), ph.sem("dve"), ph.sem("h_ready")
        turned, copied = ph.sem("turned"), ph.sem("copied")
        stored = [ph.sem("stored0"), ph.sem("stored1")]
        with ph.block() as block:
            @block.sync
            def _(sp):
                sp.dma_start(m.a(GB0, D), row(gain)).then_inc(loaded, 16)
                if h_dram is not None:
                    sp.sem_inc(stored[0], 16)
                    sp.sem_inc(stored[1], 16)
                    with sp.Fori(0, nblk // 2) as i:
                        for s in range(2):
                            sp.wait_ge(h_ready, 2 * i + s + 1)
                            sp.dma_start(h_dram[bass.ds((2 * i + s) * P, P), :],
                                         m.a(h0 + s * D, D)).then_inc(stored[s], 16)
                    for s in range(2):
                        sp.wait_ge(stored[s], 16 * (nblk // 2 + 1))

            @block.scalar
            def _(act):
                if stats:
                    for b in range(nblk):
                        if b >= 2:
                            act.wait_ge(squared, b - 1)
                        nc.scalar.activation(m.a(sq0 + (b % 2) * D, D), m.a(src + b * D, D), ACT.Square,
                                             accum_out=m.a(ST0 + b, 1)).then_inc(squared, 1)
                act.wait_ge(var_ok, 1)
                nc.scalar.activation(rstd, rstd, ACT.Sqrt).then_inc(rooted, 1)
                act.sem_inc(copied, 2)
                with act.Fori(0, nblk // 2) as i:
                    for s in range(2):
                        act.wait_ge(turned, 2 * i + s + 3)
                        out = m.dyn(dst + (2 * i + s) * P, (KC - 1) * ntok + P)
                        out = bass.AP(tensor=out.tensor, offset=out.offset,
                                      ap=[out.ap[0], [ntok, KC], [1, P]])
                        nc.scalar.activation(out, m.bank(2 * s, D).rearrange("p (c t) -> p c t", c=KC),
                                             ACT.Copy).then_inc(copied, 1)

            @block.vector
            def _(dve_e):
                if stats:
                    dve_e.wait_ge(squared, nblk)
                nc.vector.tensor_scalar(rstd, sums, 1.0 / D, EPS, ALU.mult, ALU.add).then_inc(var_ok, 1)
                dve_e.wait_ge(rooted, 1)
                nc.vector.reciprocal(rstd, rstd).then_inc(dve, 1)
                dve_e.wait_ge(dve, 1)
                dve_e.wait_ge(loaded, 16)
                with dve_e.Fori(0, nblk // 2) as i:
                    for s in range(2):
                        dve_e.wait_ge(turned, 2 * i + s + 1)
                        if h_dram is not None:
                            dve_e.wait_ge(stored[s], 16 * i + 16)
                        nc.vector.scalar_tensor_tensor(
                            out=m.a(h0 + s * D, D), in0=m.dyn(src + (2 * i + s) * D, D),
                            scalar=m.dyn(ST0 + 8 + 2 * i + s, 1), in1=m.a(GB0, D),
                            op0=ALU.mult, op1=ALU.mult).then_inc(h_ready, 1)

            @block.tensor
            def _(pe):
                pe.sem_inc(turned, 2)
                with pe.Fori(0, nblk // 2) as i:
                    for s in range(2):
                        pe.wait_ge(h_ready, 2 * i + s + 1)
                        pe.wait_ge(copied, 2 * i + s + 1)
                        for c in range(KC):
                            t = nc.tensor.transpose(m.bank(2 * s, P, at=c * P),
                                                    m.a(h0 + s * D + c * P, P), m.ident())
                        t.then_inc(turned, 1)


def project_add(nc, m, name, w, nfc, reload=None, gain=None, h_dram=None):
    ww = W0
    sq0 = W0 + nfc * D
    h0 = sq0 + 2 * D
    var0, rs0 = ST0 + 8, ST0 + 16
    with Phase(nc, name) as ph:
        w_in = [ph.sem(f"w_in{c}") for c in range(nfc)]
        x_in, summed, added, squared = ph.sem("x_in"), ph.sem("summed"), ph.sem("added"), ph.sem("squared")
        g_in, var_ok, rooted, dve_s = ph.sem("g_in"), ph.sem("var_ok"), ph.sem("rooted"), ph.sem("dve")
        h_ready, turned, copied, stored = ph.sem("h_ready"), ph.sem("turned"), ph.sem("copied"), ph.sem("stored")
        with ph.block() as block:
            @block.sync
            def _(sp):
                for c in range(nfc):
                    for p0, p1, rows in w(c):
                        sp.dma_start(m.a(ww + c * D, D, p0, p1), rows).then_inc(w_in[c], 16)
                    if c == 0 and reload is not None:
                        sp.dma_start(m.a(X0, NB * D).rearrange("p (b n) -> p b n", b=NB),
                                     reload.rearrange("(b p) n -> p b n", p=P)).then_inc(x_in, 16)
                if gain is not None:
                    sp.dma_start(m.a(GB0, D), row(gain)).then_inc(g_in, 16)
                if h_dram is not None:
                    for b in range(NB):
                        sp.wait_ge(h_ready, b + 1)
                        sp.dma_start(h_dram[b * P:(b + 1) * P, :],
                                     m.a(h0 + (b % 2) * D, D)).then_inc(stored, 16)
                        sp.wait_ge(stored, 16 * (b + 1))

            @block.tensor
            def _(pe):
                def product(c, blk):
                    for h in range(2):
                        t = nc.tensor.matmul(m.bank(2 * (blk % 4) + h), m.a(MT0 + c * S + blk * P, P),
                                             m.a(ww + c * D + h * BANK, BANK),
                                             start=(c == 0), stop=(c == nfc - 1))
                    if c == nfc - 1:
                        t.then_inc(summed, 1)

                def turn(blk):
                    pe.wait_ge(h_ready, blk + 1)
                    pe.wait_ge(added, 5 + blk % 2)
                    if blk >= 2:
                        pe.wait_ge(copied, blk - 1)
                    for c in range(KC):
                        t = nc.tensor.transpose(m.bank(2 * (blk % 2), P, at=c * P),
                                                m.a(h0 + (blk % 2) * D + c * P, P), m.ident())
                    t.then_inc(turned, 1)

                for c in range(nfc):
                    pe.wait_ge(w_in[c], 16 * len(w(c)))
                    for blk in range(4):
                        product(c, blk)
                for blk in range(4, NB):
                    pe.wait_ge(added, blk - 3)
                    for c in range(nfc):
                        product(c, blk)
                    if gain is not None and blk >= 6:
                        turn(blk - 6)
                if gain is not None:
                    for blk in range(2, NB):
                        turn(blk)

            @block.vector
            def _(dve):
                if reload is not None:
                    dve.wait_ge(x_in, 16)
                st = Steps(dve_s)

                def normalise(blk):
                    dve.wait_ge(squared, blk + 1)
                    nc.vector.tensor_scalar(m.a(var0 + blk, 1), m.a(ST0 + blk, 1), 1.0 / D, EPS,
                                            ALU.mult, ALU.add).then_inc(var_ok, 1)
                    dve.wait_ge(rooted, blk + 1)
                    nc.vector.reciprocal(m.a(rs0 + blk, 1), m.a(var0 + blk, 1)).then_inc(dve_s, st.tick())
                    dve.wait_ge(dve_s, st.n)
                    if blk == 0:
                        dve.wait_ge(g_in, 16)
                    if blk >= 2:
                        dve.wait_ge(turned, blk - 1)
                        if h_dram is not None:
                            dve.wait_ge(stored, 16 * (blk - 1))
                    nc.vector.scalar_tensor_tensor(
                        out=m.a(h0 + (blk % 2) * D, D), in0=m.a(X0 + blk * D, D), scalar=m.a(rs0 + blk, 1),
                        in1=m.a(GB0, D), op0=ALU.mult, op1=ALU.mult).then_inc(h_ready, 1)

                for blk in range(NB):
                    dve.wait_ge(summed, blk + 1)
                    x = m.a(X0 + blk * D, D)
                    nc.vector.tensor_tensor(x, m.bank(2 * (blk % 4), D), x, ALU.add).then_inc(added, 1)
                    if gain is not None and blk >= 4:
                        if blk - 4 < 2:
                            normalise(blk - 4)
                if gain is not None:
                    for blk in range(2, NB):
                        normalise(blk)

            @block.scalar
            def _(act):
                def root(blk):
                    act.wait_ge(var_ok, blk + 1)
                    v = m.a(var0 + blk, 1)
                    nc.scalar.activation(v, v, ACT.Sqrt).then_inc(rooted, 1)

                def copy(blk):
                    act.wait_ge(turned, blk + 1)
                    out = m.A[:, HT0 + blk * P:HT0 + blk * P + (KC - 1) * S + P]
                    out = bass.AP(tensor=out.tensor, offset=out.offset, ap=[out.ap[0], [S, KC], [1, P]])
                    nc.scalar.activation(out, m.bank(2 * (blk % 2), D).rearrange("p (c t) -> p c t", c=KC),
                                         ACT.Copy).then_inc(copied, 1)

                for blk in range(NB):
                    act.wait_ge(added, blk + 1)
                    if blk >= 2:
                        act.wait_ge(squared, blk - 1)
                    nc.scalar.activation(m.a(sq0 + (blk % 2) * D, D), m.a(X0 + blk * D, D), ACT.Square,
                                         accum_out=m.a(ST0 + blk, 1)).then_inc(squared, 1)
                    if gain is not None and blk in (4, 5):
                        root(blk - 4)
                if gain is not None:
                    copy(0)
                    for blk in range(2, NB):
                        root(blk)
                        copy(blk - 1)
                    copy(NB - 1)


FQ = 2 * 2 * 4 * P


def filter_taps(nc, m, d):
    z0 = W0
    a10, a20 = z0 + S, z0 + 2 * S
    u0, r0 = z0 + 3 * S, z0 + 4 * S
    w10 = z0 + 5 * S
    w20 = w10 + 64
    v0 = w20 + P
    w30 = v0 + 8
    dec0 = w30 + 4 * HW
    with Phase(nc, "taps") as ph:
        loaded, dec_in, sign_ok = ph.sem("loaded"), ph.sem("dec_in"), ph.sem("sign_ok")
        layer, arg, sined = ph.sem("layer"), ph.sem("arg"), ph.sem("sined")
        dve_s, h_sum, h_ok = ph.sem("dve"), ph.sem("h_sum"), ph.sem("h_ok")
        w3 = d["e_filt_w3"][0].rearrange("k (o q c) -> k o q c", o=2, q=2)
        with ph.block() as block:
            @block.sync
            def _(sp):
                sp.dma_start(m.a(z0, S, 0, 33), d["c_pos"]).then_inc(loaded, 16)
                sp.dma_start(m.a(w10, 64, 0, 33), d["e_filt_w1"][0]).then_inc(loaded, 16)
                for q in range(2):
                    sp.dma_start(m.a(w20 + 64 * q, 64, 0, 64), d["e_filt_w2"][0]).then_inc(loaded, 16)
                    for n, v in enumerate(("e_filt_b1", "e_filt_freq", "e_filt_b2")):
                        sp.dma_start(m.a(v0 + n, 1, 64 * q, 64 * q + 64),
                                     d[v][0].rearrange("(k o) -> k o", o=1)).then_inc(loaded, 16)
                    sp.dma_start(m.a(w30, 2 * HW, 64 * q, 64 * q + 64).rearrange("k (o c) -> k o c", o=2),
                                 w3[:, :, q, :]).then_inc(loaded, 16)
                sp.dma_start(m.a(v0 + 4, 1), d["c_sign"]).then_inc(loaded, 16)
                sp.dma_start(m.a(dec0, 8 * HW), d["c_decay"]).then_inc(dec_in, 16)

            @block.tensor
            def _(pe):
                pe.wait_ge(loaded, 16 * 13)
                for h in range(2):
                    t = nc.tensor.matmul(m.bank(h, p1=64), m.a(w10, 64, 0, 33),
                                         m.a(z0 + h * BANK, BANK, 0, 33), start=True, stop=True)
                t.then_inc(layer, 1)
                pe.wait_ge(sined, 1)
                for h in range(2):
                    t = nc.tensor.matmul(m.bank(2 + h), m.a(w20, P, 0, 64),
                                         m.a(a10 + h * BANK, BANK, 0, 64), start=True, stop=True)
                t.then_inc(layer, 1)
                pe.wait_ge(sign_ok, 2)
                for o in range(2):
                    for j in range(8):
                        for q in range(2):
                            n = 2 * (8 * o + j) + q
                            if n >= 4:
                                pe.wait_ge(h_ok, n - 3)
                            at = a20 + 2 * P * (j % 4) + j // 4
                            nc.tensor.matmul(m.bank(4 + n % 4), m.A[:, at:at + 2 * P - 1:2],
                                             m.a(w30 + (2 * q + o) * HW, HW),
                                             start=True, stop=True).then_inc(h_sum, 1)

            @block.scalar
            def _(act):
                for n, (to, p1) in enumerate(((a10, 64), (a20, P))):
                    act.wait_ge(arg, n + 1)
                    nc.scalar.activation(m.a(to, S, p1=p1), m.a(r0, S, p1=p1), ACT.Sin).then_inc(sined, 1)

            @block.vector
            def _(dve):
                st = Steps(dve_s)
                turn, big, hi = 2.0 * np.pi, 1.5 * 2.0 ** 23, 6.28125
                dve.wait_ge(loaded, 16 * 13)
                nc.vector.tensor_scalar(m.a(w30 + 2 * HW, 2 * HW), m.a(w30, 2 * HW), m.a(v0 + 4, 1), None,
                                        ALU.mult).then_inc(sign_ok, 1)
                for n in range(2):
                    p1 = 64 * (n + 1)
                    u, r = m.a(u0, S, p1=p1), m.a(r0, S, p1=p1)
                    dve.wait_ge(layer, n + 1)
                    nc.vector.tensor_scalar(u, m.bank(2 * n, S, p1=p1), m.a(v0 + 2 * n, 1, p1=p1),
                                            m.a(v0 + 1, 1, p1=p1), ALU.add, ALU.mult)\
                        .then_inc(dve_s, st.tick())
                    dve.wait_ge(dve_s, st.n)
                    nc.vector.tensor_scalar(r, u, float(1.0 / turn), big, ALU.mult, ALU.add)\
                        .then_inc(dve_s, st.tick())
                    dve.wait_ge(dve_s, st.n)
                    nc.vector.tensor_scalar(r, r, big, None, ALU.subtract).then_inc(dve_s, st.tick())
                    dve.wait_ge(dve_s, st.n)
                    nc.vector.scalar_tensor_tensor(out=u, in0=r, scalar=-hi, in1=u, op0=ALU.mult,
                                                   op1=ALU.add).then_inc(dve_s, st.tick())
                    dve.wait_ge(dve_s, st.n)
                    nc.vector.scalar_tensor_tensor(out=u, in0=r, scalar=float(hi - turn), in1=u,
                                                   op0=ALU.mult, op1=ALU.add).then_inc(dve_s, st.tick())
                    dve.wait_ge(dve_s, st.n)
                    nc.vector.tensor_scalar(r, u, 3.1415925, -3.1415925, ALU.min, ALU.max).then_inc(arg, 1)
                dve.wait_ge(sined, 2)
                nc.vector.memset(m.a(a20, 1, 64, P), 0.0).then_inc(sign_ok, 1)
                dve.wait_ge(dec_in, 16)
                for o in range(2):
                    for j in range(8):
                        for q in range(2):
                            n = 2 * (8 * o + j) + q
                            dve.wait_ge(h_sum, n + 1)
                            nc.vector.tensor_tensor(m.a((MT0, HT0)[o] + (8 * q + j) * HW, HW),
                                                    m.bank(4 + n % 4), m.a(dec0 + j * HW, HW),
                                                    ALU.mult).then_inc(h_ok, 1)


def filter_spectrum(nc, m, d, o, k_dram):
    taps = (MT0, HT0)[o]
    f0 = W0
    ko0 = f0 + 2 * FQ
    c0 = ko0 + 2 * FQ
    with Phase(nc, f"spectrum{o}") as ph:
        f_in = [ph.sem("f_in0"), ph.sem("f_in1")]
        dft, odd, k_ok = ph.sem("dft"), ph.sem("odd"), ph.sem("k_ok")
        k_out = [ph.sem("k_out0"), ph.sem("k_out1")]
        with ph.block() as block:
            @block.sync
            def _(sp):
                with sp.Fori(0, QT_N // 2) as i:
                    for s in range(2):
                        sp.wait_ge(dft, 2 * i + s + 1)
                        sp.dma_start(m.a(f0 + s * FQ, FQ), d["c_dft"][bass.ds(2 * i + s, 1), :, :]
                                     .rearrange("a p n -> (a p) n")).then_inc(f_in[s], 16)

            @block.tensor
            def _(pe):
                pe.sem_inc(dft, 2)
                with pe.Fori(0, QT_N // 2) as i:
                    for s in range(2):
                        pe.wait_ge(f_in[s], 16 * i + 16)
                        pe.wait_ge(k_ok, 2 * i + s + 1)
                        for cs in range(2):
                            for par in range(2):
                                for j in range(4):
                                    t = nc.tensor.matmul(
                                        m.bank(4 * s + 2 * cs + par),
                                        m.a(f0 + s * FQ + ((2 * cs + par) * 4 + j) * P, P),
                                        m.a(taps + (8 * cs + 4 * par + j) * HW, HW),
                                        start=(j == 0), stop=(j == 3))
                        t.then_inc(dft, 1)

            @block.scalar
            def _(act):
                act.sem_inc(k_out[0], 16)
                act.sem_inc(k_out[1], 16)
                with act.Fori(0, QT_N // 2) as i:
                    for s in range(2):
                        act.wait_ge(dft, 2 * i + s + 3)
                        odd_sums = m.bank(4 * s, 4 * BANK).rearrange("p (a b n) -> p a b n", a=2, b=2)
                        nc.scalar.activation(m.a(c0 + s * 2 * HW, 2 * HW).rearrange("p (a n) -> p a n", a=2),
                                             odd_sums[:, :, 1, :], ACT.Copy).then_inc(odd, 1)
                        act.wait_ge(k_ok, 2 * i + s + 3)
                        act.dma_start(k_dram[bass.ds(4 * o + 2 * i + s, 1), :, :]
                                      .rearrange("a p n -> (a p) n"),
                                      m.a(ko0 + s * FQ, FQ)).then_inc(k_out[s], 16)
                for s in range(2):
                    act.wait_ge(k_out[s], 16 * (QT_N // 2 + 1))

            @block.vector
            def _(dve):
                dve.sem_inc(k_ok, 2)
                with dve.Fori(0, QT_N // 2) as i:
                    for s in range(2):
                        dve.wait_ge(odd, 2 * i + s + 1)
                        dve.wait_ge(k_out[s], 16 * i + 16)
                        even = m.bank(4 * s, 4 * BANK).rearrange("p (a b n) -> p a b n", a=2, b=2)[:, :, 0, :]
                        odd_c = m.a(c0 + s * 2 * HW, 2 * HW).rearrange("p (a n) -> p a n", a=2)
                        k = m.a(ko0 + s * FQ, FQ).rearrange("p (a b n) -> p a b n", a=2, b=2)
                        nc.vector.tensor_tensor(k[:, :, 0, :], even, odd_c, ALU.add)
                        nc.vector.tensor_tensor(k[:, :, 1, :], even, odd_c, ALU.subtract).then_inc(k_ok, 1)


U0 = W0


def hyena_project(nc, m, d):
    w0 = U0 + 12 * S
    raw0 = w0 + 2 * KC * P
    cw0 = raw0 + 2 * S
    w_ap = d["e_w_in"][0].rearrange("(c p) n -> p c n", p=P)
    with Phase(nc, "hyproj") as ph:
        cw_in = ph.sem("cw_in")
        w_in = [ph.sem("w_in0"), ph.sem("w_in1")]
        summed, copied, conved, dve_s = ph.sem("summed"), ph.sem("copied"), ph.sem("conved"), ph.sem("dve")
        with ph.block() as block:
            @block.sync
            def _(sp):
                with nc.allow_non_contiguous_dma(reason="a few columns of taps and biases"):
                    for t in range(3):
                        sp.dma_start(m.a(cw0 + 12 * t, 12), d["e_conv_w"][0, t, :]
                                     .rearrange("(c p) -> p c", p=P)).then_inc(cw_in, 16)
                    sp.dma_start(m.a(cw0 + 36, 12), d["e_conv_b"][0]
                                 .rearrange("(c p) -> p c", p=P)).then_inc(cw_in, 16)
                with sp.Fori(0, 6) as i:
                    for s in range(2):
                        sp.wait_ge(summed, 2 * i + s + 1)
                        sp.dma_start(m.a(w0 + s * KC * P, KC * P).rearrange("p (c n) -> p c n", c=KC),
                                     w_ap[:, :, bass.ds((2 * i + s) * P, P)]).then_inc(w_in[s], 16)

            @block.tensor
            def _(pe):
                pe.sem_inc(summed, 2)
                with pe.Fori(0, 6) as i:
                    for s in range(2):
                        pe.wait_ge(w_in[s], 16 * i + 16)
                        pe.wait_ge(copied, 2 * i + s + 1)
                        for h in range(2):
                            for c in range(KC):
                                t = nc.tensor.matmul(m.bank(2 * s + h), m.a(w0 + (s * KC + c) * P, P),
                                                     m.a(HT0 + c * S + h * BANK, BANK),
                                                     start=(c == 0), stop=(c == KC - 1))
                        t.then_inc(summed, 1)

            @block.scalar
            def _(act):
                act.sem_inc(copied, 2)
                with act.Fori(0, 6) as i:
                    for s in range(2):
                        act.wait_ge(summed, 2 * i + s + 3)
                        act.wait_ge(conved, 2 * i + s + 1)
                        nc.scalar.activation(m.a(raw0 + s * S, S), m.bank(2 * s, S),
                                             ACT.Copy).then_inc(copied, 1)

            @block.vector
            def _(dve):
                dve.sem_inc(conved, 2)
                dve.wait_ge(cw_in, 64)
                st = Steps(dve_s)
                with dve.Fori(0, 6) as i:
                    st.enter(i, 4)
                    for s in range(2):
                        b = 2 * i + s
                        tap = lambda t: m.dyn(cw0 + 12 * t + b, 1)
                        dve.wait_ge(copied, b + 3)
                        nc.vector.tensor_scalar(m.dyn(U0 + b * S, S), m.a(raw0 + s * S, S), tap(1), tap(3),
                                                ALU.mult, ALU.add).then_inc(dve_s, st.tick())
                        dve.wait_ge(dve_s, st.n)
                        left = m.dyn(U0 + b * S + 1, S - 1)
                        nc.vector.scalar_tensor_tensor(out=left, in0=m.a(raw0 + s * S, S - 1),
                                                       scalar=tap(0), in1=left, op0=ALU.mult,
                                                       op1=ALU.add).then_inc(dve_s, st.tick())
                        dve.wait_ge(dve_s, st.n)
                        right = m.dyn(U0 + b * S, S - 1)
                        nc.vector.scalar_tensor_tensor(out=right, in0=m.a(raw0 + s * S + 1, S - 1),
                                                       scalar=tap(2), in1=right, op0=ALU.mult,
                                                       op1=ALU.add).then_inc(conved, 1)
                    st.leave(6)


def long_conv(nc, m, d, o, k_dram):
    zt0 = U0 + 12 * S
    xs0 = zt0 + 8 * HW
    bias0 = xs0 + FQ
    odd0 = bias0 + 8
    t0 = odd0 + 2 * HW
    assert t0 + 4 * HW <= TOTAL
    pr0 = HT0
    f0, k0 = X0, X0 + 2 * FQ
    g0 = MT0
    with Phase(nc, f"conv{o}") as ph:
        b_in = ph.sem("b_in")
        f_in = [ph.sem("f_in0"), ph.sem("f_in1")]
        k_in = [ph.sem("k_in0"), ph.sem("k_in1")]
        g_in = [ph.pool_dma(m), ph.pool_dma(m)]
        turned, time_ok, dft, odd = ph.sem("turned"), ph.sem("time_ok"), ph.sem("dft"), ph.sem("odd")
        xs_ok, y_ok, inv, gated, dve_s = ph.sem("xs_ok"), ph.sem("y_ok"), ph.sem("inv"), ph.sem("gated"), ph.sem("dve")
        with ph.block() as block:
            @block.sync
            def _(sp):
                with nc.allow_non_contiguous_dma(reason="a few columns of biases"):
                    sp.dma_start(m.a(bias0, 4), d["e_hy_bias"][0, o, :]
                                 .rearrange("(c p) -> p c", p=P)).then_inc(b_in, 16)
                with sp.Fori(0, QT_N // 2) as i:
                    for s in range(2):
                        sp.wait_ge(dft, 2 * i + s + 1)
                        sp.dma_start(m.a(f0 + s * FQ, FQ), d["c_dft"][bass.ds(2 * i + s, 1), :, :]
                                     .rearrange("a p n -> (a p) n")).then_inc(f_in[s], 16)
                        sp.wait_ge(y_ok, 2 * i + s + 1)
                        sp.dma_start(m.a(k0 + s * FQ, FQ), k_dram[bass.ds(4 * o + 2 * i + s, 1), :, :]
                                     .rearrange("a p n -> (a p) n")).then_inc(k_in[s], 16)

            @block.gpsimd
            def _(pool):
                for q in range(QT_N):
                    if q >= 2:
                        pool.wait_ge(inv, q - 1)
                    pool.dma_start(m.a(g0 + (q % 2) * FQ, FQ), d["c_idft"][q]).then_inc(g_in[q % 2], 16)

            @block.tensor
            def _(pe):
                pe.sem_inc(dft, 2)
                for j in range(8):
                    for c in range(4):
                        at = U0 + c * S + 2 * P * (j % 4) + j // 4
                        t = nc.tensor.transpose(m.bank(j, P, at=c * P), m.A[:, at:at + 2 * P - 1:2],
                                                m.ident())
                    t.then_inc(turned, 1)
                pe.wait_ge(time_ok, 8)
                with pe.Fori(0, QT_N // 2) as i:
                    for s in range(2):
                        pe.wait_ge(f_in[s], 16 * i + 16)
                        pe.wait_ge(xs_ok, 2 * i + s + 1)
                        for cs in range(2):
                            for par in range(2):
                                for j in range(4):
                                    t = nc.tensor.matmul(
                                        m.bank(4 * s + 2 * cs + par),
                                        m.a(f0 + s * FQ + ((2 * cs + par) * 4 + j) * P, P),
                                        m.a(zt0 + (4 * par + j) * HW, HW), start=(j == 0), stop=(j == 3))
                        t.then_inc(dft, 1)
                for q in range(QT_N):
                    pe.wait_ge(g_in[q % 2], 16 * (q // 2 + 1))
                    pe.wait_ge(y_ok, 2 + (q + 1 if q >= 1 else QT_N))
                    for c in range(4):
                        for par in range(2):
                            for cs in range(2):
                                t = nc.tensor.matmul(
                                    m.bank(2 * c + par),
                                    m.a(pr0 + q * FQ + (2 * cs + par) * HW + c * P, P),
                                    m.a(g0 + (q % 2) * FQ + (2 * cs + par) * HW, HW),
                                    start=(q == 0 and cs == 0), stop=(q == QT_N - 1 and cs == 1))
                    t.then_inc(inv, 1)

            @block.scalar
            def _(act):
                for j in range(8):
                    act.wait_ge(turned, j + 1)
                    nc.scalar.activation(m.a(zt0 + j * HW, HW), m.bank(j), ACT.Copy).then_inc(time_ok, 1)
                with act.Fori(0, QT_N // 2) as i:
                    for s in range(2):
                        act.wait_ge(dft, 2 * i + s + 3)
                        act.wait_ge(xs_ok, 2 * i + s + 2)
                        odd_sums = m.bank(4 * s, 4 * BANK).rearrange("p (a b n) -> p a b n", a=2, b=2)
                        nc.scalar.activation(m.a(odd0, 2 * HW).rearrange("p (a n) -> p a n", a=2),
                                             odd_sums[:, :, 1, :], ACT.Copy).then_inc(odd, 1)

            @block.vector
            def _(dve):
                dve.sem_inc(xs_ok, 2)
                dve.sem_inc(y_ok, 2)
                st = Steps(dve_s)
                with dve.Fori(0, QT_N // 2) as i:
                    st.enter(i, 14)
                    for s in range(2):
                        dve.wait_ge(odd, 2 * i + s + 1)
                        even = m.bank(4 * s, 4 * BANK).rearrange("p (a b n) -> p a b n", a=2, b=2)[:, :, 0, :]
                        odd_c = m.a(odd0, 2 * HW).rearrange("p (a n) -> p a n", a=2)
                        x = m.a(xs0, FQ).rearrange("p (a b n) -> p a b n", a=2, b=2)
                        nc.vector.tensor_tensor(x[:, :, 0, :], even, odd_c, ALU.add).then_inc(dve_s, st.tick())
                        nc.vector.tensor_tensor(x[:, :, 1, :], even, odd_c, ALU.subtract).then_inc(xs_ok, 1)
                        dve.wait_ge(k_in[s], 16 * i + 16)
                        dve.wait_ge(dve_s, st.n)
                        dve.wait_ge(xs_ok, 2 * i + s + 3)
                        xc, xs = m.a(xs0, 2 * HW), m.a(xs0 + 2 * HW, 2 * HW)
                        kc, ks = m.a(k0 + s * FQ, 2 * HW), m.a(k0 + s * FQ + 2 * HW, 2 * HW)
                        ta, tb = m.a(t0, 2 * HW), m.a(t0 + 2 * HW, 2 * HW)
                        dve.wait_ge(y_ok, 2 * i + s + 2)
                        nc.vector.tensor_tensor(ta, xc, kc, ALU.mult).then_inc(dve_s, st.tick())
                        nc.vector.tensor_tensor(tb, xs, ks, ALU.mult).then_inc(dve_s, st.tick())
                        dve.wait_ge(dve_s, st.n)
                        nc.vector.tensor_tensor(xc, xc, ks, ALU.mult).then_inc(dve_s, st.tick())
                        nc.vector.tensor_tensor(xs, xs, kc, ALU.mult).then_inc(dve_s, st.tick())
                        dve.wait_ge(dve_s, st.n)
                        nc.vector.tensor_tensor(ta, ta, tb, ALU.subtract).then_inc(dve_s, st.tick())
                        dve.wait_ge(dve_s, st.n)
                        nc.vector.tensor_tensor(tb, xc, xs, ALU.add).then_inc(dve_s, st.tick())
                        dve.wait_ge(dve_s, st.n)
                        y = m.a(t0, FQ).rearrange("p (a b n) -> p a b n", a=2, b=2)
                        pr = m.dyn(pr0 + (2 * i + s) * FQ, FQ).rearrange("p (a b n) -> p a b n", a=2, b=2)
                        nc.vector.tensor_tensor(pr[:, :, 0, :], y[:, :, 0, :], y[:, :, 1, :], ALU.add)
                        nc.vector.tensor_tensor(pr[:, :, 1, :], y[:, :, 0, :], y[:, :, 1, :],
                                                ALU.subtract).then_inc(y_ok, 1)
                    st.leave(QT_N // 2)
                dve.wait_ge(b_in, 16)
                dve.wait_ge(inv, QT_N)
                for c in range(4):
                    for par in range(2):
                        at = c * S + par
                        z = m.A[:, U0 + at:U0 + at + S - 1:2]
                        g = m.A[:, U0 + (4 * o + 4) * S + at:U0 + (4 * o + 4) * S + at + S - 1:2]
                        to = z if o == 0 else m.A[:, MT0 + at:MT0 + at + S - 1:2]
                        tmp = m.a(t0 + (par * 2) * HW, HW)
                        nc.vector.scalar_tensor_tensor(out=tmp, in0=z, scalar=m.a(bias0 + c, 1),
                                                       in1=m.bank(2 * c + par), op0=ALU.mult,
                                                       op1=ALU.add).then_inc(dve_s, st.tick())
                        dve.wait_ge(dve_s, st.n)
                        nc.vector.tensor_tensor(to, tmp, g, ALU.mult).then_inc(gated, 1)
def diff_attention(nc, m, d, y_dram):
    DW = 3 * 512
    w0 = W0
    q0 = w0 + 3 * KC * P
    k0, vt0, v0 = q0 + S, q0 + 2 * S, q0 + 3 * S
    mh0 = v0 + S
    MHN = 2 * S - P
    e0 = mh0 + MHN
    at0 = e0 + 4 * S
    oa0 = at0 + 2 * S
    sub0 = oa0 + S
    l0 = sub0 + P
    sm0 = l0 + 384
    sq0 = sm0 + 32
    zero0 = sq0 + P
    assert zero0 + D <= TOTAL
    lam_init = 0.8 - 0.6 * float(np.exp(-0.3 * 0))
    SCALE = 64 ** -0.5
    w_ap = d["e_w_in"][0].rearrange("(c p) n -> p c n", p=P)
    with Phase(nc, "diff") as ph:
        loaded = ph.sem("loaded")
        w_in = [ph.sem(f"w_in{t}") for t in range(3)]
        proj = [ph.sem(f"proj{t}") for t in range(3)]
        qkv_ok, v_turned, v_ok = ph.sem("qkv_ok"), ph.sem("v_turned"), ph.sem("v_ok")
        dve_s, lam_s, lam_e = ph.sem("dve"), ph.sem("lam_s"), ph.sem("lam_e")
        scored, maxed, neg_ok, exped = ph.sem("scored"), ph.sem("maxed"), ph.sem("neg_ok"), ph.sem("exped")
        a_ok, a_turned, at_ok = ph.sem("a_ok"), ph.sem("a_turned"), ph.sem("at_ok")
        pv, o_ok, var_ok, rooted = ph.sem("pv"), ph.sem("o_ok"), ph.sem("var_ok"), ph.sem("rooted")
        normed, o_turned, mixed = ph.sem("normed"), ph.sem("o_turned"), ph.sem("mixed")
        passed = ph.sem("passed")
        zeroed, cleared = ph.sem("zeroed"), ph.pool_dma(m)
        with ph.block() as block:
            @block.gpsimd
            def _(pool):
                first = 2 * S // P
                nc.gpsimd.memset(m.a(zero0, D), 0.0).then_inc(zeroed, 1)
                pool.wait_ge(zeroed, 1)
                with pool.Fori(first, NBLK) as j:
                    pool.dma_start(y_dram[bass.ds(j * P, P), :], m.a(zero0, D)).then_inc(cleared, 16)
                pool.wait_ge(cleared, 16 * (NBLK - first))

            @block.sync
            def _(sp):
                sp.dma_start(m.a(l0, 256), row(d["e_lam"][0].rearrange("a n -> (a n)"))).then_inc(loaded, 16)
                sp.dma_start(m.a(sub0, P), row(d["e_subln"][0])).then_inc(loaded, 16)
                sp.dma_start(m.a(mh0, MHN), d["c_dist"]).then_inc(loaded, 16)
                with sp.Fori(0, 4) as i:
                    for t in range(3):
                        sp.wait_ge(proj[t], i + 1)
                        sp.dma_start(m.a(w0 + t * KC * P, KC * P).rearrange("p (c n) -> p c n", c=KC),
                                     w_ap[:, :, bass.ds(i * P + DW + t * 512, P)]).then_inc(w_in[t], 16)

            @block.tensor
            def _(pe):
                for t in range(3):
                    pe.sem_inc(proj[t], 1)
                with pe.Fori(0, 4) as i:
                    for t, b in ((0, 4), (1, 6), (2, 0)):
                        pe.wait_ge(w_in[t], 16 * i + 16)
                        if t == 1:
                            pe.wait_ge(mixed, i + 1)
                        for h in range(2):
                            for c in range(KC):
                                x = nc.tensor.matmul(m.bank(b + h), m.a(w0 + (t * KC + c) * P, P),
                                                     m.a(HT0 + c * S + h * BANK, BANK),
                                                     start=(c == 0), stop=(c == KC - 1))
                        x.then_inc(proj[t], 1)
                    pe.wait_ge(qkv_ok, 3 * i + 3)
                    for j in range(NB):
                        x = nc.tensor.transpose(m.bank(2, P, at=j * P), m.a(vt0 + j * P, P), m.ident())
                    x.then_inc(v_turned, 1)
                    pe.wait_ge(v_ok, i + 1)

                    def scores(u):
                        for s in range(2):
                            pe.wait_ge(maxed, 16 * i + 2 * u + s + 1)
                            for h in range(2):
                                x = nc.tensor.matmul(m.bank(2 * s + h), m.a(q0 + u * P, P, 64 * s, 64 * s + 64),
                                                     m.a(k0 + h * BANK, BANK, 64 * s, 64 * s + 64),
                                                     start=True, stop=True)
                            x.then_inc(scored, 1)

                    scores(0)
                    for u in range(NB + 1):
                        if u >= 1:
                            pe.wait_ge(a_ok, 8 * i + u)
                            for j in range(NB):
                                x = nc.tensor.transpose(m.bank(4, P, at=j * P),
                                                        m.a(e0 + ((u - 1) % 2) * 2 * S + j * P, P), m.ident())
                            x.then_inc(a_turned, 1)
                        if u < NB - 1:
                            scores(u + 1)
                        if u >= 1:
                            pe.wait_ge(at_ok, 8 * i + u)
                            pe.wait_ge(o_ok, 8 * i + u)
                            for j in range(NB):
                                x = nc.tensor.matmul(m.bank(6, P),
                                                     m.a(at0 + ((u - 1) % 2) * S + j * P, P),
                                                     m.a(v0 + j * P, P), start=(j == 0), stop=(j == NB - 1))
                            x.then_inc(pv, 1)
                    pe.wait_ge(normed, i + 1)
                    for u in range(NB):
                        x = nc.tensor.transpose(m.bank(6, P, at=u * P), m.a(oa0 + u * P, P), m.ident())
                    x.then_inc(o_turned, 1)

            @block.scalar
            def _(act):
                act.wait_ge(lam_s, 1)
                nc.scalar.activation(m.a(l0 + 370, 2), m.a(l0 + 368, 2), ACT.Exp).then_inc(lam_e, 1)
                act.sem_inc(mixed, 1)
                act.sem_inc(o_ok, 1)
                with act.Fori(0, 4) as i:
                    for t, b, to in ((0, 4, q0), (1, 6, k0), (2, 0, vt0)):
                        act.wait_ge(proj[t], i + 2)
                        nc.scalar.activation(m.a(to, S), m.bank(b, S), ACT.Copy).then_inc(qkv_ok, 1)
                    act.wait_ge(v_turned, i + 1)
                    nc.scalar.activation(m.a(v0, S), m.bank(2, S), ACT.Copy).then_inc(v_ok, 1)
                    for u in range(NB + 1):
                        if u < NB:
                            for s in range(2):
                                e = m.a(e0 + (2 * (u % 2) + s) * S, S)
                                c = sm0 + 16 * (u % 2) + s
                                act.wait_ge(neg_ok, 16 * i + 2 * u + s + 1)
                                nc.scalar.activation(e, e, ACT.Exp, bias=m.a(c + 2, 1), scale=SCALE,
                                                     accum_out=m.a(c + 4, 1)).then_inc(exped, 1)
                        if u >= 1:
                            act.wait_ge(a_turned, 8 * i + u)
                            nc.scalar.activation(m.a(at0 + ((u - 1) % 2) * S, S), m.bank(4, S),
                                                 ACT.Copy).then_inc(at_ok, 1)
                            act.wait_ge(pv, 8 * i + u)
                            act.wait_ge(o_ok, 8 * i + u)
                            nc.scalar.activation(m.a(sq0, P), m.bank(6, P), ACT.Square,
                                                 accum_out=m.a(ST0 + 16 + u - 1, 1))
                            nc.scalar.activation(m.a(oa0 + (u - 1) * P, P), m.bank(6, P),
                                                 ACT.Copy).then_inc(o_ok, 1)
                    act.wait_ge(var_ok, i + 1)
                    nc.scalar.activation(m.a(ST0 + 24, NB), m.a(ST0 + 24, NB), ACT.Sqrt).then_inc(rooted, 1)
                    act.wait_ge(o_turned, i + 1)
                    nc.scalar.activation(m.dyn(MT0 + 4 * S + i * S, S), m.bank(6, S),
                                         ACT.Copy).then_inc(mixed, 1)

            @block.vector
            def _(dve):
                st = Steps(dve_s)

                def tick(x):
                    x.then_inc(dve_s, st.tick())
                    dve.wait_ge(dve_s, st.n)

                dve.sem_inc(maxed, 2)
                dve.wait_ge(loaded, 48)
                nc.vector.tensor_tensor(m.a(l0, 64), m.a(l0, 64), m.a(l0 + 64, 64), ALU.mult)
                tick(nc.vector.tensor_tensor(m.a(l0 + 128, 64), m.a(l0 + 128, 64), m.a(l0 + 192, 64), ALU.mult))
                nc.vector.reduce_sum(m.a(l0 + 368, 1), m.a(l0, 64), AX_X)
                nc.vector.reduce_sum(m.a(l0 + 369, 1), m.a(l0 + 128, 64), AX_X).then_inc(lam_s, 1)
                dve.wait_ge(lam_e, 1)
                neg_lam = m.a(l0 + 372, 1)
                nc.vector.tensor_scalar(m.a(sub0, P), m.a(sub0, P), 1.0 - lam_init, None, ALU.mult)
                tick(nc.vector.tensor_tensor(neg_lam, m.a(l0 + 371, 1), m.a(l0 + 370, 1), ALU.subtract))
                tick(nc.vector.tensor_scalar(neg_lam, neg_lam, -lam_init, None, ALU.add))
                with dve.Fori(0, 4) as i:
                    st.enter(i, 1 + 8 * 2 + 1 + 1)
                    tick(nc.vector.tensor_scalar(m.a(mh0, MHN), m.a(mh0, MHN), 0.25, None, ALU.mult))
                    for u in range(NB + 1):
                        if u < NB:
                            for s in range(2):
                                c = sm0 + 16 * (u % 2) + s
                                dve.wait_ge(scored, 16 * i + 2 * u + s + 1)
                                if s == 0 and u >= 2:
                                    dve.wait_ge(a_turned, 8 * i + u - 1)
                                dve.sem_inc(passed, 1)
                                nc.vector.tensor_tensor_reduce(
                                    m.a(e0 + (2 * (u % 2) + s) * S, S), m.a(mh0 + (NB - 1 - u) * P, S),
                                    m.bank(2 * s, S), 1.0, -3.0e38, ALU.add, ALU.max,
                                    m.a(c, 1)).then_inc(maxed, 1)
                                dve.wait_ge(maxed, 16 * i + 2 * u + s + 3)
                                nc.vector.tensor_scalar(m.a(c + 2, 1), m.a(c, 1), -SCALE, None,
                                                        ALU.mult).then_inc(neg_ok, 1)
                        if u >= 1:
                            c = sm0 + 16 * ((u - 1) % 2)
                            ea = e0 + 2 * ((u - 1) % 2) * S
                            dve.wait_ge(exped, 16 * i + 2 * u)
                            tick(nc.vector.reciprocal(m.a(c + 6, 2), m.a(c + 4, 2)))
                            tick(nc.vector.tensor_scalar(m.a(ea + S, S), m.a(ea + S, S), m.a(c + 7, 1),
                                                         neg_lam, ALU.mult, ALU.mult))
                            nc.vector.scalar_tensor_tensor(out=m.a(ea, S), in0=m.a(ea, S),
                                                           scalar=m.a(c + 6, 1), in1=m.a(ea + S, S),
                                                           op0=ALU.mult, op1=ALU.add).then_inc(a_ok, 1)
                    dve.wait_ge(o_ok, 8 * i + 9)
                    nc.vector.tensor_scalar(m.a(ST0 + 24, NB), m.a(ST0 + 16, NB), 1.0 / P, EPS,
                                            ALU.mult, ALU.add).then_inc(var_ok, 1)
                    dve.wait_ge(rooted, i + 1)
                    tick(nc.vector.reciprocal(m.a(ST0 + 24, NB), m.a(ST0 + 24, NB)))
                    for u in range(NB):
                        o = m.a(oa0 + u * P, P)
                        x = nc.vector.scalar_tensor_tensor(out=o, in0=o, scalar=m.a(ST0 + 24 + u, 1),
                                                           in1=m.a(sub0, P), op0=ALU.mult, op1=ALU.mult)
                    x.then_inc(normed, 1)
                    tick(nc.vector.memset(m.a(sm0 + 31, 1), 0.0))
                    st.leave(4)


def window_attention(nc, m, d):
    HD, HG, WINW = 64, 4, 3 * P
    NT = HG + 2
    w0 = W0
    q0 = w0 + NT * KC * P
    k0 = q0 + HG * S
    v0 = k0 + S
    mh0 = v0 + S
    e0 = mh0 + 2 * HG * WINW
    pt0 = e0 + 2 * 8 * WINW
    oa0 = pt0 + 2 * 2 * WINW
    sk0 = oa0 + 2 * 4 * P
    sm0 = sk0 + 32
    assert sm0 + 128 <= TOTAL, sm0 + 128 - TOTAL
    SCALE = HD ** -0.5
    w_ap = d["o_w_in"][0].rearrange("(c p) n -> p c n", p=P)
    STEPS = 2 * HG

    def keys(u):
        return max(u - 1, 0), min(u + 1, NB - 1)

    with Phase(nc, "gqa") as ph:
        loaded = ph.sem("loaded")
        w_in = [ph.sem(f"w_in{t}") for t in range(NT)]
        proj = [ph.sem(f"proj{t}") for t in range(NT)]
        qkv_ok, v_turned, v_ok = ph.sem("qkv_ok"), ph.sem("v_turned"), ph.sem("v_ok")
        dve_s, scored, maxed, neg_ok = ph.sem("dve"), ph.sem("scored"), ph.sem("maxed"), ph.sem("neg_ok")
        exped, p_turned, pt_ok, pv = ph.sem("exped"), ph.sem("p_turned"), ph.sem("pt_ok"), ph.sem("pv")
        o_ok, o_turned, mixed, sink_e = ph.sem("o_ok"), ph.sem("o_turned"), ph.sem("mixed"), ph.sem("sink_e")
        passed = ph.sem("passed")
        vt = q0
        with ph.block() as block:
            @block.sync
            def _(sp):
                sp.dma_start(m.a(sk0, 16), row(d["o_sink"][0])).then_inc(loaded, 16)
                sp.dma_start(m.a(mh0, 2 * HG * WINW), d["c_window"]).then_inc(loaded, 16)
                with sp.Fori(0, 2) as i:
                    for t in (5, 4, 0, 1, 2, 3):
                        sp.wait_ge(proj[t], i + 1)
                        if t < HG:
                            for g in range(2):
                                sp.dma_start(m.a(w0 + t * KC * P, KC * P)
                                             .rearrange("p (c n) -> p c n", c=KC)[:, :, 64 * g:64 * g + 64],
                                             w_ap[:, :, bass.ds(i * 512 + g * 256 + t * 64, 64)])\
                                    .then_inc(w_in[t], 16)
                        else:
                            sp.dma_start(m.a(w0 + t * KC * P, KC * P).rearrange("p (c n) -> p c n", c=KC),
                                         w_ap[:, :, bass.ds(i * P + 1024 + (t - 4) * 256, P)])\
                                .then_inc(w_in[t], 16)

            @block.tensor
            def _(pe):
                for t in range(NT):
                    pe.sem_inc(proj[t], 1)
                with pe.Fori(0, 2) as i:
                    def project(t, b):
                        pe.wait_ge(w_in[t], (32 if t < HG else 16) * (i + 1))
                        for h in range(2):
                            for c in range(KC):
                                x = nc.tensor.matmul(m.bank(b + h), m.a(w0 + (t * KC + c) * P, P),
                                                     m.a(HT0 + c * S + h * BANK, BANK),
                                                     start=(c == 0), stop=(c == KC - 1))
                        x.then_inc(proj[t], 1)

                    pe.wait_ge(mixed, 8 * i + 1)
                    project(5, 0)
                    project(4, 2)
                    project(0, 4)
                    project(1, 6)
                    pe.wait_ge(qkv_ok, 6 * i + 1)
                    for j in range(NB):
                        x = nc.tensor.transpose(m.bank(0, P, at=j * P), m.a(vt + j * P, P), m.ident())
                    x.then_inc(v_turned, 1)
                    pe.wait_ge(qkv_ok, 6 * i + 2)
                    project(2, 2)
                    pe.wait_ge(v_ok, i + 1)
                    project(3, 0)
                    pe.wait_ge(qkv_ok, 6 * i + 6)

                    def scores(n):
                        j, u0 = n // 2, 4 * (n % 2)
                        for u in range(u0, u0 + 4):
                            a, z = keys(u)
                            for s in range(2):
                                pe.wait_ge(maxed, 64 * i + 8 * n + 2 * (u - u0) + s + 1)
                                nc.tensor.matmul(m.bank(2 * (u % 2) + s, (z - a + 1) * P),
                                                 m.a(q0 + j * S + u * P, P, 64 * s, 64 * s + 64),
                                                 m.a(k0 + a * P, (z - a + 1) * P, 64 * s, 64 * s + 64),
                                                 start=True, stop=True).then_inc(scored, 1)

                    def turn_probs(n, u, s):
                        a, z = keys(u)
                        k = 8 * n + 2 * (u % 4) + s
                        pe.wait_ge(exped, 64 * i + k + 1)
                        pe.wait_ge(pt_ok, 64 * i + k + 1)
                        for b in range(z - a + 1):
                            x = nc.tensor.transpose(
                                m.bank(4 + s, P, at=b * P),
                                m.a(e0 + (n % 2) * 8 * WINW + (2 * (u % 4) + s) * WINW + b * P, P),
                                m.ident())
                        x.then_inc(p_turned, 1)

                    def weigh(n, u, s):
                        a, z = keys(u)
                        k = 8 * n + 2 * (u % 4) + s
                        pe.wait_ge(pt_ok, 64 * i + k + 3)
                        if k % 8 == 0:
                            pe.wait_ge(o_ok, 8 * i + n + 1)
                        for b in range(z - a + 1):
                            x = nc.tensor.matmul(
                                m.bank(6, HD, at=(u % 4) * P + s * HD),
                                m.a(pt0 + ((u % 2) * 2 + s) * WINW + b * P, P),
                                m.a(v0 + (a + b) * P + s * HD, HD),
                                start=(b == 0), stop=(b == z - a))
                        x.then_inc(pv, 1)

                    def outputs(n):
                        u0 = 4 * (n % 2)
                        for u in range(u0, u0 + 5):
                            for s in range(2):
                                if u < u0 + 4:
                                    turn_probs(n, u, s)
                                if u > u0:
                                    weigh(n, u - 1, s)

                    def turn_outputs(n):
                        pe.wait_ge(o_ok, 8 * i + n + 2)
                        pe.wait_ge(mixed, 8 * i + n + 1)
                        for u in range(4):
                            x = nc.tensor.transpose(m.bank(7, P, at=u * P),
                                                    m.a(oa0 + (n % 2) * 4 * P + u * P, P), m.ident())
                        x.then_inc(o_turned, 1)

                    scores(0)
                    for n in range(STEPS):
                        if n + 1 < STEPS:
                            scores(n + 1)
                        outputs(n)
                        if n >= 1:
                            turn_outputs(n - 1)
                    turn_outputs(STEPS - 1)

            @block.scalar
            def _(act):
                act.sem_inc(mixed, 1)
                act.sem_inc(pt_ok, 2)
                with act.Fori(0, 2) as i:
                    act.wait_ge(proj[5], i + 2)
                    nc.scalar.activation(m.a(vt, S), m.bank(0, S), ACT.Copy).then_inc(qkv_ok, 1)
                    act.wait_ge(proj[4], i + 2)
                    nc.scalar.activation(m.a(k0, S), m.bank(2, S), ACT.Copy).then_inc(qkv_ok, 1)
                    act.wait_ge(v_turned, i + 1)
                    nc.scalar.activation(m.a(v0, S), m.bank(0, S), ACT.Copy).then_inc(v_ok, 1)
                    for t, b in ((0, 4), (1, 6), (2, 2), (3, 0)):
                        act.wait_ge(proj[t], i + 2)
                        nc.scalar.activation(m.a(q0 + t * S, S), m.bank(b, S), ACT.Copy).then_inc(qkv_ok, 1)

                    def exps(n):
                        act.wait_ge(neg_ok, 8 * i + n + 1)
                        u0 = 4 * (n % 2)
                        c = sm0 + 64 * (n % 2)
                        nc.scalar.activation(m.a(c + 24, 8), m.a(c + 24, 8), ACT.Exp).then_inc(sink_e, 1)
                        for u in range(u0, u0 + 4):
                            a, z = keys(u)
                            for s in range(2):
                                k = 2 * (u - u0) + s
                                e = m.a(e0 + (n % 2) * 8 * WINW + k * WINW, (z - a + 1) * P)
                                nc.scalar.activation(e, e, ACT.Exp, bias=m.a(c + 8 + k, 1), scale=SCALE,
                                                     accum_out=m.a(c + 16 + k, 1)).then_inc(exped, 1)

                    def moves(n):
                        u0 = 4 * (n % 2)
                        for u in range(u0, u0 + 4):
                            a, z = keys(u)
                            for s in range(2):
                                k = 8 * n + 2 * (u - u0) + s
                                act.wait_ge(p_turned, 64 * i + k + 1)
                                nc.scalar.activation(m.a(pt0 + ((u % 2) * 2 + s) * WINW, (z - a + 1) * P),
                                                     m.bank(4 + s, (z - a + 1) * P),
                                                     ACT.Copy).then_inc(pt_ok, 1)

                    def mix(n):
                        act.wait_ge(o_turned, 8 * i + n + 1)
                        nc.scalar.activation(m.dyn(MT0 + i * 4 * S + (n // 2) * S + (n % 2) * BANK, BANK),
                                             m.bank(7), ACT.Copy).then_inc(mixed, 1)

                    exps(0)
                    for n in range(STEPS):
                        moves(n)
                        if n + 1 < STEPS:
                            exps(n + 1)
                        if n >= 1:
                            mix(n - 1)
                    mix(STEPS - 1)

            @block.vector
            def _(dve):
                st = Steps(dve_s)

                def tick(x):
                    x.then_inc(dve_s, st.tick())
                    dve.wait_ge(dve_s, st.n)

                dve.sem_inc(maxed, 4)
                dve.sem_inc(o_ok, 1)
                dve.wait_ge(loaded, 32)
                with dve.Fori(0, 2) as i:
                    st.enter(i, 2 + STEPS * 3)
                    tick(nc.vector.tensor_scalar(m.a(sk0 + 16, 8), m.dyn(sk0 + i * 8, 8), 1.0 / SCALE, None,
                                                 ALU.mult))

                    def head(n):
                        j, u0 = n // 2, 4 * (n % 2)
                        c = sm0 + 64 * (n % 2)
                        if n >= 2:
                            dve.wait_ge(p_turned, 64 * i + 8 * (n - 1))
                        for u in range(u0, u0 + 4):
                            a, z = keys(u)
                            for s in range(2):
                                k = 2 * (u - u0) + s
                                w = (z - a + 1) * P
                                dve.wait_ge(scored, 64 * i + 8 * n + k + 1)
                                dve.sem_inc(passed, 1)
                                nc.vector.tensor_tensor_reduce(
                                    m.a(e0 + (n % 2) * 8 * WINW + k * WINW, w),
                                    m.a(mh0 + (2 * j + s) * WINW + (a - u + 1) * P, w),
                                    m.bank(2 * (u % 2) + s, w), 1.0, -3.0e38, ALU.add, ALU.max,
                                    m.a(c + k, 1)).then_inc(maxed, 1)
                        dve.wait_ge(maxed, 64 * i + 8 * n + 8 + 4)
                        mx = m.a(c, 8).rearrange("p (u s) -> p u s", s=2)
                        for s in range(2):
                            x = nc.vector.tensor_scalar(mx[:, :, s], mx[:, :, s], m.a(sk0 + 16 + 4 * s + j, 1),
                                                        None, ALU.max)
                        tick(x)
                        for s in range(2):
                            x = nc.vector.tensor_scalar(m.a(c + 24, 8).rearrange("p (u s) -> p u s", s=2)[:, :, s],
                                                        mx[:, :, s], m.a(sk0 + 16 + 4 * s + j, 1), -SCALE,
                                                        ALU.subtract, ALU.mult)
                        nc.vector.tensor_scalar(m.a(c + 8, 8), m.a(c, 8), -SCALE, None,
                                                ALU.mult).then_inc(neg_ok, 1)

                    def tail(n):
                        c = sm0 + 64 * (n % 2)
                        dve.wait_ge(exped, 64 * i + 8 * n + 8)
                        dve.wait_ge(sink_e, 8 * i + n + 1)
                        tick(nc.vector.tensor_tensor(m.a(c + 16, 8), m.a(c + 16, 8), m.a(c + 24, 8), ALU.add))
                        tick(nc.vector.reciprocal(m.a(c + 16, 8), m.a(c + 16, 8)))
                        dve.wait_ge(pv, 64 * i + 8 * n + 8)
                        nc.vector.tensor_tensor(
                            m.a(oa0 + (n % 2) * 4 * P, 4 * P).rearrange("p (k e) -> p k e", k=8),
                            m.bank(6, 4 * P).rearrange("p (k e) -> p k e", k=8),
                            m.a(c + 16, 8).rearrange("p (k o) -> p k o", o=1).to_broadcast([P, 8, HD]),
                            ALU.mult).then_inc(o_ok, 1)

                    head(0)
                    for n in range(STEPS):
                        if n + 1 < STEPS:
                            head(n + 1)
                        tail(n)
                    tick(nc.vector.tensor_scalar(m.a(mh0, 2 * HG * WINW), m.a(mh0, 2 * HG * WINW), 0.0625, None,
                                                 ALU.mult))
                    st.leave(2)
def cross_attention(nc, m, d, layer):
    w0 = W0
    q0 = w0 + 6 * KC * P
    k0 = q0 + 2 * S
    v0 = k0 + 2 * M_LEN
    e0 = v0 + 2 * M_LEN
    pt0 = e0 + 2 * NB * M_LEN
    sm0 = pt0 + 2 * S
    assert sm0 + 48 <= TOTAL
    SCALE = 128 ** -0.5
    wq = d["c_wq"][layer].rearrange("(c p) n -> p c n", p=P)
    wkv = d["c_wkv"][layer].rearrange("(c p) n -> p c n", p=P)
    with Phase(nc, f"cross{layer}") as ph:
        w_in = [[ph.sem(f"w{t}_in{s}") for s in range(2)] for t in "qkv"]
        qp, kp, vp, kv_ok, q_ok = ph.sem("qp"), ph.sem("kp"), ph.sem("vp"), ph.sem("kv_ok"), ph.sem("q_ok")
        scored, neg_ok, exped, p_ok = ph.sem("scored"), ph.sem("neg_ok"), ph.sem("exped"), ph.sem("p_ok")
        p_turned, pt_ok, pv, mixed, dve_s = ph.sem("p_turned"), ph.sem("pt_ok"), ph.sem("pv"), ph.sem("mixed"), ph.sem("dve")
        with ph.block() as block:
            @block.sync
            def _(sp):
                for h in range(XH):
                    s = h % 2
                    for t, w in enumerate((wq[:, :, h * P:(h + 1) * P], wkv[:, :, h * P:(h + 1) * P],
                                           wkv[:, :, (XH + h) * P:(XH + h + 1) * P])):
                        if h >= 2:
                            sp.wait_ge((qp, kp, vp)[t], h - 1)
                        sp.dma_start(m.a(w0 + (3 * s + t) * KC * P, KC * P)
                                     .rearrange("p (c n) -> p c n", c=KC), w).then_inc(w_in[t][s], 16)

            @block.tensor
            def _(pe):
                def project(h):
                    s = h % 2
                    w = lambda t, c: w0 + ((3 * s + t) * KC + c) * P
                    for t in range(3):
                        pe.wait_ge(w_in[t][s], 16 * (h // 2 + 1))
                        if h >= 1 and t == 0:
                            pe.wait_ge(kv_ok, 2 * h)
                        if h >= 2 and t == 0:
                            pe.wait_ge(pt_ok, 2 * (h - 1))
                        if t == 0:
                            for b in range(2):
                                for c in range(KC):
                                    x = nc.tensor.matmul(m.bank(b), m.a(w(0, c), P),
                                                         m.a(HT0 + c * S + b * BANK, BANK),
                                                         start=(c == 0), stop=(c == KC - 1))
                            x.then_inc(qp, 1)
                        elif t == 1:
                            for c in range(KC):
                                x = nc.tensor.matmul(m.bank(6, M_LEN), m.a(w(1, c), P),
                                                     m.a(ME0 + c * M_LEN, M_LEN),
                                                     start=(c == 0), stop=(c == KC - 1))
                            x.then_inc(kp, 1)
                        else:
                            for b in range(2):
                                for c in range(KC):
                                    x = nc.tensor.matmul(m.bank(7, P, at=b * P),
                                                         m.a(ME0 + c * M_LEN + b * P, P), m.a(w(2, c), P),
                                                         start=(c == 0), stop=(c == KC - 1))
                            x.then_inc(vp, 1)

                def scores(h):
                    s = h % 2
                    pe.wait_ge(q_ok, h + 1)
                    pe.wait_ge(kv_ok, 2 * h + 1)
                    if h >= 1:
                        pe.wait_ge(mixed, h)
                    for u in range(NB):
                        x = nc.tensor.matmul(m.bank(2 + u // 2, M_LEN, at=(u % 2) * M_LEN),
                                             m.a(q0 + s * S + u * P, P), m.a(k0 + s * M_LEN, M_LEN),
                                             start=True, stop=True)
                    x.then_inc(scored, 1)

                def outputs(h):
                    s = h % 2
                    pe.wait_ge(p_ok, h + 1)
                    pe.wait_ge(kv_ok, 2 * min(h + 2, XH))
                    pe.wait_ge(q_ok, min(h + 2, XH))
                    for b in range(2):
                        for u in range(NB):
                            x = nc.tensor.transpose(m.bank(6 * b, P, at=u * P),
                                                    m.a(e0 + (s * NB + u) * M_LEN + b * P, P), m.ident())
                        x.then_inc(p_turned, 1)
                    pe.wait_ge(pt_ok, 2 * h + 2)
                    for half in range(2):
                        for b in range(2):
                            x = nc.tensor.matmul(m.bank(2 + half), m.a(v0 + s * M_LEN + b * P, P),
                                                 m.a(pt0 + b * S + half * BANK, BANK),
                                                 start=(b == 0), stop=(b == 1))
                    x.then_inc(pv, 1)

                project(0)
                scores(0)
                for h in range(XH):
                    if h + 1 < XH:
                        project(h + 1)
                    outputs(h)
                    if h + 1 < XH:
                        scores(h + 1)

            @block.scalar
            def _(act):
                def copies(h):
                    s = h % 2
                    act.wait_ge(qp, h + 1)
                    nc.scalar.activation(m.a(q0 + s * S, S), m.bank(0, S), ACT.Copy).then_inc(q_ok, 1)
                    act.wait_ge(kp, h + 1)
                    nc.scalar.activation(m.a(k0 + s * M_LEN, M_LEN), m.bank(6, M_LEN),
                                         ACT.Copy).then_inc(kv_ok, 1)
                    act.wait_ge(vp, h + 1)
                    nc.scalar.activation(m.a(v0 + s * M_LEN, M_LEN), m.bank(7, M_LEN),
                                         ACT.Copy).then_inc(kv_ok, 1)

                copies(0)
                for h in range(XH):
                    s = h % 2
                    c = sm0 + 24 * s
                    act.wait_ge(neg_ok, h + 1)
                    for u in range(NB):
                        x = nc.scalar.activation(m.a(e0 + (s * NB + u) * M_LEN, M_LEN),
                                                 m.bank(2 + u // 2, M_LEN, at=(u % 2) * M_LEN), ACT.Exp,
                                                 bias=m.a(c + 8 + u, 1), scale=SCALE,
                                                 accum_out=m.a(c + 16 + u, 1))
                    x.then_inc(exped, 1)
                    if h + 1 < XH:
                        copies(h + 1)
                    for b in range(2):
                        act.wait_ge(p_turned, 2 * h + b + 1)
                        nc.scalar.activation(m.a(pt0 + b * S, S), m.bank(6 * b, S), ACT.Copy).then_inc(pt_ok, 1)
                    act.wait_ge(pv, h + 1)
                    nc.scalar.activation(m.a(MT0 + h * S, S), m.bank(2, S), ACT.Copy).then_inc(mixed, 1)

            @block.vector
            def _(dve):
                st = Steps(dve_s)

                def tick(x):
                    x.then_inc(dve_s, st.tick())
                    dve.wait_ge(dve_s, st.n)

                for h in range(XH):
                    s = h % 2
                    c = sm0 + 24 * s
                    dve.wait_ge(scored, h + 1)
                    tick(nc.vector.tensor_reduce(m.a(c, NB), m.bank(2, 4 * BANK)
                                                 .rearrange("p (u n) -> p u n", u=NB), AX_X, ALU.max))
                    nc.vector.tensor_scalar(m.a(c + 8, NB), m.a(c, NB), -SCALE, None, ALU.mult).then_inc(neg_ok, 1)
                    dve.wait_ge(exped, h + 1)
                    tick(nc.vector.reciprocal(m.a(c + 16, NB), m.a(c + 16, NB)))
                    e = m.a(e0 + s * NB * M_LEN, NB * M_LEN).rearrange("p (u n) -> p u n", u=NB)
                    r = m.a(c + 16, NB).rearrange("p (u o) -> p u o", o=1).to_broadcast([P, NB, M_LEN])
                    nc.vector.tensor_tensor(e, e, r, ALU.mult).then_inc(p_ok, 1)


SLOT0 = ST0 + 64
WT0 = ST0 + 80
TRIPS = ST0 + 100
BE0 = ST0 + 104


def route(nc, m, d, layer, table):
    at = W0

    def room(n):
        nonlocal at
        at += n
        return at - n

    NR = NG + NE
    wr0, bias0, lg0 = room(KC * NR), room(NR), room(NB * NR)
    iota0, tri0, tok0, one0, zero0 = room(NBLK), room(P), room(NB), room(P), room(NBLK)
    g80, gm0, gi0, gf0, goh0 = room(64), room(64), room(64), room(NB), room(NB * NG)
    es0, em0, ei0, tmp0 = room(64), room(64), room(64), room(64)
    ef0, gx0, gs0, ed0, den0 = room(2 * NB), room(NB * NG), room(NB), room(NB), room(NB)
    mk0, ms0, tot0, pre0, sl0, pick0 = room(512), room(256), room(256), room(256), room(256), room(512)
    cnt0, i1280, cmp0, nb0, pend0, pst0 = room(NE), room(NB), room(NE * NB), room(NE), room(NE), room(NE)
    ones0, le0, be0, tr0, slf0 = room(NE), room(NBLK * NE), room(NBLK), room(NBLK), room(2 * NB)
    assert at <= TOTAL

    def b3(ap, a, b):
        return ap.rearrange("p (a o) -> p a o", o=1).to_broadcast([P, a, b])

    def b2(ap, a, b):
        return ap.rearrange("p (o b) -> p o b", o=1).to_broadcast([P, a, b])

    def t3(ap, a):
        return ap.rearrange("p (a b) -> p a b", a=a)

    with Phase(nc, f"route{layer}") as ph:
        loaded, zeroed, cleared, logits = ph.sem("loaded"), ph.sem("zeroed"), ph.sem("cleared"), ph.sem("logits")
        ex_in, ex_out, marked, counted = ph.sem("ex_in"), ph.sem("ex_out"), ph.sem("marked"), ph.sem("counted")
        slots_ok, scattered, dve_s = ph.sem("slots_ok"), ph.pool_dma(m), ph.sem("dve")
        with ph.block() as block:
            @block.sync
            def _(sp):
                wr = t3(m.a(wr0, KC * NR), KC)
                sp.dma_start(wr[:, :, NG:NR], d["f_w_exp"][layer].rearrange("(c p) n -> p c n", p=P)).then_inc(loaded, 16)
                sp.dma_start(wr[:, :, 0:NG], d["f_w_grp"][layer].rearrange("(c p) n -> p c n", p=P)).then_inc(loaded, 16)
                sp.dma_start(m.a(bias0, NG), row(d["f_b_grp"][layer])).then_inc(loaded, 16)
                sp.dma_start(m.a(bias0 + NG, NE), row(d["f_b_exp"][layer])).then_inc(loaded, 16)
                sp.dma_start(m.a(iota0, NBLK), d["c_iota"]).then_inc(loaded, 16)
                sp.dma_start(m.a(tri0, P), d["c_tri"]).then_inc(loaded, 16)
                sp.dma_start(m.a(tok0, NB).bitcast(I32), d["c_tok"]).then_inc(loaded, 16)
                sp.wait_ge(zeroed, 1)
                sp.dma_start(table.rearrange("(p n) o -> p (n o)", p=P),
                             m.a(zero0, NBLK).bitcast(I32)).then_inc(cleared, 16)
                sp.wait_ge(cleared, 16)

            @block.gpsimd
            def _(pool):
                nc.gpsimd.memset(m.a(one0, P), 1.0)
                nc.gpsimd.memset(m.a(zero0, NBLK), 0.0).then_inc(zeroed, 1)
                pool.wait_ge(cleared, 16)
                pool.wait_ge(slots_ok, 1)
                pool.wait_ge(loaded, 112)
                for k in range(2):
                    for b in range(NB):
                        pool.indirect_dma_start(
                            table, bass.IndirectOffsetOnAxis(ap=m.a(SLOT0 + 8 * k + b, 1).bitcast(U32), axis=0),
                            m.a(tok0 + b, 1).bitcast(I32), None).then_inc(scattered, 16)
                pool.wait_ge(scattered, 16 * 2 * NB)

            @block.tensor
            def _(pe):
                pe.wait_ge(loaded, 112)
                for b in range(NB):
                    for c in range(KC):
                        x = nc.tensor.matmul(m.bank(0, NR, at=b * NR), m.a(HT0 + c * S + b * P, P),
                                             m.a(wr0 + c * NR, NR), start=(c == 0), stop=(c == KC - 1))
                x.then_inc(logits, 1)
                pe.wait_ge(marked, 1)
                pe.wait_ge(zeroed, 1)
                nc.tensor.matmul(m.bank(1, 256), m.a(tri0, P), m.a(ms0, 256), start=True, stop=True)
                nc.tensor.matmul(m.bank(2, 256), m.a(one0, P), m.a(ms0, 256), start=True,
                                 stop=True).then_inc(counted, 1)

            @block.scalar
            def _(act):
                act.wait_ge(ex_in, 1)
                nc.scalar.activation(m.a(gx0, NB * NG), m.a(gx0, NB * NG), ACT.Exp)
                nc.scalar.activation(m.a(ed0, NB), m.a(ed0, NB), ACT.Exp).then_inc(ex_out, 1)

            @block.vector
            def _(dve):
                st = Steps(dve_s)
                v = nc.vector

                def tick(x):
                    x.then_inc(dve_s, st.tick())
                    dve.wait_ge(dve_s, st.n)

                v.memset(m.a(g80, 64), -3.0e38)
                dve.wait_ge(loaded, 112)
                dve.wait_ge(logits, 1)
                lg = t3(m.a(lg0, NB * NR), NB)
                tick(v.tensor_tensor(lg, t3(m.bank(0, NB * NR), NB), b2(m.a(bias0, NR), NB, NR), ALU.add))
                tick(v.tensor_copy(t3(m.a(g80, 64), NB)[:, :, 0:NG], lg[:, :, 0:NG]))
                for b in range(NB):
                    x = v.max(m.a(gm0 + 8 * b, 8), m.a(g80 + 8 * b, 8))
                tick(x)
                for b in range(NB):
                    x = v.max_index(m.a(gi0 + 8 * b, 8).bitcast(U32), m.a(gm0 + 8 * b, 8), m.a(g80 + 8 * b, 8))
                tick(x)
                gm = t3(m.a(gm0, 64), NB)[:, :, 0:1]
                tick(v.tensor_copy(m.a(gf0, NB), t3(m.a(gi0, 64), NB)[:, :, 0].bitcast(U32)))
                v.tensor_tensor(t3(m.a(gx0, NB * NG), NB), lg[:, :, 0:NG], gm.to_broadcast([P, NB, NG]),
                                ALU.subtract)
                tick(v.tensor_tensor(t3(m.a(goh0, NB * NG), NB), b3(m.a(gf0, NB), NB, NG),
                                     b2(m.a(iota0, NG), NB, NG), ALU.is_equal))
                goh = t3(m.a(goh0, NB * NG), NB)
                es, tmp = t3(m.a(es0, 64), NB), t3(m.a(tmp0, 64), NB)
                for g in range(NG):
                    part = lg[:, :, NG + EG * g:NG + EG * (g + 1)]
                    tick(v.tensor_tensor(es if g == 0 else tmp, part,
                                         goh[:, :, g:g + 1].to_broadcast([P, NB, EG]), ALU.mult))
                    if g:
                        tick(v.tensor_tensor(es, es, tmp, ALU.add))
                for b in range(NB):
                    x = v.max(m.a(em0 + 8 * b, 8), m.a(es0 + 8 * b, 8))
                tick(x)
                for b in range(NB):
                    x = v.max_index(m.a(ei0 + 8 * b, 8).bitcast(U32), m.a(em0 + 8 * b, 8), m.a(es0 + 8 * b, 8))
                em = t3(m.a(em0, 64), NB)
                tick(x)
                v.tensor_tensor(m.a(ed0, NB), em[:, :, 1], em[:, :, 0], ALU.subtract).then_inc(ex_in, 1)
                for k in range(2):
                    tick(v.tensor_copy(m.a(ef0 + k * NB, NB), t3(m.a(ei0, 64), NB)[:, :, k].bitcast(U32)))
                    tick(v.scalar_tensor_tensor(out=m.a(ef0 + k * NB, NB), in0=m.a(gf0, NB), scalar=float(EG),
                                                in1=m.a(ef0 + k * NB, NB), op0=ALU.mult, op1=ALU.add))
                    tick(v.tensor_tensor(t3(m.a(mk0 + 256 * k, 256), NB), b3(m.a(ef0 + k * NB, NB), NB, NE),
                                         b2(m.a(iota0, NE), NB, NE), ALU.is_equal))
                v.tensor_tensor(m.a(ms0, 256), m.a(mk0, 256), m.a(mk0 + 256, 256), ALU.add).then_inc(marked, 1)
                dve.wait_ge(ex_out, 1)
                tick(v.tensor_reduce(m.a(gs0, NB), t3(m.a(gx0, NB * NG), NB), AX_X, ALU.add))
                tick(v.scalar_tensor_tensor(out=m.a(den0, NB), in0=m.a(ed0, NB), scalar=1.0, in1=m.a(gs0, NB),
                                            op0=ALU.add, op1=ALU.mult))
                tick(v.reciprocal(m.a(WT0, NB), m.a(den0, NB)))
                v.tensor_tensor(m.a(WT0 + NB, NB), m.a(WT0, NB), m.a(ed0, NB), ALU.mult)
                dve.wait_ge(counted, 1)
                v.memset(m.a(pre0, NE), 0.0)
                tick(v.tensor_copy(m.a(tot0, 256), m.bank(2, 256)))
                for b in range(1, NB + 1):
                    to = cnt0 if b == NB else pre0 + b * NE
                    tick(v.tensor_tensor(m.a(to, NE), m.a(pre0 + (b - 1) * NE, NE),
                                         m.a(tot0 + (b - 1) * NE, NE), ALU.add))
                v.tensor_tensor(m.a(sl0, 256), m.a(pre0, 256), m.bank(1, 256), ALU.add)
                tick(v.tensor_scalar(m.a(i1280, NB), m.a(iota0, NB), float(P), None, ALU.mult))
                tick(v.tensor_tensor(t3(m.a(cmp0, NE * NB), NE), b3(m.a(cnt0, NE), NE, NB),
                                     b2(m.a(i1280, NB), NE, NB), ALU.is_gt))
                v.memset(m.a(ones0, NE), 1.0)
                tick(v.tensor_reduce(m.a(nb0, NE), t3(m.a(cmp0, NE * NB), NE), AX_X, ALU.add))
                tick(v.tensor_tensor_scan(m.a(pend0, NE), m.a(ones0, NE), m.a(nb0, NE), 0.0, ALU.mult, ALU.add))
                tick(v.tensor_tensor(m.a(pst0, NE), m.a(pend0, NE), m.a(nb0, NE), ALU.subtract))
                tick(v.tensor_scalar(m.a(pst0, NE), m.a(pst0, NE), float(P), None, ALU.mult))
                tick(v.tensor_tensor(t3(m.a(sl0, 256), NB), t3(m.a(sl0, 256), NB), b2(m.a(pst0, NE), NB, NE),
                                     ALU.add))
                for k in range(2):
                    tick(v.tensor_tensor(m.a(pick0 + 256 * k, 256), m.a(mk0 + 256 * k, 256), m.a(sl0, 256),
                                         ALU.mult))
                tick(v.tensor_reduce(m.a(slf0, 2 * NB), t3(m.a(pick0, 512), 2 * NB), AX_X, ALU.add))
                v.tensor_copy(m.a(SLOT0, 2 * NB).bitcast(U32), m.a(slf0, 2 * NB)).then_inc(slots_ok, 1)
                tick(v.tensor_tensor(t3(m.a(le0, NBLK * NE), NBLK), b2(m.a(pend0, NE), NBLK, NE),
                                     b3(m.a(iota0, NBLK), NBLK, NE), ALU.is_le))
                tick(v.tensor_reduce(m.a(be0, NBLK), t3(m.a(le0, NBLK * NE), NBLK), AX_X, ALU.add))
                tick(v.tensor_scalar(m.a(be0, NBLK), m.a(be0, NBLK), float(NE - 1), None, ALU.min))
                v.tensor_copy(m.a(BE0, NBLK).bitcast(I32), m.a(be0, NBLK))
                tick(v.tensor_tensor(m.a(tr0, NBLK // 2), m.a(pend0 + NE - 1, 1).to_broadcast([P, NBLK // 2]),
                                     m.a(iota0, NBLK).rearrange("p (a b) -> p a b", b=2)[:, :, 0], ALU.is_gt))
                tick(v.tensor_reduce(m.a(cnt0, 1), m.a(tr0, NBLK // 2), AX_X, ALU.add))
                tick(v.tensor_copy(m.a(TRIPS, 1).bitcast(I32), m.a(cnt0, 1)))


def experts(nc, m, d, layer, table, h_dram, y_dram):
    WE = KC * EH
    w0 = HT0
    small = ID0
    assert w0 + 4 * WE <= small
    w2 = W0
    wat = [[w0, w0 + WE, w0 + 2 * WE], [w0 + 3 * WE, w2, w2 + WE]]
    x0 = w2 + 2 * WE
    xt0 = x0 + 2 * D
    hm0 = xt0 + 2 * D
    ht0 = hm0 + 2 * EH
    y0 = ht0 + 2 * EH
    ix0 = y0 + 2 * D
    assert ix0 + 2 <= TOTAL
    HC = EH // P
    w_aps = (d["f_w_gate"].rearrange("l e (p c) n -> (l e) p (c n)", p=P),
             d["f_w_up"].rearrange("l e (p c) n -> (l e) p (c n)", p=P),
             d["f_w_down"].rearrange("l e (p c) n -> (l e) p (c n)", p=P))
    trips_ap = m.a(TRIPS, 1, 0, 1).bitcast(I32)
    with Phase(nc, f"experts{layer}") as ph:
        w_in = [[ph.sem(f"w{t}_in{s}") for s in range(2)] for t in range(3)]
        gated, upped, downed = ph.sem("gated"), ph.sem("upped"), ph.sem("downed")
        ix_in, x_in = [ph.pool_dma(m), ph.pool_dma(m)], [ph.pool_dma(m), ph.pool_dma(m)]
        x_turned, xt_ok, silu, hm_ok = ph.sem("x_turned"), ph.sem("xt_ok"), ph.sem("silu"), ph.sem("hm_ok")
        h_turned, ht_ok, y_ok = ph.sem("h_turned"), ph.sem("ht_ok"), ph.sem("y_ok")
        y_out, passed = [ph.sem("y_out0"), ph.sem("y_out1")], ph.sem("passed")
        with ph.block() as block:
            @block.sync
            def _(sp):
                trips = sp.value_load(trips_ap, min_val=8, max_val=NBLK // 2)
                with sp.Fori(0, trips) as i:
                    for s in range(2):
                        e = sp.value_load(m.dyn(BE0 + 2 * i + s, 1, 0, 1).bitcast(I32), min_val=0, max_val=NE - 1)
                        for t, used in enumerate((gated, upped, downed)):
                            sp.wait_ge(used, 2 * i + s + 1)
                            sp.dma_start(m.a(wat[s][t], WE), w_aps[t][bass.ds(e + layer * NE, 1), :, :]
                                         .rearrange("a p n -> (a p) n")).then_inc(w_in[t][s], 16)

            @block.gpsimd
            def _(pool):
                trips = pool.value_load(trips_ap, min_val=8, max_val=NBLK // 2)
                with pool.Fori(0, trips) as i:
                    for s in range(2):
                        pool.wait_ge(x_turned, 2 * i + s + 1)
                        pool.dma_start(m.a(ix0 + s, 1).bitcast(I32),
                                       table[bass.ds((2 * i + s) * P, P), :]).then_inc(ix_in[s], 16)
                        pool.wait_ge(ix_in[s], 16 * i + 16)
                        pool.sem_inc(passed, 1)
                        pool.indirect_dma_start(
                            m.a(x0 + s * D, D), None, h_dram,
                            bass.IndirectOffsetOnAxis(ap=m.a(ix0 + s, 1).bitcast(U32), axis=0))\
                            .then_inc(x_in[s], 16)

            @block.tensor
            def _(pe):
                trips = pe.value_load(trips_ap, min_val=8, max_val=NBLK // 2)
                for q in (gated, upped, downed, x_turned):
                    pe.sem_inc(q, 2)

                def turn_x(n, s, i):
                    pe.wait_ge(x_in[s], 16 * i + 16)
                    pe.wait_ge(xt_ok, n + 1)
                    for c in range(KC):
                        x = nc.tensor.transpose(m.bank(0, P, at=c * P),
                                                m.A[:, x0 + s * D + c:x0 + (s + 1) * D:KC], m.ident())
                    x.then_inc(x_turned, 1)

                def gate_up(n, s, i):
                    pe.wait_ge(xt_ok, n + 2)
                    for t, b, done in ((0, 2, gated), (1, 3, upped)):
                        pe.wait_ge(w_in[t][s], 16 * i + 16)
                        pe.wait_ge((silu, hm_ok)[t], n + 1)
                        for c in range(KC):
                            x = nc.tensor.matmul(m.bank(b), m.a(xt0 + s * D + c * P, P),
                                                 m.a(wat[s][t] + c * EH, EH),
                                                 start=(c == 0), stop=(c == KC - 1))
                        x.then_inc(done, 1)

                def turn_h(n, s):
                    pe.wait_ge(hm_ok, n + 2)
                    pe.wait_ge(ht_ok, n + 1)
                    for c in range(HC):
                        x = nc.tensor.transpose(m.bank(4, P, at=c * P),
                                                m.A[:, hm0 + s * EH + c:hm0 + (s + 1) * EH:HC], m.ident())
                    x.then_inc(h_turned, 1)

                def down(n, s, i):
                    pe.wait_ge(ht_ok, n + 2)
                    pe.wait_ge(w_in[2][s], 16 * i + 16)
                    pe.wait_ge(y_ok, n + 2)
                    for h in range(2):
                        for c in range(HC):
                            x = nc.tensor.matmul(m.bank(5 + h), m.a(ht0 + s * EH + c * P, P),
                                                 m.a(wat[s][2] + c * D + h * BANK, BANK),
                                                 start=(c == 0), stop=(c == HC - 1))
                    x.then_inc(downed, 1)

                turn_x(0, 0, 0)
                gate_up(0, 0, 0)
                turn_x(1, 1, 0)
                turn_h(0, 0)
                with pe.Fori(0, trips - 1) as i:
                    gate_up(2 * i + 1, 1, i)
                    turn_x(2 * i + 2, 0, i + 1)
                    down(2 * i, 0, i)
                    turn_h(2 * i + 1, 1)
                    gate_up(2 * i + 2, 0, i + 1)
                    turn_x(2 * i + 3, 1, i + 1)
                    down(2 * i + 1, 1, i)
                    turn_h(2 * i + 2, 0)
                last = trips * 2 - 1
                gate_up(last, 1, trips - 1)
                down(last - 1, 0, trips - 1)
                turn_h(last, 1)
                down(last, 1, trips - 1)

            @block.scalar
            def _(act):
                trips = act.value_load(trips_ap, min_val=8, max_val=NBLK // 2)
                for q in (xt_ok, silu, ht_ok):
                    act.sem_inc(q, 1)
                act.sem_inc(y_ok, 2)
                for s in range(2):
                    act.sem_inc(y_out[s], 16)

                def copy_x(n, s):
                    act.wait_ge(x_turned, n + 3)
                    nc.scalar.activation(m.a(xt0 + s * D, D), m.bank(0, D), ACT.Copy).then_inc(xt_ok, 1)

                def gate(n, s):
                    act.wait_ge(gated, n + 3)
                    act.wait_ge(h_turned, n + 1)
                    nc.scalar.activation(m.a(hm0 + s * EH, EH), m.bank(2), ACT.Silu).then_inc(silu, 1)

                def copy_h(n, s):
                    act.wait_ge(h_turned, n + 2)
                    nc.scalar.activation(m.a(ht0 + s * EH, EH), m.bank(4), ACT.Copy).then_inc(ht_ok, 1)

                def store_y(n, s, i):
                    act.wait_ge(downed, n + 3)
                    act.wait_ge(y_out[s], 16 * i + 16)
                    nc.scalar.activation(m.a(y0 + s * D, D), m.bank(5, D), ACT.Copy).then_inc(y_ok, 1)
                    act.wait_ge(y_ok, n + 3)
                    act.dma_start(y_dram[bass.ds(n * P, P), :], m.a(y0 + s * D, D)).then_inc(y_out[s], 16)

                copy_x(0, 0)
                gate(0, 0)
                copy_x(1, 1)
                copy_h(0, 0)
                with act.Fori(0, trips - 1) as i:
                    gate(2 * i + 1, 1)
                    copy_x(2 * i + 2, 0)
                    store_y(2 * i, 0, i)
                    copy_h(2 * i + 1, 1)
                    gate(2 * i + 2, 0)
                    copy_x(2 * i + 3, 1)
                    store_y(2 * i + 1, 1, i)
                    copy_h(2 * i + 2, 0)
                last = trips * 2 - 1
                gate(last, 1)
                store_y(last - 1, 0, trips - 1)
                copy_h(last, 1)
                store_y(last, 1, trips - 1)
                for s in range(2):
                    act.wait_ge(y_out[s], trips * 16 + 16)
                    act.sem_inc(passed, 1)

            @block.vector
            def _(dve):
                trips = dve.value_load(trips_ap, min_val=8, max_val=NBLK // 2)
                dve.sem_inc(hm_ok, 1)
                dve.sem_inc(h_turned, 1)
                with dve.Fori(0, trips) as i:
                    for s in range(2):
                        n = 2 * i + s
                        dve.wait_ge(silu, n + 2)
                        dve.wait_ge(upped, n + 3)
                        h = m.a(hm0 + s * EH, EH)
                        nc.vector.tensor_tensor(h, h, m.bank(3), ALU.mult).then_inc(hm_ok, 1)


def combine(nc, m, layer, y_dram):
    NS = 4
    y0 = W0
    sq0 = y0 + NS * D
    with Phase(nc, f"combine{layer}") as ph:
        y_in = [ph.pool_dma(m) for s in range(NS)]
        added, squared = ph.sem("added"), ph.sem("squared")
        with ph.block() as block:
            @block.gpsimd
            def _(pool):
                for n in range(2 * NB):
                    b, k = n // 2, n % 2
                    if n >= NS:
                        pool.wait_ge(added, n - NS + 1)
                    pool.indirect_dma_start(
                        m.a(y0 + (n % NS) * D, D), None, y_dram,
                        bass.IndirectOffsetOnAxis(ap=m.a(SLOT0 + 8 * k + b, 1).bitcast(U32), axis=0))\
                        .then_inc(y_in[n % NS], 16)

            @block.vector
            def _(dve):
                for n in range(2 * NB):
                    b, k = n // 2, n % 2
                    dve.wait_ge(y_in[n % NS], 16 * (n // NS + 1))
                    if k:
                        dve.wait_ge(added, n)
                    x = m.a(X0 + b * D, D)
                    nc.vector.scalar_tensor_tensor(out=x, in0=m.a(y0 + (n % NS) * D, D),
                                                   scalar=m.a(WT0 + 8 * k + b, 1), in1=x,
                                                   op0=ALU.mult, op1=ALU.add).then_inc(added, 1)

            @block.scalar
            def _(act):
                for b in range(NB):
                    act.wait_ge(added, 2 * b + 2)
                    if b >= 2:
                        act.wait_ge(squared, b - 1)
                    nc.scalar.activation(m.a(sq0 + (b % 2) * D, D), m.a(X0 + b * D, D), ACT.Square,
                                         accum_out=m.a(ST0 + b, 1)).then_inc(squared, 1)


def final_norm(nc, m, gain, out):
    rstd = m.a(ST0 + 8, NB)
    with Phase(nc, "final") as ph:
        loaded, var_ok, rooted, dve_s = ph.sem("loaded"), ph.sem("var_ok"), ph.sem("rooted"), ph.sem("dve")
        normed, stored = ph.sem("normed"), ph.sem("stored")
        with ph.block() as block:
            @block.sync
            def _(sp):
                sp.dma_start(m.a(GB0, D), row(gain)).then_inc(loaded, 16)
                for b in range(NB):
                    sp.wait_ge(normed, b + 1)
                    sp.dma_start(out[0, b * P:(b + 1) * P, :], m.a(X0 + b * D, D)).then_inc(stored, 16)
                sp.wait_ge(stored, 16 * NB)

            @block.scalar
            def _(act):
                act.wait_ge(var_ok, 1)
                nc.scalar.activation(rstd, rstd, ACT.Sqrt).then_inc(rooted, 1)

            @block.vector
            def _(dve):
                nc.vector.tensor_scalar(rstd, m.a(ST0, NB), 1.0 / D, EPS, ALU.mult, ALU.add).then_inc(var_ok, 1)
                dve.wait_ge(rooted, 1)
                nc.vector.reciprocal(rstd, rstd).then_inc(dve_s, 1)
                dve.wait_ge(dve_s, 1)
                dve.wait_ge(loaded, 16)
                for b in range(NB):
                    x = m.a(X0 + b * D, D)
                    nc.vector.scalar_tensor_tensor(out=x, in0=x, scalar=m.a(ST0 + 8 + b, 1), in1=m.a(GB0, D),
                                                   op0=ALU.mult, op1=ALU.mult).then_inc(normed, 1)


def load_memory(nc, m, d):
    with Phase(nc, "memory") as ph:
        loaded = ph.sem("loaded")
        with ph.block() as block:
            @block.sync
            def _(sp):
                sp.dma_start(m.ident(), d["c_ident"]).then_inc(loaded, 16)
                sp.dma_start(m.a(X0, 2 * D).rearrange("p (b n) -> p b n", b=2),
                             d["mem"][0].rearrange("(b p) n -> p b n", p=P)).then_inc(loaded, 16)
                sp.wait_ge(loaded, 32)


def program(nc, d, out, stop=None):
    def scratch(name, shape, dt=F32):
        return nc.dram_tensor(name, shape, dt, kind="Internal").ap()

    spectra = scratch("spectra", (2 * QT_N, P, FQ))
    h_dram = scratch("h_tokens", (S, D))
    y_dram = scratch("y_slots", (NSLOT, D))
    table = scratch("slot_table", (NSLOT, 1), I32)

    def rows(w):
        return lambda c: [(0, P, w[c * P:(c + 1) * P, :])]

    w_o = d["o_w_out"][0].rearrange("(i s j e) n -> i j s e n", i=2, s=2, j=4)
    steps = [
        lambda: load_memory(nc, m, d),
        lambda: norm_transpose(nc, m, "memnorm", d["g_mem"], X0, ME0, 2),
        lambda: load_start(nc, m, d),
        lambda: filter_taps(nc, m, d),
        lambda: filter_spectrum(nc, m, d, 0, spectra),
        lambda: filter_spectrum(nc, m, d, 1, spectra),
        lambda: norm_transpose(nc, m, "enorm", d["e_norm"][0], X0, HT0, NB),
        lambda: diff_attention(nc, m, d, y_dram),
        lambda: hyena_project(nc, m, d),
        lambda: long_conv(nc, m, d, 0, spectra),
        lambda: long_conv(nc, m, d, 1, spectra),
        lambda: project_add(nc, m, "eout", rows(d["e_w_out"][0]), 8, reload=d["x"][0],
                            gain=d["c_norm"][0]),
    ]
    for layer in range(2):
        if layer == 1:
            steps += [
                lambda: norm_transpose(nc, m, "onorm", d["o_norm"][0], X0, HT0, NB, stats=False),
                lambda: window_attention(nc, m, d),
                lambda: project_add(nc, m, "oout", lambda c: [
                    (64 * s, 64 * s + 64, w_o[c // 4, c % 4, s]) for s in range(2)], 8,
                    gain=d["c_norm"][1]),
            ]
        steps += [
            lambda L=layer: cross_attention(nc, m, d, L),
            lambda L=layer: project_add(nc, m, f"cout{L}", rows(d["c_wo"][L]), 4,
                                        gain=d["f_norm"][L], h_dram=h_dram),
            lambda L=layer: route(nc, m, d, L, table),
            lambda L=layer: experts(nc, m, d, L, table, h_dram, y_dram),
            lambda L=layer: combine(nc, m, L, y_dram),
        ]
    steps.append(lambda: final_norm(nc, m, d["g_final"], out))
    with ExitStack() as stack:
        m = Core(nc, stack)
        for step in steps[:stop]:
            step()


def constants():
    f8 = np.float64
    c = {"c_ident": np.eye(P)}
    pos = np.arange(S, dtype=np.float32)
    t = np.linspace(0.0, 1.0, S, dtype=np.float32)
    bands = np.linspace(1e-4, 15, 16, dtype=np.float32)
    ang = bands[None] * (2.0 * np.pi * pos[:, None] / S).astype(np.float32)
    c["c_pos"] = np.concatenate([t[:, None], np.cos(ang), -np.sin(ang)], axis=1).T
    deltas = np.linspace(np.log(1e-2) / 1.5, np.log(1e-2) / 0.3, HW, dtype=np.float32)
    decay = np.exp(-t[:, None] * np.abs(deltas)[None])
    c["c_decay"] = decay.reshape(4, P, 2, HW).transpose(1, 2, 0, 3).reshape(P, 8 * HW)
    c["c_sign"] = np.where(np.arange(P) < 64, 1.0, -1.0)[:, None]
    times = np.arange(S).reshape(4, P, 2)
    freq = (np.arange(S // 2) + 0.5).reshape(4, P)
    ang = np.pi * times[None, None].astype(f8) * freq[:, :, None, None, None] / S
    both = np.stack([np.cos(ang), np.sin(ang)])
    c["c_dft"] = both.transpose(1, 4, 0, 5, 3, 2).reshape(4, P, -1)
    c["c_idft"] = both.transpose(1, 2, 0, 5, 3, 4).reshape(4, P, -1) / S
    p = np.arange(P)[:, None]
    c["c_dist"] = -8.0 * np.abs(p - (np.arange(2 * S - P)[None] - (S - P)))
    rel = np.abs(p + P - np.arange(3 * P)[None])
    heads = np.array([[s * 4 + j for s in range(2)] for j in range(4)]).reshape(8, 1, 1)
    slopes = 2.0 ** (-8.0 * (heads + 1) / 16)
    c["c_window"] = np.where(rel[None] <= P, -8.0 * slopes * rel[None], -1e30).transpose(1, 0, 2).reshape(P, -1)
    c["c_iota"] = np.broadcast_to(np.arange(NBLK), (P, NBLK))
    c["c_tri"] = np.triu(np.ones((P, P)), 1)
    out = {k: np.ascontiguousarray(v, dtype=np.float32) for k, v in c.items()}
    out["c_tok"] = np.ascontiguousarray((np.arange(NB)[None] * P + p).astype(np.int32))
    return out


_INS = ['x', 'mem', 'e_norm', 'e_w_in', 'e_conv_w', 'e_conv_b', 'e_filt_w1', 'e_filt_b1', 'e_filt_w2',
        'e_filt_b2', 'e_filt_w3', 'e_filt_freq', 'e_hy_bias', 'e_lam', 'e_subln', 'e_w_out', 'o_norm',
        'o_w_in', 'o_sink', 'o_w_out', 'c_norm', 'c_wq', 'c_wkv', 'c_wo', 'f_norm', 'f_w_grp', 'f_b_grp',
        'f_w_exp', 'f_b_exp', 'f_w_gate', 'f_w_up', 'f_w_down', 'g_mem', 'g_final']
STOP = None


def kernel(**inputs):
    import concourse.bacc as _bacc
    from concourse.bass_utils import run_bass_kernel_spmd as _run

    nc = _bacc.Bacc("TRN2", target_bir_lowering=False, num_devices=1)
    arrays = {f"in_{n}": np.ascontiguousarray(inputs[n]) for n in _INS}
    arrays.update({f"in_{n}": v for n, v in constants().items()})
    d = {n[3:]: nc.dram_tensor(n, v.shape, mybir.dt.from_np(v.dtype), kind="ExternalInput").ap()
         for n, v in arrays.items()}
    out = nc.dram_tensor("out_0", (1, S, D), F32, kind="ExternalOutput").ap()
    program(nc, d, out, STOP)
    r = _run(nc, [arrays], core_ids=[0])
    return r.results[0]["out_0"]
```

```python
from contextlib import ExitStack

import numpy as np
import concourse.bass as bass
from concourse import mybir
from concourse.alu_op_type import AluOpType as ALU

ACT = mybir.ActivationFunctionType
F32 = mybir.dt.float32
I32 = mybir.dt.int32
U32 = mybir.dt.uint32
AX_X = mybir.AxisListType.X

P = 128
S = 1024
D = 1024
NB = S // P
KC = D // P
BANK = 512
EPS = 1e-6
HW = 512
QT_N = 4
M_LEN = 256
XH = 4
NE = 32
NG = 4
EG = NE // NG
NR = NG + NE
ROUTE_BANK = 5
EH = 512
NBLK = 2 * S // P + NE
NSLOT = NBLK * P

X0 = 0
HT0 = X0 + NB * D
MT0 = HT0 + KC * S
ID0 = MT0 + KC * S
ST0 = ID0 + P
GB0 = ST0 + 256
ME0 = GB0 + D
W0 = ME0 + KC * M_LEN
TOTAL = 53200
WN = TOTAL - W0


class Steps:

    def __init__(self, sem):
        self.sem, self.k, self.i, self.per = sem, 0, None, 0

    def enter(self, i, per):
        self.i, self.per, self.k0 = i, per, self.k

    def leave(self, trips):
        assert self.k - self.k0 == self.per, (self.k - self.k0, self.per)
        self.k, self.i = self.k0 + trips * self.per, None

    def tick(self):
        self.k += 1
        return 1

    @property
    def n(self):
        return self.k if self.i is None else self.i * self.per + self.k


class Core:

    def __init__(self, nc, stack):
        self.nc = nc
        self.A = stack.enter_context(nc.sbuf_tensor("sbuf", [P, TOTAL], F32))
        self.PS = stack.enter_context(nc.psum_tensor("psum", [P, 8 * BANK], F32))
        self.pool_dma = iter([stack.enter_context(nc.semaphore(f"pool_dma{n}")) for n in range(31)])

    def a(self, at, n, p0=0, p1=P):
        return self.A[p0:p1, at:at + n]

    def dyn(self, at, n, p0=0, p1=P):
        return self.A[p0:p1, bass.ds(at, n)]

    def bank(self, b, n=BANK, p0=0, p1=P, at=0):
        return self.PS[p0:p1, b * BANK + at:b * BANK + at + n]

    def ident(self, n=P):
        return self.A[0:n, ID0:ID0 + n]


class Phase:

    def __init__(self, nc, name):
        self.nc, self.name = nc, name

    def __enter__(self):
        self.stack, self.sems = ExitStack(), []
        return self

    def sem(self, name):
        s = self.stack.enter_context(self.nc.semaphore(f"{self.name}_{name}"))
        self.sems.append(s)
        return s

    def pool_dma(self, m):
        return next(m.pool_dma)

    def block(self):
        return self.nc.Block()

    def __exit__(self, *exc):
        if exc[0] is None:
            for s in self.sems:
                self.nc.sync.sem_clear(s)
            self.nc.all_engine_barrier()
        self.stack.close()


def row(ap):
    n = ap.shape[0]
    return ap.rearrange("(a n) -> a n", a=1).to_broadcast([P, n])


def load_start(nc, m, d):
    with Phase(nc, "start") as ph:
        loaded = ph.sem("loaded")
        with ph.block() as block:
            @block.sync
            def _(sp):
                sp.dma_start(m.ident(), d["c_ident"]).then_inc(loaded, 16)
                sp.dma_start(m.a(X0, NB * D).rearrange("p (b n) -> p b n", b=NB),
                             d["x"][0].rearrange("(b p) n -> p b n", p=P)).then_inc(loaded, 16)
                sp.wait_ge(loaded, 32)


def norm_transpose(nc, m, name, gain, src, dst, nblk, stats=True, h_dram=None):
    ntok = nblk * P
    sums, rstd = m.a(ST0, nblk), m.a(ST0 + 8, nblk)
    h0 = W0
    sq0 = W0 + 2 * D
    with Phase(nc, name) as ph:
        loaded, squared, var_ok = ph.sem("loaded"), ph.sem("squared"), ph.sem("var_ok")
        rooted, dve, h_ready = ph.sem("rooted"), ph.sem("dve"), ph.sem("h_ready")
        turned, copied = ph.sem("turned"), ph.sem("copied")
        stored = [ph.sem("stored0"), ph.sem("stored1")]
        with ph.block() as block:
            @block.sync
            def _(sp):
                sp.dma_start(m.a(GB0, D), row(gain)).then_inc(loaded, 16)
                if h_dram is not None:
                    sp.sem_inc(stored[0], 16)
                    sp.sem_inc(stored[1], 16)
                    with sp.Fori(0, nblk // 2) as i:
                        for s in range(2):
                            sp.wait_ge(h_ready, 2 * i + s + 1)
                            sp.dma_start(h_dram[bass.ds((2 * i + s) * P, P), :],
                                         m.a(h0 + s * D, D)).then_inc(stored[s], 16)
                    for s in range(2):
                        sp.wait_ge(stored[s], 16 * (nblk // 2 + 1))

            @block.scalar
            def _(act):
                if stats:
                    for b in range(nblk):
                        if b >= 2:
                            act.wait_ge(squared, b - 1)
                        nc.scalar.activation(m.a(sq0 + (b % 2) * D, D), m.a(src + b * D, D), ACT.Square,
                                             accum_out=m.a(ST0 + b, 1)).then_inc(squared, 1)
                act.wait_ge(var_ok, 1)
                nc.scalar.activation(rstd, rstd, ACT.Sqrt).then_inc(rooted, 1)
                act.sem_inc(copied, 2)
                with act.Fori(0, nblk // 2) as i:
                    for s in range(2):
                        act.wait_ge(turned, 2 * i + s + 3)
                        out = m.dyn(dst + (2 * i + s) * P, (KC - 1) * ntok + P)
                        out = bass.AP(tensor=out.tensor, offset=out.offset,
                                      ap=[out.ap[0], [ntok, KC], [1, P]])
                        nc.scalar.activation(out, m.bank(2 * s, D).rearrange("p (c t) -> p c t", c=KC),
                                             ACT.Copy).then_inc(copied, 1)

            @block.vector
            def _(dve_e):
                if stats:
                    dve_e.wait_ge(squared, nblk)
                nc.vector.tensor_scalar(rstd, sums, 1.0 / D, EPS, ALU.mult, ALU.add).then_inc(var_ok, 1)
                dve_e.wait_ge(rooted, 1)
                nc.vector.reciprocal(rstd, rstd).then_inc(dve, 1)
                dve_e.wait_ge(dve, 1)
                dve_e.wait_ge(loaded, 16)
                with dve_e.Fori(0, nblk // 2) as i:
                    for s in range(2):
                        dve_e.wait_ge(turned, 2 * i + s + 1)
                        if h_dram is not None:
                            dve_e.wait_ge(stored[s], 16 * i + 16)
                        nc.vector.scalar_tensor_tensor(
                            out=m.a(h0 + s * D, D), in0=m.dyn(src + (2 * i + s) * D, D),
                            scalar=m.dyn(ST0 + 8 + 2 * i + s, 1), in1=m.a(GB0, D),
                            op0=ALU.mult, op1=ALU.mult).then_inc(h_ready, 1)

            @block.tensor
            def _(pe):
                pe.sem_inc(turned, 2)
                with pe.Fori(0, nblk // 2) as i:
                    for s in range(2):
                        pe.wait_ge(h_ready, 2 * i + s + 1)
                        pe.wait_ge(copied, 2 * i + s + 1)
                        for c in range(KC):
                            t = nc.tensor.transpose(m.bank(2 * s, P, at=c * P),
                                                    m.a(h0 + s * D + c * P, P), m.ident())
                        t.then_inc(turned, 1)


def project_add(nc, m, name, w, nfc, reload=None, gain=None, h_dram=None, router=None):
    ww = W0
    sq0 = W0 + nfc * D
    h0 = sq0 + 2 * D
    wr0 = h0 + 2 * D
    var0, rs0 = ST0 + 8, ST0 + 16
    with Phase(nc, name) as ph:
        w_in = [ph.sem(f"w_in{c}") for c in range(nfc)]
        x_in, summed, added, squared = ph.sem("x_in"), ph.sem("summed"), ph.sem("added"), ph.sem("squared")
        g_in, var_ok, rooted, dve_s = ph.sem("g_in"), ph.sem("var_ok"), ph.sem("rooted"), ph.sem("dve")
        h_ready, turned, copied, stored = ph.sem("h_ready"), ph.sem("turned"), ph.sem("copied"), ph.sem("stored")
        wr_in = ph.sem("wr_in")
        with ph.block() as block:
            @block.sync
            def _(sp):
                for c in range(nfc):
                    for p0, p1, rows in w(c):
                        sp.dma_start(m.a(ww + c * D, D, p0, p1), rows).then_inc(w_in[c], 16)
                    if c == 0 and reload is not None:
                        sp.dma_start(m.a(X0, NB * D).rearrange("p (b n) -> p b n", b=NB),
                                     reload.rearrange("(b p) n -> p b n", p=P)).then_inc(x_in, 16)
                if gain is not None:
                    sp.dma_start(m.a(GB0, D), row(gain)).then_inc(g_in, 16)
                if router is not None:
                    wr = m.a(wr0, KC * NR).rearrange("p (c n) -> p c n", c=KC)
                    for w_r, n0, n1 in router:
                        sp.dma_start(wr[:, :, n0:n1],
                                     w_r.rearrange("(c p) n -> p c n", p=P)).then_inc(wr_in, 16)
                if h_dram is not None:
                    for b in range(NB):
                        sp.wait_ge(h_ready, b + 1)
                        sp.dma_start(h_dram[b * P:(b + 1) * P, :],
                                     m.a(h0 + (b % 2) * D, D)).then_inc(stored, 16)
                        sp.wait_ge(stored, 16 * (b + 1))

            @block.tensor
            def _(pe):
                def product(c, blk):
                    for h in range(2):
                        t = nc.tensor.matmul(m.bank(2 * (blk % 4) + h), m.a(MT0 + c * S + blk * P, P),
                                             m.a(ww + c * D + h * BANK, BANK),
                                             start=(c == 0), stop=(c == nfc - 1))
                    if c == nfc - 1:
                        t.then_inc(summed, 1)

                def turn(blk):
                    pe.wait_ge(h_ready, blk + 1)
                    pe.wait_ge(added, 5 + blk % 2)
                    if blk >= 2:
                        pe.wait_ge(copied, blk - 1)
                    for c in range(KC):
                        t = nc.tensor.transpose(m.bank(2 * (blk % 2), P, at=c * P),
                                                m.a(h0 + (blk % 2) * D + c * P, P), m.ident())
                    t.then_inc(turned, 1)

                def logits(blk):
                    if blk == 0:
                        pe.wait_ge(wr_in, 16 * len(router))
                        pe.wait_ge(added, 7)
                    pe.wait_ge(copied, blk + 1)
                    for c in range(KC):
                        nc.tensor.matmul(m.bank(ROUTE_BANK, NR, at=blk * NR),
                                         m.a(HT0 + c * S + blk * P, P), m.a(wr0 + c * NR, NR),
                                         start=(c == 0), stop=(c == KC - 1))

                for c in range(nfc):
                    pe.wait_ge(w_in[c], 16 * len(w(c)))
                    for blk in range(4):
                        product(c, blk)
                for blk in range(4, NB):
                    pe.wait_ge(added, blk - 3)
                    for c in range(nfc):
                        product(c, blk)
                    if gain is not None and blk >= 6:
                        turn(blk - 6)
                if gain is not None:
                    for blk in range(2, NB):
                        turn(blk)
                        if router is not None:
                            logits(blk - 2)
                if router is not None:
                    logits(NB - 2)
                    logits(NB - 1)

            @block.vector
            def _(dve):
                if reload is not None:
                    dve.wait_ge(x_in, 16)
                st = Steps(dve_s)

                def roots(g):
                    dve.wait_ge(squared, 4 * g + 4)
                    nc.vector.tensor_scalar(m.a(var0 + 4 * g, 4), m.a(ST0 + 4 * g, 4), 1.0 / D, EPS,
                                            ALU.mult, ALU.add).then_inc(var_ok, 1)
                    dve.wait_ge(rooted, g + 1)
                    nc.vector.reciprocal(m.a(rs0 + 4 * g, 4), m.a(var0 + 4 * g, 4)).then_inc(dve_s, st.tick())
                    dve.wait_ge(dve_s, st.n)

                def normalise(blk):
                    if blk == 0:
                        dve.wait_ge(g_in, 16)
                    if blk >= 2:
                        dve.wait_ge(turned, blk - 1)
                        if h_dram is not None:
                            dve.wait_ge(stored, 16 * (blk - 1))
                    nc.vector.scalar_tensor_tensor(
                        out=m.a(h0 + (blk % 2) * D, D), in0=m.a(X0 + blk * D, D), scalar=m.a(rs0 + blk, 1),
                        in1=m.a(GB0, D), op0=ALU.mult, op1=ALU.mult).then_inc(h_ready, 1)

                for blk in range(NB):
                    dve.wait_ge(summed, blk + 1)
                    x = m.a(X0 + blk * D, D)
                    nc.vector.tensor_tensor(x, m.bank(2 * (blk % 4), D), x, ALU.add).then_inc(added, 1)
                    if gain is not None and blk in (4, 5):
                        if blk == 4:
                            roots(0)
                        normalise(blk - 4)
                if gain is not None:
                    normalise(2)
                    roots(1)
                    for blk in range(3, NB):
                        normalise(blk)

            @block.scalar
            def _(act):
                def root(g):
                    act.wait_ge(var_ok, g + 1)
                    v = m.a(var0 + 4 * g, 4)
                    nc.scalar.activation(v, v, ACT.Sqrt).then_inc(rooted, 1)

                def copy(blk):
                    act.wait_ge(turned, blk + 1)
                    out = m.A[:, HT0 + blk * P:HT0 + blk * P + (KC - 1) * S + P]
                    out = bass.AP(tensor=out.tensor, offset=out.offset, ap=[out.ap[0], [S, KC], [1, P]])
                    nc.scalar.activation(out, m.bank(2 * (blk % 2), D).rearrange("p (c t) -> p c t", c=KC),
                                         ACT.Copy).then_inc(copied, 1)

                for blk in range(NB):
                    act.wait_ge(added, blk + 1)
                    if blk >= 2:
                        act.wait_ge(squared, blk - 1)
                    nc.scalar.activation(m.a(sq0 + (blk % 2) * D, D), m.a(X0 + blk * D, D), ACT.Square,
                                         accum_out=m.a(ST0 + blk, 1)).then_inc(squared, 1)
                    if gain is not None and blk == 4:
                        root(0)
                if gain is not None:
                    copy(0)
                    copy(1)
                    root(1)
                    for blk in range(2, NB):
                        copy(blk)


FQ = 2 * 2 * 4 * P


def filter_taps(nc, m, d):
    z0 = W0
    a10, a20 = z0 + S, z0 + 2 * S
    u0, r0 = z0 + 3 * S, z0 + 4 * S
    w10 = z0 + 5 * S
    w20 = w10 + 64
    v0 = w20 + P
    w30 = v0 + 8
    dec0 = w30 + 4 * HW
    with Phase(nc, "taps") as ph:
        loaded, dec_in, sign_ok = ph.sem("loaded"), ph.sem("dec_in"), ph.sem("sign_ok")
        layer, arg, sined = ph.sem("layer"), ph.sem("arg"), ph.sem("sined")
        dve_s, h_sum, h_ok = ph.sem("dve"), ph.sem("h_sum"), ph.sem("h_ok")
        w3 = d["e_filt_w3"][0].rearrange("k (o q c) -> k o q c", o=2, q=2)
        with ph.block() as block:
            @block.sync
            def _(sp):
                sp.dma_start(m.a(z0, S, 0, 33), d["c_pos"]).then_inc(loaded, 16)
                sp.dma_start(m.a(w10, 64, 0, 33), d["e_filt_w1"][0]).then_inc(loaded, 16)
                for q in range(2):
                    sp.dma_start(m.a(w20 + 64 * q, 64, 0, 64), d["e_filt_w2"][0]).then_inc(loaded, 16)
                    for n, v in enumerate(("e_filt_b1", "e_filt_freq", "e_filt_b2")):
                        sp.dma_start(m.a(v0 + n, 1, 64 * q, 64 * q + 64),
                                     d[v][0].rearrange("(k o) -> k o", o=1)).then_inc(loaded, 16)
                    sp.dma_start(m.a(w30, 2 * HW, 64 * q, 64 * q + 64).rearrange("k (o c) -> k o c", o=2),
                                 w3[:, :, q, :]).then_inc(loaded, 16)
                sp.dma_start(m.a(v0 + 4, 1), d["c_sign"]).then_inc(loaded, 16)
                sp.dma_start(m.a(dec0, 8 * HW), d["c_decay"]).then_inc(dec_in, 16)

            @block.tensor
            def _(pe):
                pe.wait_ge(loaded, 16 * 13)
                for h in range(2):
                    t = nc.tensor.matmul(m.bank(h, p1=64), m.a(w10, 64, 0, 33),
                                         m.a(z0 + h * BANK, BANK, 0, 33), start=True, stop=True)
                t.then_inc(layer, 1)
                pe.wait_ge(sined, 1)
                for h in range(2):
                    t = nc.tensor.matmul(m.bank(2 + h), m.a(w20, P, 0, 64),
                                         m.a(a10 + h * BANK, BANK, 0, 64), start=True, stop=True)
                t.then_inc(layer, 1)
                pe.wait_ge(sign_ok, 2)
                for o in range(2):
                    for j in range(8):
                        for q in range(2):
                            n = 2 * (8 * o + j) + q
                            if n >= 4:
                                pe.wait_ge(h_ok, n - 3)
                            at = a20 + 2 * P * (j % 4) + j // 4
                            nc.tensor.matmul(m.bank(4 + n % 4), m.A[:, at:at + 2 * P - 1:2],
                                             m.a(w30 + (2 * q + o) * HW, HW),
                                             start=True, stop=True).then_inc(h_sum, 1)

            @block.scalar
            def _(act):
                for n, (to, p1) in enumerate(((a10, 64), (a20, P))):
                    act.wait_ge(arg, n + 1)
                    nc.scalar.activation(m.a(to, S, p1=p1), m.a(r0, S, p1=p1), ACT.Sin).then_inc(sined, 1)

            @block.vector
            def _(dve):
                st = Steps(dve_s)
                turn, big, hi = 2.0 * np.pi, 1.5 * 2.0 ** 23, 6.28125
                dve.wait_ge(loaded, 16 * 13)
                nc.vector.tensor_scalar(m.a(w30 + 2 * HW, 2 * HW), m.a(w30, 2 * HW), m.a(v0 + 4, 1), None,
                                        ALU.mult).then_inc(sign_ok, 1)
                for n in range(2):
                    p1 = 64 * (n + 1)
                    u, r = m.a(u0, S, p1=p1), m.a(r0, S, p1=p1)
                    dve.wait_ge(layer, n + 1)
                    nc.vector.tensor_scalar(u, m.bank(2 * n, S, p1=p1), m.a(v0 + 2 * n, 1, p1=p1),
                                            m.a(v0 + 1, 1, p1=p1), ALU.add, ALU.mult)\
                        .then_inc(dve_s, st.tick())
                    dve.wait_ge(dve_s, st.n)
                    nc.vector.tensor_scalar(r, u, float(1.0 / turn), big, ALU.mult, ALU.add)\
                        .then_inc(dve_s, st.tick())
                    dve.wait_ge(dve_s, st.n)
                    nc.vector.tensor_scalar(r, r, big, None, ALU.subtract).then_inc(dve_s, st.tick())
                    dve.wait_ge(dve_s, st.n)
                    nc.vector.scalar_tensor_tensor(out=u, in0=r, scalar=-hi, in1=u, op0=ALU.mult,
                                                   op1=ALU.add).then_inc(dve_s, st.tick())
                    dve.wait_ge(dve_s, st.n)
                    nc.vector.scalar_tensor_tensor(out=u, in0=r, scalar=float(hi - turn), in1=u,
                                                   op0=ALU.mult, op1=ALU.add).then_inc(dve_s, st.tick())
                    dve.wait_ge(dve_s, st.n)
                    nc.vector.tensor_scalar(r, u, 3.1415925, -3.1415925, ALU.min, ALU.max).then_inc(arg, 1)
                dve.wait_ge(sined, 2)
                nc.vector.memset(m.a(a20, 1, 64, P), 0.0).then_inc(sign_ok, 1)
                dve.wait_ge(dec_in, 16)
                for o in range(2):
                    for j in range(8):
                        for q in range(2):
                            n = 2 * (8 * o + j) + q
                            dve.wait_ge(h_sum, n + 1)
                            nc.vector.tensor_tensor(m.a((MT0, HT0)[o] + (8 * q + j) * HW, HW),
                                                    m.bank(4 + n % 4), m.a(dec0 + j * HW, HW),
                                                    ALU.mult).then_inc(h_ok, 1)


def filter_spectrum(nc, m, d, o, k_dram):
    taps = (MT0, HT0)[o]
    f0 = W0
    ko0 = f0 + 2 * FQ
    c0 = ko0 + 2 * FQ
    with Phase(nc, f"spectrum{o}") as ph:
        f_in = [ph.sem("f_in0"), ph.sem("f_in1")]
        dft, odd, k_ok = ph.sem("dft"), ph.sem("odd"), ph.sem("k_ok")
        k_out = [ph.sem("k_out0"), ph.sem("k_out1")]
        with ph.block() as block:
            @block.sync
            def _(sp):
                with sp.Fori(0, QT_N // 2) as i:
                    for s in range(2):
                        sp.wait_ge(dft, 2 * i + s + 1)
                        sp.dma_start(m.a(f0 + s * FQ, FQ), d["c_dft"][bass.ds(2 * i + s, 1), :, :]
                                     .rearrange("a p n -> (a p) n")).then_inc(f_in[s], 16)

            @block.tensor
            def _(pe):
                pe.sem_inc(dft, 2)
                with pe.Fori(0, QT_N // 2) as i:
                    for s in range(2):
                        pe.wait_ge(f_in[s], 16 * i + 16)
                        pe.wait_ge(k_ok, 2 * i + s + 1)
                        for cs in range(2):
                            for par in range(2):
                                for j in range(4):
                                    t = nc.tensor.matmul(
                                        m.bank(4 * s + 2 * cs + par),
                                        m.a(f0 + s * FQ + ((2 * cs + par) * 4 + j) * P, P),
                                        m.a(taps + (8 * cs + 4 * par + j) * HW, HW),
                                        start=(j == 0), stop=(j == 3))
                        t.then_inc(dft, 1)

            @block.scalar
            def _(act):
                act.sem_inc(k_out[0], 16)
                act.sem_inc(k_out[1], 16)
                with act.Fori(0, QT_N // 2) as i:
                    for s in range(2):
                        act.wait_ge(dft, 2 * i + s + 3)
                        odd_sums = m.bank(4 * s, 4 * BANK).rearrange("p (a b n) -> p a b n", a=2, b=2)
                        nc.scalar.activation(m.a(c0 + s * 2 * HW, 2 * HW).rearrange("p (a n) -> p a n", a=2),
                                             odd_sums[:, :, 1, :], ACT.Copy).then_inc(odd, 1)
                        act.wait_ge(k_ok, 2 * i + s + 3)
                        act.dma_start(k_dram[bass.ds(4 * o + 2 * i + s, 1), :, :]
                                      .rearrange("a p n -> (a p) n"),
                                      m.a(ko0 + s * FQ, FQ)).then_inc(k_out[s], 16)
                for s in range(2):
                    act.wait_ge(k_out[s], 16 * (QT_N // 2 + 1))

            @block.vector
            def _(dve):
                dve.sem_inc(k_ok, 2)
                with dve.Fori(0, QT_N // 2) as i:
                    for s in range(2):
                        dve.wait_ge(odd, 2 * i + s + 1)
                        dve.wait_ge(k_out[s], 16 * i + 16)
                        even = m.bank(4 * s, 4 * BANK).rearrange("p (a b n) -> p a b n", a=2, b=2)[:, :, 0, :]
                        odd_c = m.a(c0 + s * 2 * HW, 2 * HW).rearrange("p (a n) -> p a n", a=2)
                        k = m.a(ko0 + s * FQ, FQ).rearrange("p (a b n) -> p a b n", a=2, b=2)
                        nc.vector.tensor_tensor(k[:, :, 0, :], even, odd_c, ALU.add)
                        nc.vector.tensor_tensor(k[:, :, 1, :], even, odd_c, ALU.subtract).then_inc(k_ok, 1)


U0 = W0


def hyena_project(nc, m, d):
    w0 = U0 + 12 * S
    raw0 = w0 + 2 * KC * P
    cw0 = raw0 + 2 * S
    w_ap = d["e_w_in"][0].rearrange("(c p) n -> p c n", p=P)
    with Phase(nc, "hyproj") as ph:
        cw_in = ph.sem("cw_in")
        w_in = [ph.sem("w_in0"), ph.sem("w_in1")]
        summed, copied, conved, dve_s = ph.sem("summed"), ph.sem("copied"), ph.sem("conved"), ph.sem("dve")
        with ph.block() as block:
            @block.sync
            def _(sp):
                with nc.allow_non_contiguous_dma(reason="a few columns of taps and biases"):
                    for t in range(3):
                        sp.dma_start(m.a(cw0 + 12 * t, 12), d["e_conv_w"][0, t, :]
                                     .rearrange("(c p) -> p c", p=P)).then_inc(cw_in, 16)
                    sp.dma_start(m.a(cw0 + 36, 12), d["e_conv_b"][0]
                                 .rearrange("(c p) -> p c", p=P)).then_inc(cw_in, 16)
                with sp.Fori(0, 6) as i:
                    for s in range(2):
                        sp.wait_ge(summed, 2 * i + s + 1)
                        sp.dma_start(m.a(w0 + s * KC * P, KC * P).rearrange("p (c n) -> p c n", c=KC),
                                     w_ap[:, :, bass.ds((2 * i + s) * P, P)]).then_inc(w_in[s], 16)

            @block.tensor
            def _(pe):
                pe.sem_inc(summed, 2)
                with pe.Fori(0, 6) as i:
                    for s in range(2):
                        pe.wait_ge(w_in[s], 16 * i + 16)
                        pe.wait_ge(copied, 2 * i + s + 1)
                        for h in range(2):
                            for c in range(KC):
                                t = nc.tensor.matmul(m.bank(2 * s + h), m.a(w0 + (s * KC + c) * P, P),
                                                     m.a(HT0 + c * S + h * BANK, BANK),
                                                     start=(c == 0), stop=(c == KC - 1))
                        t.then_inc(summed, 1)

            @block.scalar
            def _(act):
                act.sem_inc(copied, 2)
                with act.Fori(0, 6) as i:
                    for s in range(2):
                        act.wait_ge(summed, 2 * i + s + 3)
                        act.wait_ge(conved, 2 * i + s + 1)
                        nc.scalar.activation(m.a(raw0 + s * S, S), m.bank(2 * s, S),
                                             ACT.Copy).then_inc(copied, 1)

            @block.vector
            def _(dve):
                dve.sem_inc(conved, 2)
                dve.wait_ge(cw_in, 64)
                st = Steps(dve_s)
                with dve.Fori(0, 6) as i:
                    st.enter(i, 4)
                    for s in range(2):
                        b = 2 * i + s
                        tap = lambda t: m.dyn(cw0 + 12 * t + b, 1)
                        dve.wait_ge(copied, b + 3)
                        nc.vector.tensor_scalar(m.dyn(U0 + b * S, S), m.a(raw0 + s * S, S), tap(1), tap(3),
                                                ALU.mult, ALU.add).then_inc(dve_s, st.tick())
                        dve.wait_ge(dve_s, st.n)
                        left = m.dyn(U0 + b * S + 1, S - 1)
                        nc.vector.scalar_tensor_tensor(out=left, in0=m.a(raw0 + s * S, S - 1),
                                                       scalar=tap(0), in1=left, op0=ALU.mult,
                                                       op1=ALU.add).then_inc(dve_s, st.tick())
                        dve.wait_ge(dve_s, st.n)
                        right = m.dyn(U0 + b * S, S - 1)
                        nc.vector.scalar_tensor_tensor(out=right, in0=m.a(raw0 + s * S + 1, S - 1),
                                                       scalar=tap(2), in1=right, op0=ALU.mult,
                                                       op1=ALU.add).then_inc(conved, 1)
                    st.leave(6)


def long_conv(nc, m, d, o, k_dram):
    zt0 = U0 + 12 * S
    xs0 = zt0 + 8 * HW
    bias0 = xs0 + FQ
    odd0 = bias0 + 8
    t0 = odd0 + 2 * HW
    assert t0 + 4 * HW <= TOTAL
    pr0 = HT0
    f0, k0 = X0, X0 + 2 * FQ
    g0 = MT0
    with Phase(nc, f"conv{o}") as ph:
        b_in = ph.sem("b_in")
        f_in = [ph.sem("f_in0"), ph.sem("f_in1")]
        k_in = [ph.sem("k_in0"), ph.sem("k_in1")]
        g_in = [ph.pool_dma(m), ph.pool_dma(m)]
        turned, time_ok, dft, odd = ph.sem("turned"), ph.sem("time_ok"), ph.sem("dft"), ph.sem("odd")
        xs_ok, y_ok, inv, gated, dve_s = ph.sem("xs_ok"), ph.sem("y_ok"), ph.sem("inv"), ph.sem("gated"), ph.sem("dve")
        with ph.block() as block:
            @block.sync
            def _(sp):
                with nc.allow_non_contiguous_dma(reason="a few columns of biases"):
                    sp.dma_start(m.a(bias0, 4), d["e_hy_bias"][0, o, :]
                                 .rearrange("(c p) -> p c", p=P)).then_inc(b_in, 16)
                with sp.Fori(0, QT_N // 2) as i:
                    for s in range(2):
                        sp.wait_ge(dft, 2 * i + s + 1)
                        sp.dma_start(m.a(f0 + s * FQ, FQ), d["c_dft"][bass.ds(2 * i + s, 1), :, :]
                                     .rearrange("a p n -> (a p) n")).then_inc(f_in[s], 16)
                        sp.wait_ge(y_ok, 2 * i + s + 1)
                        sp.dma_start(m.a(k0 + s * FQ, FQ), k_dram[bass.ds(4 * o + 2 * i + s, 1), :, :]
                                     .rearrange("a p n -> (a p) n")).then_inc(k_in[s], 16)

            @block.gpsimd
            def _(pool):
                for q in range(QT_N):
                    if q >= 2:
                        pool.wait_ge(inv, q - 1)
                    pool.dma_start(m.a(g0 + (q % 2) * FQ, FQ), d["c_idft"][q]).then_inc(g_in[q % 2], 16)

            @block.tensor
            def _(pe):
                pe.sem_inc(dft, 2)
                for j in range(8):
                    for c in range(4):
                        at = U0 + c * S + 2 * P * (j % 4) + j // 4
                        t = nc.tensor.transpose(m.bank(j, P, at=c * P), m.A[:, at:at + 2 * P - 1:2],
                                                m.ident())
                    t.then_inc(turned, 1)
                pe.wait_ge(time_ok, 8)
                with pe.Fori(0, QT_N // 2) as i:
                    for s in range(2):
                        pe.wait_ge(f_in[s], 16 * i + 16)
                        pe.wait_ge(xs_ok, 2 * i + s + 1)
                        for cs in range(2):
                            for par in range(2):
                                for j in range(4):
                                    t = nc.tensor.matmul(
                                        m.bank(4 * s + 2 * cs + par),
                                        m.a(f0 + s * FQ + ((2 * cs + par) * 4 + j) * P, P),
                                        m.a(zt0 + (4 * par + j) * HW, HW), start=(j == 0), stop=(j == 3))
                        t.then_inc(dft, 1)
                for q in range(QT_N):
                    pe.wait_ge(g_in[q % 2], 16 * (q // 2 + 1))
                    pe.wait_ge(y_ok, 2 + (q + 1 if q >= 1 else QT_N))
                    for c in range(4):
                        for par in range(2):
                            for cs in range(2):
                                t = nc.tensor.matmul(
                                    m.bank(2 * c + par),
                                    m.a(pr0 + q * FQ + (2 * cs + par) * HW + c * P, P),
                                    m.a(g0 + (q % 2) * FQ + (2 * cs + par) * HW, HW),
                                    start=(q == 0 and cs == 0), stop=(q == QT_N - 1 and cs == 1))
                    t.then_inc(inv, 1)

            @block.scalar
            def _(act):
                for j in range(8):
                    act.wait_ge(turned, j + 1)
                    nc.scalar.activation(m.a(zt0 + j * HW, HW), m.bank(j), ACT.Copy).then_inc(time_ok, 1)
                with act.Fori(0, QT_N // 2) as i:
                    for s in range(2):
                        act.wait_ge(dft, 2 * i + s + 3)
                        act.wait_ge(xs_ok, 2 * i + s + 2)
                        odd_sums = m.bank(4 * s, 4 * BANK).rearrange("p (a b n) -> p a b n", a=2, b=2)
                        nc.scalar.activation(m.a(odd0, 2 * HW).rearrange("p (a n) -> p a n", a=2),
                                             odd_sums[:, :, 1, :], ACT.Copy).then_inc(odd, 1)

            @block.vector
            def _(dve):
                dve.sem_inc(xs_ok, 2)
                dve.sem_inc(y_ok, 2)
                st = Steps(dve_s)
                with dve.Fori(0, QT_N // 2) as i:
                    st.enter(i, 14)
                    for s in range(2):
                        dve.wait_ge(odd, 2 * i + s + 1)
                        even = m.bank(4 * s, 4 * BANK).rearrange("p (a b n) -> p a b n", a=2, b=2)[:, :, 0, :]
                        odd_c = m.a(odd0, 2 * HW).rearrange("p (a n) -> p a n", a=2)
                        x = m.a(xs0, FQ).rearrange("p (a b n) -> p a b n", a=2, b=2)
                        nc.vector.tensor_tensor(x[:, :, 0, :], even, odd_c, ALU.add).then_inc(dve_s, st.tick())
                        nc.vector.tensor_tensor(x[:, :, 1, :], even, odd_c, ALU.subtract).then_inc(xs_ok, 1)
                        dve.wait_ge(k_in[s], 16 * i + 16)
                        dve.wait_ge(dve_s, st.n)
                        dve.wait_ge(xs_ok, 2 * i + s + 3)
                        xc, xs = m.a(xs0, 2 * HW), m.a(xs0 + 2 * HW, 2 * HW)
                        kc, ks = m.a(k0 + s * FQ, 2 * HW), m.a(k0 + s * FQ + 2 * HW, 2 * HW)
                        ta, tb = m.a(t0, 2 * HW), m.a(t0 + 2 * HW, 2 * HW)
                        dve.wait_ge(y_ok, 2 * i + s + 2)
                        nc.vector.tensor_tensor(ta, xc, kc, ALU.mult).then_inc(dve_s, st.tick())
                        nc.vector.tensor_tensor(tb, xs, ks, ALU.mult).then_inc(dve_s, st.tick())
                        dve.wait_ge(dve_s, st.n)
                        nc.vector.tensor_tensor(xc, xc, ks, ALU.mult).then_inc(dve_s, st.tick())
                        nc.vector.tensor_tensor(xs, xs, kc, ALU.mult).then_inc(dve_s, st.tick())
                        dve.wait_ge(dve_s, st.n)
                        nc.vector.tensor_tensor(ta, ta, tb, ALU.subtract).then_inc(dve_s, st.tick())
                        dve.wait_ge(dve_s, st.n)
                        nc.vector.tensor_tensor(tb, xc, xs, ALU.add).then_inc(dve_s, st.tick())
                        dve.wait_ge(dve_s, st.n)
                        y = m.a(t0, FQ).rearrange("p (a b n) -> p a b n", a=2, b=2)
                        pr = m.dyn(pr0 + (2 * i + s) * FQ, FQ).rearrange("p (a b n) -> p a b n", a=2, b=2)
                        nc.vector.tensor_tensor(pr[:, :, 0, :], y[:, :, 0, :], y[:, :, 1, :], ALU.add)
                        nc.vector.tensor_tensor(pr[:, :, 1, :], y[:, :, 0, :], y[:, :, 1, :],
                                                ALU.subtract).then_inc(y_ok, 1)
                    st.leave(QT_N // 2)
                dve.wait_ge(b_in, 16)
                dve.wait_ge(inv, QT_N)
                for c in range(4):
                    for par in range(2):
                        at = c * S + par
                        z = m.A[:, U0 + at:U0 + at + S - 1:2]
                        g = m.A[:, U0 + (4 * o + 4) * S + at:U0 + (4 * o + 4) * S + at + S - 1:2]
                        to = z if o == 0 else m.A[:, MT0 + at:MT0 + at + S - 1:2]
                        tmp = m.a(t0 + (par * 2) * HW, HW)
                        nc.vector.scalar_tensor_tensor(out=tmp, in0=z, scalar=m.a(bias0 + c, 1),
                                                       in1=m.bank(2 * c + par), op0=ALU.mult,
                                                       op1=ALU.add).then_inc(dve_s, st.tick())
                        dve.wait_ge(dve_s, st.n)
                        nc.vector.tensor_tensor(to, tmp, g, ALU.mult).then_inc(gated, 1)
def diff_attention(nc, m, d, y_dram):
    DW = 3 * 512
    w0 = W0
    q0 = w0 + 3 * KC * P
    k0, vt0, v0 = q0 + S, q0 + 2 * S, q0 + 3 * S
    mh0 = v0 + S
    MHN = 2 * S - P
    e0 = mh0 + MHN
    at0 = e0 + 4 * S
    oa0 = at0 + 2 * S
    sub0 = oa0 + S
    l0 = sub0 + P
    sm0 = l0 + 384
    sq0 = sm0 + 32
    zero0 = sq0 + P
    assert zero0 + D <= TOTAL
    lam_init = 0.8 - 0.6 * float(np.exp(-0.3 * 0))
    SCALE = 64 ** -0.5
    w_ap = d["e_w_in"][0].rearrange("(c p) n -> p c n", p=P)
    with Phase(nc, "diff") as ph:
        loaded = ph.sem("loaded")
        w_in = [ph.sem(f"w_in{t}") for t in range(3)]
        proj = [ph.sem(f"proj{t}") for t in range(2)]
        q_ok, k_ok, v_half, vt_ok = ph.sem("q_ok"), ph.sem("k_ok"), ph.sem("v_half"), ph.sem("vt_ok")
        v_turned, v_ok = ph.sem("v_turned"), ph.sem("v_ok")
        dve_s, lam_s, lam_e = ph.sem("dve"), ph.sem("lam_s"), ph.sem("lam_e")
        scored, maxed, neg_ok, exped = ph.sem("scored"), ph.sem("maxed"), ph.sem("neg_ok"), ph.sem("exped")
        a_ok, a_turned, at_ok = ph.sem("a_ok"), ph.sem("a_turned"), ph.sem("at_ok")
        pv, o_ok, var_ok, rooted = ph.sem("pv"), ph.sem("o_ok"), ph.sem("var_ok"), ph.sem("rooted")
        normed, o_turned, mixed = ph.sem("normed"), ph.sem("o_turned"), ph.sem("mixed")
        passed = ph.sem("passed")
        zeroed, cleared = ph.sem("zeroed"), ph.pool_dma(m)
        with ph.block() as block:
            @block.gpsimd
            def _(pool):
                first = 2 * S // P
                nc.gpsimd.memset(m.a(zero0, D), 0.0).then_inc(zeroed, 1)
                pool.wait_ge(zeroed, 1)
                with pool.Fori(first, NBLK) as j:
                    pool.dma_start(y_dram[bass.ds(j * P, P), :], m.a(zero0, D)).then_inc(cleared, 16)
                pool.wait_ge(cleared, 16 * (NBLK - first))

            @block.sync
            def _(sp):
                sp.dma_start(m.a(l0, 256), row(d["e_lam"][0].rearrange("a n -> (a n)"))).then_inc(loaded, 16)
                sp.dma_start(m.a(sub0, P), row(d["e_subln"][0])).then_inc(loaded, 16)
                sp.dma_start(m.a(mh0, MHN), d["c_dist"]).then_inc(loaded, 16)
                with sp.Fori(0, 4) as i:
                    for t in range(3):
                        if t < 2:
                            sp.wait_ge(proj[t], i + 1)
                        else:
                            sp.wait_ge(v_half, 2 * i + 1)
                        sp.dma_start(m.a(w0 + t * KC * P, KC * P).rearrange("p (c n) -> p c n", c=KC),
                                     w_ap[:, :, bass.ds(i * P + DW + t * 512, P)]).then_inc(w_in[t], 16)

            @block.tensor
            def _(pe):
                for t in (*proj, v_half):
                    pe.sem_inc(t, 1)

                def project(t, bank, h):
                    for c in range(KC):
                        x = nc.tensor.matmul(m.bank(bank + h), m.a(w0 + (t * KC + c) * P, P),
                                             m.a(HT0 + c * S + h * BANK, BANK),
                                             start=(c == 0), stop=(c == KC - 1))
                    return x

                def queries(i):
                    pe.wait_ge(w_in[0], 16 * i + 16)
                    project(0, 4, 0)
                    project(0, 4, 1).then_inc(proj[0], 1)

                def scores(i, u, s):
                    pe.wait_ge(maxed, 16 * i + 2 * u + s + 1)
                    for h in range(2):
                        x = nc.tensor.matmul(m.bank(2 * s + h), m.a(q0 + u * P, P, 64 * s, 64 * s + 64),
                                             m.a(k0 + h * BANK, BANK, 64 * s, 64 * s + 64),
                                             start=True, stop=True)
                    x.then_inc(scored, 1)

                def pair(i):
                    pe.wait_ge(w_in[1], 16 * i + 16)
                    pe.wait_ge(o_ok, 8 * i + 1)
                    project(1, 6, 0)
                    project(1, 6, 1).then_inc(proj[1], 1)
                    pe.wait_ge(w_in[2], 16 * i + 16)
                    pe.wait_ge(q_ok, i + 1)
                    project(2, 4, 0).then_inc(v_half, 1)
                    pe.wait_ge(k_ok, i + 1)
                    pe.wait_ge(mixed, i + 1)
                    scores(i, 0, 0)
                    scores(i, 0, 1)
                    x = project(2, 4, 1)
                    x.then_inc(v_half, 1)
                    scores(i, 1, 0)
                    scores(i, 1, 1)
                    pe.wait_ge(vt_ok, 2 * i + 2)
                    for j in range(NB):
                        x = nc.tensor.transpose(m.bank(6, P, at=j * P), m.a(vt0 + j * P, P), m.ident())
                    x.then_inc(v_turned, 1)
                    for u in range(1, NB + 1):
                        if u < NB - 1:
                            scores(i, u + 1, 0)
                        pe.wait_ge(a_ok, 8 * i + u)
                        for j in range(NB):
                            x = nc.tensor.transpose(m.bank(4, P, at=j * P),
                                                    m.a(e0 + ((u - 1) % 2) * 2 * S + j * P, P), m.ident())
                        x.then_inc(a_turned, 1)
                        if u < NB - 1:
                            scores(i, u + 1, 1)
                        if u == 1:
                            pe.wait_ge(v_ok, i + 1)
                        pe.wait_ge(at_ok, 8 * i + u)
                        pe.wait_ge(o_ok, 8 * i + u)
                        for j in range(NB):
                            x = nc.tensor.matmul(m.bank(6, P),
                                                 m.a(at0 + ((u - 1) % 2) * S + j * P, P),
                                                 m.a(v0 + j * P, P), start=(j == 0), stop=(j == NB - 1))
                        x.then_inc(pv, 1)

                def turn_outputs(i):
                    pe.wait_ge(normed, i + 1)
                    pe.wait_ge(maxed, 16 * i + 18)
                    for u in range(NB):
                        x = nc.tensor.transpose(m.bank(2, P, at=u * P), m.a(oa0 + u * P, P), m.ident())
                    x.then_inc(o_turned, 1)

                queries(0)
                with pe.Fori(0, 3) as i:
                    pair(i)
                    queries(i + 1)
                    turn_outputs(i)
                pair(3)
                turn_outputs(3)

            @block.scalar
            def _(act):
                act.wait_ge(lam_s, 1)
                nc.scalar.activation(m.a(l0 + 370, 2), m.a(l0 + 368, 2), ACT.Exp).then_inc(lam_e, 1)
                act.sem_inc(mixed, 1)
                act.sem_inc(o_ok, 1)

                def queries(i):
                    act.wait_ge(proj[0], i + 2)
                    nc.scalar.activation(m.a(q0, S), m.bank(4, S), ACT.Copy).then_inc(q_ok, 1)

                def values(i, h):
                    act.wait_ge(v_half, 2 * i + h + 2)
                    nc.scalar.activation(m.a(vt0 + h * BANK, BANK), m.bank(4 + h), ACT.Copy).then_inc(vt_ok, 1)

                def exps(i, u):
                    for s in range(2):
                        e = m.a(e0 + (2 * (u % 2) + s) * S, S)
                        c = sm0 + 16 * (u % 2) + s
                        act.wait_ge(neg_ok, 16 * i + 2 * u + s + 1)
                        nc.scalar.activation(e, e, ACT.Exp, bias=m.a(c + 2, 1), scale=SCALE,
                                             accum_out=m.a(c + 4, 1)).then_inc(exped, 1)

                def pair(i):
                    act.wait_ge(proj[1], i + 2)
                    nc.scalar.activation(m.a(k0, S), m.bank(6, S), ACT.Copy).then_inc(k_ok, 1)
                    values(i, 0)
                    exps(i, 0)
                    values(i, 1)
                    act.wait_ge(v_turned, i + 1)
                    nc.scalar.activation(m.a(v0, S), m.bank(6, S), ACT.Copy).then_inc(v_ok, 1)
                    for u in range(1, NB + 1):
                        if u < NB:
                            exps(i, u)
                        act.wait_ge(a_turned, 8 * i + u)
                        nc.scalar.activation(m.a(at0 + ((u - 1) % 2) * S, S), m.bank(4, S),
                                             ACT.Copy).then_inc(at_ok, 1)
                        act.wait_ge(pv, 8 * i + u)
                        act.wait_ge(o_ok, 8 * i + u)
                        inv = m.a(sm0 + 16 * ((u - 1) % 2) + 6, 1)
                        nc.scalar.activation(m.a(sq0, P), m.bank(6, P), ACT.Square, scale=inv,
                                             accum_out=m.a(ST0 + 16 + u - 1, 1))
                        nc.scalar.activation(m.a(oa0 + (u - 1) * P, P), m.bank(6, P),
                                             ACT.Copy, scale=inv).then_inc(o_ok, 1)
                    act.wait_ge(var_ok, i + 1)
                    nc.scalar.activation(m.a(ST0 + 24, NB), m.a(ST0 + 24, NB), ACT.Sqrt).then_inc(rooted, 1)

                def turned_outputs(i):
                    act.wait_ge(o_turned, i + 1)
                    nc.scalar.activation(m.dyn(MT0 + 4 * S + i * S, S), m.bank(2, S),
                                         ACT.Copy).then_inc(mixed, 1)

                queries(0)
                with act.Fori(0, 3) as i:
                    pair(i)
                    queries(i + 1)
                    turned_outputs(i)
                pair(3)
                turned_outputs(3)

            @block.vector
            def _(dve):
                st = Steps(dve_s)

                def tick(x):
                    x.then_inc(dve_s, st.tick())
                    dve.wait_ge(dve_s, st.n)

                dve.sem_inc(maxed, 2)
                dve.wait_ge(loaded, 48)
                nc.vector.tensor_tensor(m.a(l0, 64), m.a(l0, 64), m.a(l0 + 64, 64), ALU.mult)
                tick(nc.vector.tensor_tensor(m.a(l0 + 128, 64), m.a(l0 + 128, 64), m.a(l0 + 192, 64), ALU.mult))
                nc.vector.reduce_sum(m.a(l0 + 368, 1), m.a(l0, 64), AX_X)
                nc.vector.reduce_sum(m.a(l0 + 369, 1), m.a(l0 + 128, 64), AX_X).then_inc(lam_s, 1)
                dve.wait_ge(lam_e, 1)
                neg_lam = m.a(l0 + 372, 1)
                nc.vector.tensor_scalar(m.a(sub0, P), m.a(sub0, P), 1.0 - lam_init, None, ALU.mult)
                tick(nc.vector.tensor_tensor(neg_lam, m.a(l0 + 371, 1), m.a(l0 + 370, 1), ALU.subtract))
                tick(nc.vector.tensor_scalar(neg_lam, neg_lam, -lam_init, None, ALU.add))

                def scores(i, u):
                    for s in range(2):
                        c = sm0 + 16 * (u % 2) + s
                        dve.wait_ge(scored, 16 * i + 2 * u + s + 1)
                        if s == 0 and u >= 2:
                            dve.wait_ge(a_turned, 8 * i + u - 1)
                        dve.sem_inc(passed, 1)
                        nc.vector.tensor_tensor_reduce(
                            m.a(e0 + (2 * (u % 2) + s) * S, S), m.a(mh0 + (NB - 1 - u) * P, S),
                            m.bank(2 * s, S), 1.0, -3.0e38, ALU.add, ALU.max,
                            m.a(c, 1)).then_inc(maxed, 1)
                        dve.wait_ge(maxed, 16 * i + 2 * u + s + 3)
                        nc.vector.tensor_scalar(m.a(c + 2, 1), m.a(c, 1), -SCALE, None,
                                                ALU.mult).then_inc(neg_ok, 1)

                def difference(i, u):
                    c = sm0 + 16 * (u % 2)
                    ea = e0 + 2 * (u % 2) * S
                    dve.wait_ge(exped, 16 * i + 2 * u + 2)
                    if u >= 2:
                        dve.wait_ge(o_ok, 8 * i + u)
                    tick(nc.vector.reciprocal(m.a(c + 6, 2), m.a(c + 4, 2)))
                    tick(nc.vector.tensor_scalar(m.a(c + 8, 1), m.a(c + 7, 1), m.a(c + 4, 1), neg_lam,
                                                 ALU.mult, ALU.mult))
                    nc.vector.scalar_tensor_tensor(out=m.a(ea, S), in0=m.a(ea + S, S),
                                                   scalar=m.a(c + 8, 1), in1=m.a(ea, S),
                                                   op0=ALU.mult, op1=ALU.add).then_inc(a_ok, 1)

                def pair(i):
                    tick(nc.vector.tensor_scalar(m.a(mh0, MHN), m.a(mh0, MHN), 0.25, None, ALU.mult))
                    scores(i, 0)
                    for u in range(1, NB + 1):
                        if u < NB:
                            scores(i, u)
                        difference(i, u - 1)
                    dve.wait_ge(o_ok, 8 * i + 9)
                    nc.vector.tensor_scalar(m.a(ST0 + 24, NB), m.a(ST0 + 16, NB), 1.0 / P, EPS,
                                            ALU.mult, ALU.add).then_inc(var_ok, 1)
                    dve.wait_ge(rooted, i + 1)
                    tick(nc.vector.reciprocal(m.a(ST0 + 24, NB), m.a(ST0 + 24, NB)))
                    for u in range(NB):
                        o = m.a(oa0 + u * P, P)
                        x = nc.vector.scalar_tensor_tensor(out=o, in0=o, scalar=m.a(ST0 + 24 + u, 1),
                                                           in1=m.a(sub0, P), op0=ALU.mult, op1=ALU.mult)
                    x.then_inc(normed, 1)
                    tick(nc.vector.memset(m.a(sm0 + 31, 1), 0.0))

                with dve.Fori(0, 3) as i:
                    st.enter(i, 1 + NB * 2 + 1 + 1)
                    pair(i)
                    st.leave(3)
                pair(3)


def window_attention(nc, m, d):
    HD, HG, WINW = 64, 4, 3 * P
    NT = HG + 2
    w0 = W0
    q0 = w0 + NT * KC * P
    k0 = q0 + HG * S
    v0 = k0 + S
    mh0 = v0 + S
    e0 = mh0 + 2 * HG * WINW
    pt0 = e0 + 2 * 8 * WINW
    oa0 = pt0 + 2 * 2 * WINW
    sk0 = oa0 + 2 * 4 * P
    sm0 = sk0 + 32
    assert sm0 + 128 <= TOTAL, sm0 + 128 - TOTAL
    SCALE = HD ** -0.5
    w_ap = d["o_w_in"][0].rearrange("(c p) n -> p c n", p=P)
    STEPS = 2 * HG

    def keys(u):
        return max(u - 1, 0), min(u + 1, NB - 1)

    with Phase(nc, "gqa") as ph:
        loaded = ph.sem("loaded")
        w_in = [ph.sem(f"w_in{t}") for t in range(NT)]
        proj = [ph.sem(f"proj{t}") for t in range(NT)]
        qkv_ok, v_turned, v_ok = ph.sem("qkv_ok"), ph.sem("v_turned"), ph.sem("v_ok")
        dve_s, scored, maxed, neg_ok = ph.sem("dve"), ph.sem("scored"), ph.sem("maxed"), ph.sem("neg_ok")
        exped, p_turned, pt_ok, pv = ph.sem("exped"), ph.sem("p_turned"), ph.sem("pt_ok"), ph.sem("pv")
        o_ok, o_turned, mixed, sink_e = ph.sem("o_ok"), ph.sem("o_turned"), ph.sem("mixed"), ph.sem("sink_e")
        passed = ph.sem("passed")
        vt = q0
        with ph.block() as block:
            @block.sync
            def _(sp):
                sp.dma_start(m.a(sk0, 16), row(d["o_sink"][0])).then_inc(loaded, 16)
                sp.dma_start(m.a(mh0, 2 * HG * WINW), d["c_window"]).then_inc(loaded, 16)
                with sp.Fori(0, 2) as i:
                    for t in (5, 4, 0, 1, 2, 3):
                        sp.wait_ge(proj[t], i + 1)
                        if t < HG:
                            for g in range(2):
                                sp.dma_start(m.a(w0 + t * KC * P, KC * P)
                                             .rearrange("p (c n) -> p c n", c=KC)[:, :, 64 * g:64 * g + 64],
                                             w_ap[:, :, bass.ds(i * 512 + g * 256 + t * 64, 64)])\
                                    .then_inc(w_in[t], 16)
                        else:
                            sp.dma_start(m.a(w0 + t * KC * P, KC * P).rearrange("p (c n) -> p c n", c=KC),
                                         w_ap[:, :, bass.ds(i * P + 1024 + (t - 4) * 256, P)])\
                                .then_inc(w_in[t], 16)

            @block.tensor
            def _(pe):
                for t in range(NT):
                    pe.sem_inc(proj[t], 1)
                with pe.Fori(0, 2) as i:
                    def project(t, b):
                        pe.wait_ge(w_in[t], (32 if t < HG else 16) * (i + 1))
                        for h in range(2):
                            for c in range(KC):
                                x = nc.tensor.matmul(m.bank(b + h), m.a(w0 + (t * KC + c) * P, P),
                                                     m.a(HT0 + c * S + h * BANK, BANK),
                                                     start=(c == 0), stop=(c == KC - 1))
                        x.then_inc(proj[t], 1)

                    pe.wait_ge(mixed, 8 * i + 1)
                    project(5, 0)
                    project(4, 2)
                    project(0, 4)
                    project(1, 6)
                    pe.wait_ge(qkv_ok, 6 * i + 1)
                    for j in range(NB):
                        x = nc.tensor.transpose(m.bank(0, P, at=j * P), m.a(vt + j * P, P), m.ident())
                    x.then_inc(v_turned, 1)
                    pe.wait_ge(qkv_ok, 6 * i + 2)
                    project(2, 2)
                    pe.wait_ge(v_ok, i + 1)
                    project(3, 0)
                    pe.wait_ge(qkv_ok, 6 * i + 6)

                    def scores(n):
                        j, u0 = n // 2, 4 * (n % 2)
                        for u in range(u0, u0 + 4):
                            a, z = keys(u)
                            for s in range(2):
                                pe.wait_ge(maxed, 64 * i + 8 * n + 2 * (u - u0) + s + 1)
                                nc.tensor.matmul(m.bank(2 * (u % 2) + s, (z - a + 1) * P),
                                                 m.a(q0 + j * S + u * P, P, 64 * s, 64 * s + 64),
                                                 m.a(k0 + a * P, (z - a + 1) * P, 64 * s, 64 * s + 64),
                                                 start=True, stop=True).then_inc(scored, 1)

                    def turn_probs(n, u, s):
                        a, z = keys(u)
                        k = 8 * n + 2 * (u % 4) + s
                        pe.wait_ge(exped, 64 * i + k + 1)
                        pe.wait_ge(pt_ok, 64 * i + k + 1)
                        for b in range(z - a + 1):
                            x = nc.tensor.transpose(
                                m.bank(4 + s, P, at=b * P),
                                m.a(e0 + (n % 2) * 8 * WINW + (2 * (u % 4) + s) * WINW + b * P, P),
                                m.ident())
                        x.then_inc(p_turned, 1)

                    def weigh(n, u, s):
                        a, z = keys(u)
                        k = 8 * n + 2 * (u % 4) + s
                        pe.wait_ge(pt_ok, 64 * i + k + 3)
                        if k % 8 == 0:
                            pe.wait_ge(o_ok, 8 * i + n + 1)
                        for b in range(z - a + 1):
                            x = nc.tensor.matmul(
                                m.bank(6, HD, at=(u % 4) * P + s * HD),
                                m.a(pt0 + ((u % 2) * 2 + s) * WINW + b * P, P),
                                m.a(v0 + (a + b) * P + s * HD, HD),
                                start=(b == 0), stop=(b == z - a))
                        x.then_inc(pv, 1)

                    def outputs(n):
                        u0 = 4 * (n % 2)
                        for u in range(u0, u0 + 5):
                            for s in range(2):
                                if u < u0 + 4:
                                    turn_probs(n, u, s)
                                if u > u0:
                                    weigh(n, u - 1, s)

                    def turn_outputs(n):
                        pe.wait_ge(o_ok, 8 * i + n + 2)
                        pe.wait_ge(mixed, 8 * i + n + 1)
                        for u in range(4):
                            x = nc.tensor.transpose(m.bank(7, P, at=u * P),
                                                    m.a(oa0 + (n % 2) * 4 * P + u * P, P), m.ident())
                        x.then_inc(o_turned, 1)

                    scores(0)
                    for n in range(STEPS):
                        if n + 1 < STEPS:
                            scores(n + 1)
                        outputs(n)
                        if n >= 1:
                            turn_outputs(n - 1)
                    turn_outputs(STEPS - 1)

            @block.scalar
            def _(act):
                act.sem_inc(mixed, 1)
                act.sem_inc(pt_ok, 2)
                with act.Fori(0, 2) as i:
                    act.wait_ge(proj[5], i + 2)
                    nc.scalar.activation(m.a(vt, S), m.bank(0, S), ACT.Copy).then_inc(qkv_ok, 1)
                    act.wait_ge(proj[4], i + 2)
                    nc.scalar.activation(m.a(k0, S), m.bank(2, S), ACT.Copy).then_inc(qkv_ok, 1)
                    act.wait_ge(v_turned, i + 1)
                    nc.scalar.activation(m.a(v0, S), m.bank(0, S), ACT.Copy).then_inc(v_ok, 1)
                    for t, b in ((0, 4), (1, 6), (2, 2), (3, 0)):
                        act.wait_ge(proj[t], i + 2)
                        nc.scalar.activation(m.a(q0 + t * S, S), m.bank(b, S), ACT.Copy).then_inc(qkv_ok, 1)

                    def exps(n):
                        act.wait_ge(neg_ok, 8 * i + n + 1)
                        u0 = 4 * (n % 2)
                        c = sm0 + 64 * (n % 2)
                        nc.scalar.activation(m.a(c + 24, 8), m.a(c + 24, 8), ACT.Exp).then_inc(sink_e, 1)
                        for u in range(u0, u0 + 4):
                            a, z = keys(u)
                            for s in range(2):
                                k = 2 * (u - u0) + s
                                e = m.a(e0 + (n % 2) * 8 * WINW + k * WINW, (z - a + 1) * P)
                                nc.scalar.activation(e, e, ACT.Exp, bias=m.a(c + 8 + k, 1), scale=SCALE,
                                                     accum_out=m.a(c + 16 + k, 1)).then_inc(exped, 1)

                    def moves(n):
                        u0 = 4 * (n % 2)
                        for u in range(u0, u0 + 4):
                            a, z = keys(u)
                            for s in range(2):
                                k = 8 * n + 2 * (u - u0) + s
                                act.wait_ge(p_turned, 64 * i + k + 1)
                                nc.scalar.activation(m.a(pt0 + ((u % 2) * 2 + s) * WINW, (z - a + 1) * P),
                                                     m.bank(4 + s, (z - a + 1) * P),
                                                     ACT.Copy).then_inc(pt_ok, 1)

                    def mix(n):
                        act.wait_ge(o_turned, 8 * i + n + 1)
                        nc.scalar.activation(m.dyn(MT0 + i * 4 * S + (n // 2) * S + (n % 2) * BANK, BANK),
                                             m.bank(7), ACT.Copy).then_inc(mixed, 1)

                    exps(0)
                    for n in range(STEPS):
                        moves(n)
                        if n + 1 < STEPS:
                            exps(n + 1)
                        if n >= 1:
                            mix(n - 1)
                    mix(STEPS - 1)

            @block.vector
            def _(dve):
                st = Steps(dve_s)

                def tick(x):
                    x.then_inc(dve_s, st.tick())
                    dve.wait_ge(dve_s, st.n)

                dve.sem_inc(maxed, 4)
                dve.sem_inc(o_ok, 1)
                dve.wait_ge(loaded, 32)
                with dve.Fori(0, 2) as i:
                    st.enter(i, 2 + STEPS * 3)
                    tick(nc.vector.tensor_scalar(m.a(sk0 + 16, 8), m.dyn(sk0 + i * 8, 8), 1.0 / SCALE, None,
                                                 ALU.mult))

                    def head(n):
                        j, u0 = n // 2, 4 * (n % 2)
                        c = sm0 + 64 * (n % 2)
                        if n >= 2:
                            dve.wait_ge(p_turned, 64 * i + 8 * (n - 1))
                        for u in range(u0, u0 + 4):
                            a, z = keys(u)
                            for s in range(2):
                                k = 2 * (u - u0) + s
                                w = (z - a + 1) * P
                                dve.wait_ge(scored, 64 * i + 8 * n + k + 1)
                                dve.sem_inc(passed, 1)
                                nc.vector.tensor_tensor_reduce(
                                    m.a(e0 + (n % 2) * 8 * WINW + k * WINW, w),
                                    m.a(mh0 + (2 * j + s) * WINW + (a - u + 1) * P, w),
                                    m.bank(2 * (u % 2) + s, w), 1.0, -3.0e38, ALU.add, ALU.max,
                                    m.a(c + k, 1)).then_inc(maxed, 1)
                        dve.wait_ge(maxed, 64 * i + 8 * n + 8 + 4)
                        mx = m.a(c, 8).rearrange("p (u s) -> p u s", s=2)
                        for s in range(2):
                            x = nc.vector.tensor_scalar(mx[:, :, s], mx[:, :, s], m.a(sk0 + 16 + 4 * s + j, 1),
                                                        None, ALU.max)
                        tick(x)
                        for s in range(2):
                            x = nc.vector.tensor_scalar(m.a(c + 24, 8).rearrange("p (u s) -> p u s", s=2)[:, :, s],
                                                        mx[:, :, s], m.a(sk0 + 16 + 4 * s + j, 1), -SCALE,
                                                        ALU.subtract, ALU.mult)
                        nc.vector.tensor_scalar(m.a(c + 8, 8), m.a(c, 8), -SCALE, None,
                                                ALU.mult).then_inc(neg_ok, 1)

                    def tail(n):
                        c = sm0 + 64 * (n % 2)
                        dve.wait_ge(exped, 64 * i + 8 * n + 8)
                        dve.wait_ge(sink_e, 8 * i + n + 1)
                        tick(nc.vector.tensor_tensor(m.a(c + 16, 8), m.a(c + 16, 8), m.a(c + 24, 8), ALU.add))
                        tick(nc.vector.reciprocal(m.a(c + 16, 8), m.a(c + 16, 8)))
                        dve.wait_ge(pv, 64 * i + 8 * n + 8)
                        nc.vector.tensor_tensor(
                            m.a(oa0 + (n % 2) * 4 * P, 4 * P).rearrange("p (k e) -> p k e", k=8),
                            m.bank(6, 4 * P).rearrange("p (k e) -> p k e", k=8),
                            m.a(c + 16, 8).rearrange("p (k o) -> p k o", o=1).to_broadcast([P, 8, HD]),
                            ALU.mult).then_inc(o_ok, 1)

                    head(0)
                    for n in range(STEPS):
                        if n + 1 < STEPS:
                            head(n + 1)
                        tail(n)
                    tick(nc.vector.tensor_scalar(m.a(mh0, 2 * HG * WINW), m.a(mh0, 2 * HG * WINW), 0.0625, None,
                                                 ALU.mult))
                    st.leave(2)
def cross_attention(nc, m, d, layer):
    w0 = W0
    q0 = w0 + 6 * KC * P
    k0 = q0 + 2 * S
    v0 = k0 + 2 * M_LEN
    e0 = v0 + 2 * M_LEN
    pt0 = e0 + 2 * NB * M_LEN
    sm0 = pt0 + 2 * S
    assert sm0 + 48 <= TOTAL
    SCALE = 128 ** -0.5
    wq = d["c_wq"][layer].rearrange("(c p) n -> p c n", p=P)
    wkv = d["c_wkv"][layer].rearrange("(c p) n -> p c n", p=P)
    with Phase(nc, f"cross{layer}") as ph:
        w_in = [[ph.sem(f"w{t}_in{s}") for s in range(2)] for t in "qkv"]
        qp, kp, vp, kv_ok, q_ok = ph.sem("qp"), ph.sem("kp"), ph.sem("vp"), ph.sem("kv_ok"), ph.sem("q_ok")
        scored, neg_ok, exped, p_ok = ph.sem("scored"), ph.sem("neg_ok"), ph.sem("exped"), ph.sem("p_ok")
        p_turned, pt_ok, pv, mixed, dve_s = ph.sem("p_turned"), ph.sem("pt_ok"), ph.sem("pv"), ph.sem("mixed"), ph.sem("dve")
        with ph.block() as block:
            @block.sync
            def _(sp):
                for h in range(XH):
                    s = h % 2
                    for t, w in enumerate((wq[:, :, h * P:(h + 1) * P], wkv[:, :, h * P:(h + 1) * P],
                                           wkv[:, :, (XH + h) * P:(XH + h + 1) * P])):
                        if h >= 2:
                            sp.wait_ge((qp, kp, vp)[t], h - 1)
                        sp.dma_start(m.a(w0 + (3 * s + t) * KC * P, KC * P)
                                     .rearrange("p (c n) -> p c n", c=KC), w).then_inc(w_in[t][s], 16)

            @block.tensor
            def _(pe):
                def project(h):
                    s = h % 2
                    w = lambda t, c: w0 + ((3 * s + t) * KC + c) * P
                    for t in range(3):
                        pe.wait_ge(w_in[t][s], 16 * (h // 2 + 1))
                        if h >= 1 and t == 0:
                            pe.wait_ge(kv_ok, 2 * h)
                        if h >= 2 and t == 0:
                            pe.wait_ge(pt_ok, 2 * (h - 1))
                        if t == 0:
                            for b in range(2):
                                for c in range(KC):
                                    x = nc.tensor.matmul(m.bank(b), m.a(w(0, c), P),
                                                         m.a(HT0 + c * S + b * BANK, BANK),
                                                         start=(c == 0), stop=(c == KC - 1))
                            x.then_inc(qp, 1)
                        elif t == 1:
                            for c in range(KC):
                                x = nc.tensor.matmul(m.bank(6, M_LEN), m.a(w(1, c), P),
                                                     m.a(ME0 + c * M_LEN, M_LEN),
                                                     start=(c == 0), stop=(c == KC - 1))
                            x.then_inc(kp, 1)
                        else:
                            for b in range(2):
                                for c in range(KC):
                                    x = nc.tensor.matmul(m.bank(7, P, at=b * P),
                                                         m.a(ME0 + c * M_LEN + b * P, P), m.a(w(2, c), P),
                                                         start=(c == 0), stop=(c == KC - 1))
                            x.then_inc(vp, 1)

                def scores(h):
                    s = h % 2
                    pe.wait_ge(q_ok, h + 1)
                    pe.wait_ge(kv_ok, 2 * h + 1)
                    if h >= 1:
                        pe.wait_ge(mixed, h)
                    for u in range(NB):
                        x = nc.tensor.matmul(m.bank(2 + u // 2, M_LEN, at=(u % 2) * M_LEN),
                                             m.a(q0 + s * S + u * P, P), m.a(k0 + s * M_LEN, M_LEN),
                                             start=True, stop=True)
                    x.then_inc(scored, 1)

                def outputs(h):
                    s = h % 2
                    pe.wait_ge(p_ok, h + 1)
                    pe.wait_ge(kv_ok, 2 * min(h + 2, XH))
                    pe.wait_ge(q_ok, min(h + 2, XH))
                    for b in range(2):
                        for u in range(NB):
                            x = nc.tensor.transpose(m.bank(6 * b, P, at=u * P),
                                                    m.a(e0 + (s * NB + u) * M_LEN + b * P, P), m.ident())
                        x.then_inc(p_turned, 1)
                    pe.wait_ge(pt_ok, 2 * h + 2)
                    for half in range(2):
                        for b in range(2):
                            x = nc.tensor.matmul(m.bank(2 + half), m.a(v0 + s * M_LEN + b * P, P),
                                                 m.a(pt0 + b * S + half * BANK, BANK),
                                                 start=(b == 0), stop=(b == 1))
                    x.then_inc(pv, 1)

                project(0)
                scores(0)
                for h in range(XH):
                    if h + 1 < XH:
                        project(h + 1)
                    outputs(h)
                    if h + 1 < XH:
                        scores(h + 1)

            @block.scalar
            def _(act):
                def copies(h):
                    s = h % 2
                    act.wait_ge(qp, h + 1)
                    nc.scalar.activation(m.a(q0 + s * S, S), m.bank(0, S), ACT.Copy).then_inc(q_ok, 1)
                    act.wait_ge(kp, h + 1)
                    nc.scalar.activation(m.a(k0 + s * M_LEN, M_LEN), m.bank(6, M_LEN),
                                         ACT.Copy).then_inc(kv_ok, 1)
                    act.wait_ge(vp, h + 1)
                    nc.scalar.activation(m.a(v0 + s * M_LEN, M_LEN), m.bank(7, M_LEN),
                                         ACT.Copy).then_inc(kv_ok, 1)

                copies(0)
                for h in range(XH):
                    s = h % 2
                    c = sm0 + 24 * s
                    act.wait_ge(neg_ok, h + 1)
                    for u in range(NB):
                        x = nc.scalar.activation(m.a(e0 + (s * NB + u) * M_LEN, M_LEN),
                                                 m.bank(2 + u // 2, M_LEN, at=(u % 2) * M_LEN), ACT.Exp,
                                                 bias=m.a(c + 8 + u, 1), scale=SCALE,
                                                 accum_out=m.a(c + 16 + u, 1))
                    x.then_inc(exped, 1)
                    if h + 1 < XH:
                        copies(h + 1)
                    for b in range(2):
                        act.wait_ge(p_turned, 2 * h + b + 1)
                        nc.scalar.activation(m.a(pt0 + b * S, S), m.bank(6 * b, S), ACT.Copy).then_inc(pt_ok, 1)
                    act.wait_ge(pv, h + 1)
                    nc.scalar.activation(m.a(MT0 + h * S, S), m.bank(2, S), ACT.Copy).then_inc(mixed, 1)

            @block.vector
            def _(dve):
                st = Steps(dve_s)

                def tick(x):
                    x.then_inc(dve_s, st.tick())
                    dve.wait_ge(dve_s, st.n)

                for h in range(XH):
                    s = h % 2
                    c = sm0 + 24 * s
                    dve.wait_ge(scored, h + 1)
                    tick(nc.vector.tensor_reduce(m.a(c, NB), m.bank(2, 4 * BANK)
                                                 .rearrange("p (u n) -> p u n", u=NB), AX_X, ALU.max))
                    nc.vector.tensor_scalar(m.a(c + 8, NB), m.a(c, NB), -SCALE, None, ALU.mult).then_inc(neg_ok, 1)
                    dve.wait_ge(exped, h + 1)
                    tick(nc.vector.reciprocal(m.a(c + 16, NB), m.a(c + 16, NB)))
                    e = m.a(e0 + s * NB * M_LEN, NB * M_LEN).rearrange("p (u n) -> p u n", u=NB)
                    r = m.a(c + 16, NB).rearrange("p (u o) -> p u o", o=1).to_broadcast([P, NB, M_LEN])
                    nc.vector.tensor_tensor(e, e, r, ALU.mult).then_inc(p_ok, 1)


MOE_W = W0
MOE_X = MOE_W + 2 * KC * EH
MOE_XT = MOE_X + 2 * D
MOE_HM = MOE_XT + 2 * D
MOE_HT = MOE_HM + 2 * EH
MOE_Y = MOE_HT + 2 * EH
MOE_IX = MOE_Y + 2 * D
MOE_END = MOE_IX + 2

SLOT0 = ST0 + 64
WT0 = ST0 + 80
TRIPS = ST0 + 100
BE0 = ST0 + 104


def route(nc, m, d, ph, block, layer, table, routed, tabled):
    at = MOE_END

    def room(n):
        nonlocal at
        at += n
        return at - n

    bias0, lg0 = room(NR), room(NB * NR)
    iota0, tri0, tok0, one0, zero0 = room(NBLK), room(P), room(NB), room(P), room(NBLK)
    g80, gm0, gi0, gf0, goh0 = room(64), room(64), room(64), room(NB), room(NB * NG)
    es0, em0, ei0, tmp0 = room(64), room(64), room(64), room(64)
    ef0, gx0, gs0, ed0, den0 = room(2 * NB), room(NB * NG), room(NB), room(NB), room(NB)
    mk0, ms0, tot0, pre0, sl0, pick0 = room(512), room(256), room(256), room(256), room(256), room(512)
    cnt0, i1280, cmp0, nb0, pend0, pst0 = room(NE), room(NB), room(NE * NB), room(NE), room(NE), room(NE)
    ones0, le0, be0, tr0, slf0 = room(NE), room(NBLK * NE), room(NBLK), room(NBLK), room(2 * NB)
    assert at <= TOTAL

    def b3(ap, a, b):
        return ap.rearrange("p (a o) -> p a o", o=1).to_broadcast([P, a, b])

    def b2(ap, a, b):
        return ap.rearrange("p (o b) -> p o b", o=1).to_broadcast([P, a, b])

    def t3(ap, a):
        return ap.rearrange("p (a b) -> p a b", a=a)

    loaded, zeroed, cleared = ph.sem("loaded"), ph.sem("zeroed"), ph.sem("cleared")
    ex_in, ex_out, marked, counted = ph.sem("ex_in"), ph.sem("ex_out"), ph.sem("marked"), ph.sem("counted")
    slots_ok, scattered, dve_s = ph.sem("slots_ok"), ph.pool_dma(m), ph.sem("dve")
    @block.sync
    def _(sp):
        sp.dma_start(m.a(bias0, NG), row(d["f_b_grp"][layer])).then_inc(loaded, 16)
        sp.dma_start(m.a(bias0 + NG, NE), row(d["f_b_exp"][layer])).then_inc(loaded, 16)
        sp.dma_start(m.a(iota0, NBLK), d["c_iota"]).then_inc(loaded, 16)
        sp.dma_start(m.a(tri0, P), d["c_tri"]).then_inc(loaded, 16)
        sp.dma_start(m.a(tok0, NB).bitcast(I32), d["c_tok"]).then_inc(loaded, 16)
        sp.wait_ge(zeroed, 1)
        sp.dma_start(table.rearrange("(p n) o -> p (n o)", p=P),
                     m.a(zero0, NBLK).bitcast(I32)).then_inc(cleared, 16)
        sp.wait_ge(cleared, 16)

    @block.gpsimd
    def _(pool):
        nc.gpsimd.memset(m.a(one0, P), 1.0)
        nc.gpsimd.memset(m.a(zero0, NBLK), 0.0).then_inc(zeroed, 1)
        pool.wait_ge(cleared, 16)
        pool.wait_ge(slots_ok, 1)
        pool.wait_ge(loaded, 80)
        for k in range(2):
            for b in range(NB):
                pool.indirect_dma_start(
                    table, bass.IndirectOffsetOnAxis(ap=m.a(SLOT0 + 8 * k + b, 1).bitcast(U32), axis=0),
                    m.a(tok0 + b, 1).bitcast(I32), None).then_inc(scattered, 16)
        pool.wait_ge(scattered, 16 * 2 * NB)
        pool.sem_inc(tabled, 1)

    @block.tensor
    def _(pe):
        pe.wait_ge(loaded, 80)
        pe.wait_ge(marked, 1)
        pe.wait_ge(zeroed, 1)
        nc.tensor.matmul(m.bank(1, 256), m.a(tri0, P), m.a(ms0, 256), start=True, stop=True)
        nc.tensor.matmul(m.bank(2, 256), m.a(one0, P), m.a(ms0, 256), start=True,
                         stop=True).then_inc(counted, 1)

    @block.scalar
    def _(act):
        act.wait_ge(ex_in, 1)
        nc.scalar.activation(m.a(gx0, NB * NG), m.a(gx0, NB * NG), ACT.Exp)
        nc.scalar.activation(m.a(ed0, NB), m.a(ed0, NB), ACT.Exp).then_inc(ex_out, 1)

    @block.vector
    def _(dve):
        st = Steps(dve_s)
        v = nc.vector

        def tick(x):
            x.then_inc(dve_s, st.tick())
            dve.wait_ge(dve_s, st.n)

        v.memset(m.a(g80, 64), -3.0e38)
        dve.wait_ge(loaded, 80)
        lg = t3(m.a(lg0, NB * NR), NB)
        tick(v.tensor_tensor(lg, t3(m.bank(ROUTE_BANK, NB * NR), NB), b2(m.a(bias0, NR), NB, NR), ALU.add))
        tick(v.tensor_copy(t3(m.a(g80, 64), NB)[:, :, 0:NG], lg[:, :, 0:NG]))
        for b in range(NB):
            x = v.max(m.a(gm0 + 8 * b, 8), m.a(g80 + 8 * b, 8))
        tick(x)
        for b in range(NB):
            x = v.max_index(m.a(gi0 + 8 * b, 8).bitcast(U32), m.a(gm0 + 8 * b, 8), m.a(g80 + 8 * b, 8))
        tick(x)
        gm = t3(m.a(gm0, 64), NB)[:, :, 0:1]
        tick(v.tensor_copy(m.a(gf0, NB), t3(m.a(gi0, 64), NB)[:, :, 0].bitcast(U32)))
        v.tensor_tensor(t3(m.a(gx0, NB * NG), NB), lg[:, :, 0:NG], gm.to_broadcast([P, NB, NG]),
                        ALU.subtract)
        tick(v.tensor_tensor(t3(m.a(goh0, NB * NG), NB), b3(m.a(gf0, NB), NB, NG),
                             b2(m.a(iota0, NG), NB, NG), ALU.is_equal))
        goh = t3(m.a(goh0, NB * NG), NB)
        es, tmp = t3(m.a(es0, 64), NB), t3(m.a(tmp0, 64), NB)
        for g in range(NG):
            part = lg[:, :, NG + EG * g:NG + EG * (g + 1)]
            tick(v.tensor_tensor(es if g == 0 else tmp, part,
                                 goh[:, :, g:g + 1].to_broadcast([P, NB, EG]), ALU.mult))
            if g:
                tick(v.tensor_tensor(es, es, tmp, ALU.add))
        for b in range(NB):
            x = v.max(m.a(em0 + 8 * b, 8), m.a(es0 + 8 * b, 8))
        tick(x)
        for b in range(NB):
            x = v.max_index(m.a(ei0 + 8 * b, 8).bitcast(U32), m.a(em0 + 8 * b, 8), m.a(es0 + 8 * b, 8))
        em = t3(m.a(em0, 64), NB)
        tick(x)
        v.tensor_tensor(m.a(ed0, NB), em[:, :, 1], em[:, :, 0], ALU.subtract).then_inc(ex_in, 1)
        for k in range(2):
            tick(v.tensor_copy(m.a(ef0 + k * NB, NB), t3(m.a(ei0, 64), NB)[:, :, k].bitcast(U32)))
            tick(v.scalar_tensor_tensor(out=m.a(ef0 + k * NB, NB), in0=m.a(gf0, NB), scalar=float(EG),
                                        in1=m.a(ef0 + k * NB, NB), op0=ALU.mult, op1=ALU.add))
            tick(v.tensor_tensor(t3(m.a(mk0 + 256 * k, 256), NB), b3(m.a(ef0 + k * NB, NB), NB, NE),
                                 b2(m.a(iota0, NE), NB, NE), ALU.is_equal))
        v.tensor_tensor(m.a(ms0, 256), m.a(mk0, 256), m.a(mk0 + 256, 256), ALU.add).then_inc(marked, 1)
        dve.wait_ge(ex_out, 1)
        tick(v.tensor_reduce(m.a(gs0, NB), t3(m.a(gx0, NB * NG), NB), AX_X, ALU.add))
        tick(v.scalar_tensor_tensor(out=m.a(den0, NB), in0=m.a(ed0, NB), scalar=1.0, in1=m.a(gs0, NB),
                                    op0=ALU.add, op1=ALU.mult))
        tick(v.reciprocal(m.a(WT0, NB), m.a(den0, NB)))
        v.tensor_tensor(m.a(WT0 + NB, NB), m.a(WT0, NB), m.a(ed0, NB), ALU.mult)
        dve.wait_ge(counted, 1)
        v.memset(m.a(pre0, NE), 0.0)
        tick(v.tensor_copy(m.a(tot0, 256), m.bank(2, 256)))
        for b in range(1, NB + 1):
            to = cnt0 if b == NB else pre0 + b * NE
            tick(v.tensor_tensor(m.a(to, NE), m.a(pre0 + (b - 1) * NE, NE),
                                 m.a(tot0 + (b - 1) * NE, NE), ALU.add))
        v.tensor_tensor(m.a(sl0, 256), m.a(pre0, 256), m.bank(1, 256), ALU.add)
        tick(v.tensor_scalar(m.a(i1280, NB), m.a(iota0, NB), float(P), None, ALU.mult))
        tick(v.tensor_tensor(t3(m.a(cmp0, NE * NB), NE), b3(m.a(cnt0, NE), NE, NB),
                             b2(m.a(i1280, NB), NE, NB), ALU.is_gt))
        v.memset(m.a(ones0, NE), 1.0)
        tick(v.tensor_reduce(m.a(nb0, NE), t3(m.a(cmp0, NE * NB), NE), AX_X, ALU.add))
        tick(v.tensor_tensor_scan(m.a(pend0, NE), m.a(ones0, NE), m.a(nb0, NE), 0.0, ALU.mult, ALU.add))
        tick(v.tensor_tensor(m.a(pst0, NE), m.a(pend0, NE), m.a(nb0, NE), ALU.subtract))
        tick(v.tensor_scalar(m.a(pst0, NE), m.a(pst0, NE), float(P), None, ALU.mult))
        tick(v.tensor_tensor(t3(m.a(sl0, 256), NB), t3(m.a(sl0, 256), NB), b2(m.a(pst0, NE), NB, NE),
                             ALU.add))
        for k in range(2):
            tick(v.tensor_tensor(m.a(pick0 + 256 * k, 256), m.a(mk0 + 256 * k, 256), m.a(sl0, 256),
                                 ALU.mult))
        tick(v.tensor_reduce(m.a(slf0, 2 * NB), t3(m.a(pick0, 512), 2 * NB), AX_X, ALU.add))
        v.tensor_copy(m.a(SLOT0, 2 * NB).bitcast(U32), m.a(slf0, 2 * NB)).then_inc(slots_ok, 1)
        tick(v.tensor_tensor(t3(m.a(le0, NBLK * NE), NBLK), b2(m.a(pend0, NE), NBLK, NE),
                             b3(m.a(iota0, NBLK), NBLK, NE), ALU.is_le))
        tick(v.tensor_reduce(m.a(be0, NBLK), t3(m.a(le0, NBLK * NE), NBLK), AX_X, ALU.add))
        tick(v.tensor_scalar(m.a(be0, NBLK), m.a(be0, NBLK), float(NE - 1), None, ALU.min))
        v.tensor_copy(m.a(BE0, NBLK).bitcast(I32), m.a(be0, NBLK))
        tick(v.tensor_tensor(m.a(tr0, NBLK // 2), m.a(pend0 + NE - 1, 1).to_broadcast([P, NBLK // 2]),
                             m.a(iota0, NBLK).rearrange("p (a b) -> p a b", b=2)[:, :, 0], ALU.is_gt))
        tick(v.tensor_reduce(m.a(cnt0, 1), m.a(tr0, NBLK // 2), AX_X, ALU.add))
        v.tensor_copy(m.a(TRIPS, 1).bitcast(I32), m.a(cnt0, 1)).then_inc(routed, 1)


def experts(nc, m, d, ph, block, layer, table, h_dram, y_dram, routed, tabled, outputs_in):
    WE = KC * EH
    w0 = HT0
    assert w0 + 4 * WE <= ID0
    w2 = MOE_W
    wat = [[w0, w0 + WE, w0 + 2 * WE], [w0 + 3 * WE, w2, w2 + WE]]
    x0, xt0, hm0, ht0, y0, ix0 = MOE_X, MOE_XT, MOE_HM, MOE_HT, MOE_Y, MOE_IX
    HC = EH // P
    w_aps = (d["f_w_gate"].rearrange("l e (p c) n -> (l e) p (c n)", p=P),
             d["f_w_up"].rearrange("l e (p c) n -> (l e) p (c n)", p=P),
             d["f_w_down"].rearrange("l e (p c) n -> (l e) p (c n)", p=P))
    trips_ap = m.a(TRIPS, 1, 0, 1).bitcast(I32)
    w_in = [[ph.sem(f"w{t}_in{s}") for s in range(2)] for t in range(3)]
    gated, upped, downed = ph.sem("gated"), ph.sem("upped"), ph.sem("downed")
    ix_in, x_in = [ph.pool_dma(m), ph.pool_dma(m)], [ph.pool_dma(m), ph.pool_dma(m)]
    x_turned, xt_ok, silu, hm_ok = ph.sem("x_turned"), ph.sem("xt_ok"), ph.sem("silu"), ph.sem("hm_ok")
    h_turned, ht_ok, y_ok = ph.sem("h_turned"), ph.sem("ht_ok"), ph.sem("y_ok")
    y_out, passed = [ph.sem("y_out0"), ph.sem("y_out1")], ph.sem("passed")
    @block.sync
    def _(sp):
        sp.wait_ge(routed, 1)
        trips = sp.value_load(trips_ap, min_val=8, max_val=NBLK // 2)

        def load(i, s, first=False):
            e = sp.value_load(m.dyn(BE0 + 2 * i + s, 1, 0, 1).bitcast(I32), min_val=0, max_val=NE - 1)
            for t, used in enumerate((gated, upped, downed)):
                if not first:
                    sp.wait_ge(used, 2 * i + s + 1)
                sp.dma_start(m.a(wat[s][t], WE), w_aps[t][bass.ds(e + layer * NE, 1), :, :]
                             .rearrange("a p n -> (a p) n")).then_inc(w_in[t][s], 16)
                if first and s == 0 and t == 0:
                    sp.wait_ge(tabled, 1)
                if first and s == 0 and t == 1:
                    sp.wait_ge(x_in[0], 16)

        load(0, 0, first=True)
        load(0, 1, first=True)
        with sp.Fori(1, trips) as i:
            for s in range(2):
                load(i, s)

    @block.gpsimd
    def _(pool):
        pool.wait_ge(routed, 1)
        pool.wait_ge(tabled, 1)
        trips = pool.value_load(trips_ap, min_val=8, max_val=NBLK // 2)
        with pool.Fori(0, trips) as i:
            for s in range(2):
                pool.wait_ge(x_turned, 2 * i + s + 1)
                pool.dma_start(m.a(ix0 + s, 1).bitcast(I32),
                               table[bass.ds((2 * i + s) * P, P), :]).then_inc(ix_in[s], 16)
                pool.wait_ge(ix_in[s], 16 * i + 16)
                pool.sem_inc(passed, 1)
                pool.indirect_dma_start(
                    m.a(x0 + s * D, D), None, h_dram,
                    bass.IndirectOffsetOnAxis(ap=m.a(ix0 + s, 1).bitcast(U32), axis=0))\
                    .then_inc(x_in[s], 16)

    @block.tensor
    def _(pe):
        pe.wait_ge(routed, 1)
        trips = pe.value_load(trips_ap, min_val=8, max_val=NBLK // 2)
        for q in (gated, upped, downed, x_turned):
            pe.sem_inc(q, 2)

        def turn_x(n, s, i):
            pe.wait_ge(x_in[s], 16 * i + 16)
            pe.wait_ge(xt_ok, n + 1)
            for c in range(KC):
                x = nc.tensor.transpose(m.bank(0, P, at=c * P),
                                        m.A[:, x0 + s * D + c:x0 + (s + 1) * D:KC], m.ident())
            x.then_inc(x_turned, 1)

        def gate_up(n, s, i):
            pe.wait_ge(xt_ok, n + 2)
            for t, b, done in ((0, 2, gated), (1, 3, upped)):
                pe.wait_ge(w_in[t][s], 16 * i + 16)
                pe.wait_ge((silu, hm_ok)[t], n + 1)
                for c in range(KC):
                    x = nc.tensor.matmul(m.bank(b), m.a(xt0 + s * D + c * P, P),
                                         m.a(wat[s][t] + c * EH, EH),
                                         start=(c == 0), stop=(c == KC - 1))
                x.then_inc(done, 1)

        def turn_h(n, s):
            pe.wait_ge(hm_ok, n + 2)
            pe.wait_ge(ht_ok, n + 1)
            for c in range(HC):
                x = nc.tensor.transpose(m.bank(4, P, at=c * P),
                                        m.A[:, hm0 + s * EH + c:hm0 + (s + 1) * EH:HC], m.ident())
            x.then_inc(h_turned, 1)

        def down(n, s, i):
            pe.wait_ge(ht_ok, n + 2)
            pe.wait_ge(w_in[2][s], 16 * i + 16)
            pe.wait_ge(y_ok, n + 2)
            for h in range(2):
                for c in range(HC):
                    x = nc.tensor.matmul(m.bank(5 + h), m.a(ht0 + s * EH + c * P, P),
                                         m.a(wat[s][2] + c * D + h * BANK, BANK),
                                         start=(c == 0), stop=(c == HC - 1))
            x.then_inc(downed, 1)

        turn_x(0, 0, 0)
        gate_up(0, 0, 0)
        turn_x(1, 1, 0)
        turn_h(0, 0)
        with pe.Fori(0, trips - 1) as i:
            gate_up(2 * i + 1, 1, i)
            turn_x(2 * i + 2, 0, i + 1)
            down(2 * i, 0, i)
            turn_h(2 * i + 1, 1)
            gate_up(2 * i + 2, 0, i + 1)
            turn_x(2 * i + 3, 1, i + 1)
            down(2 * i + 1, 1, i)
            turn_h(2 * i + 2, 0)
        last = trips * 2 - 1
        gate_up(last, 1, trips - 1)
        down(last - 1, 0, trips - 1)
        turn_h(last, 1)
        down(last, 1, trips - 1)

    @block.scalar
    def _(act):
        act.wait_ge(routed, 1)
        trips = act.value_load(trips_ap, min_val=8, max_val=NBLK // 2)
        for q in (xt_ok, silu, ht_ok):
            act.sem_inc(q, 1)
        act.sem_inc(y_ok, 2)
        for s in range(2):
            act.sem_inc(y_out[s], 16)

        def copy_x(n, s):
            act.wait_ge(x_turned, n + 3)
            nc.scalar.activation(m.a(xt0 + s * D, D), m.bank(0, D), ACT.Copy).then_inc(xt_ok, 1)

        def gate(n, s):
            act.wait_ge(gated, n + 3)
            act.wait_ge(h_turned, n + 1)
            nc.scalar.activation(m.a(hm0 + s * EH, EH), m.bank(2), ACT.Silu).then_inc(silu, 1)

        def copy_h(n, s):
            act.wait_ge(h_turned, n + 2)
            nc.scalar.activation(m.a(ht0 + s * EH, EH), m.bank(4), ACT.Copy).then_inc(ht_ok, 1)

        def store_y(n, s, i):
            act.wait_ge(downed, n + 3)
            act.wait_ge(y_out[s], 16 * i + 16)
            nc.scalar.activation(m.a(y0 + s * D, D), m.bank(5, D), ACT.Copy).then_inc(y_ok, 1)
            act.wait_ge(y_ok, n + 3)
            act.dma_start(y_dram[bass.ds(n * P, P), :], m.a(y0 + s * D, D)).then_inc(y_out[s], 16)

        copy_x(0, 0)
        gate(0, 0)
        copy_x(1, 1)
        copy_h(0, 0)
        with act.Fori(0, trips - 1) as i:
            gate(2 * i + 1, 1)
            copy_x(2 * i + 2, 0)
            store_y(2 * i, 0, i)
            copy_h(2 * i + 1, 1)
            gate(2 * i + 2, 0)
            copy_x(2 * i + 3, 1)
            store_y(2 * i + 1, 1, i)
            copy_h(2 * i + 2, 0)
        last = trips * 2 - 1
        gate(last, 1)
        store_y(last - 1, 0, trips - 1)
        copy_h(last, 1)
        store_y(last, 1, trips - 1)
        for s in range(2):
            act.wait_ge(y_out[s], trips * 16 + 16)
            act.sem_inc(outputs_in, 1)

    @block.vector
    def _(dve):
        dve.wait_ge(routed, 1)
        trips = dve.value_load(trips_ap, min_val=8, max_val=NBLK // 2)
        dve.sem_inc(hm_ok, 1)
        dve.sem_inc(h_turned, 1)
        with dve.Fori(0, trips) as i:
            for s in range(2):
                n = 2 * i + s
                dve.wait_ge(silu, n + 2)
                dve.wait_ge(upped, n + 3)
                h = m.a(hm0 + s * EH, EH)
                nc.vector.tensor_tensor(h, h, m.bank(3), ALU.mult).then_inc(hm_ok, 1)


def combine(nc, m, ph, block, y_dram, gain, out, outputs_in):
    NS = 8
    y0, sq0, h0 = MOE_W, MOE_XT, MOE_Y
    var0, rs0 = ST0 + 8, ST0 + 16
    y_in = [ph.pool_dma(m) for s in range(NS)]
    added, squared, g_in, var_ok = ph.sem("added"), ph.sem("squared"), ph.sem("g_in"), ph.sem("var_ok")
    rooted, inverted, normed = ph.sem("rooted"), ph.sem("inverted"), ph.sem("normed")
    turned, copied, stored = ph.sem("turned"), ph.sem("copied"), ph.sem("stored")

    @block.gpsimd
    def _(pool):
        pool.wait_ge(outputs_in, 2)
        for n in range(2 * NB):
            b, k = n // 2, n % 2
            if n >= NS:
                pool.wait_ge(added, n - NS + 1)
            pool.indirect_dma_start(
                m.a(y0 + (n % NS) * D, D), None, y_dram,
                bass.IndirectOffsetOnAxis(ap=m.a(SLOT0 + 8 * k + b, 1).bitcast(U32), axis=0))\
                .then_inc(y_in[n % NS], 16)

    @block.vector
    def _(dve):
        def normalise(b):
            dve.wait_ge(squared, b + 1)
            nc.vector.tensor_scalar(m.a(var0 + b, 1), m.a(ST0 + b, 1), 1.0 / D, EPS,
                                    ALU.mult, ALU.add).then_inc(var_ok, 1)
            dve.wait_ge(rooted, b + 1)
            nc.vector.reciprocal(m.a(rs0 + b, 1), m.a(var0 + b, 1)).then_inc(inverted, 1)
            dve.wait_ge(inverted, b + 1)
            if b == 0:
                dve.wait_ge(g_in, 16)
            to = X0 + b * D if out is not None else h0 + (b % 2) * D
            if out is None and b >= 2:
                dve.wait_ge(turned, b - 1)
            nc.vector.scalar_tensor_tensor(out=m.a(to, D), in0=m.a(X0 + b * D, D), scalar=m.a(rs0 + b, 1),
                                           in1=m.a(GB0, D), op0=ALU.mult, op1=ALU.mult).then_inc(normed, 1)

        for n in range(2 * NB):
            b, k = n // 2, n % 2
            dve.wait_ge(y_in[n % NS], 16 * (n // NS + 1))
            if k:
                dve.wait_ge(added, n)
            x = m.a(X0 + b * D, D)
            nc.vector.scalar_tensor_tensor(out=x, in0=m.a(y0 + (n % NS) * D, D),
                                           scalar=m.a(WT0 + 8 * k + b, 1), in1=x,
                                           op0=ALU.mult, op1=ALU.add).then_inc(added, 1)
            if k and b >= 1:
                normalise(b - 1)
        normalise(NB - 1)

    @block.scalar
    def _(act):
        def copy(b):
            act.wait_ge(turned, b + 1)
            to = m.A[:, HT0 + b * P:HT0 + b * P + (KC - 1) * S + P]
            to = bass.AP(tensor=to.tensor, offset=to.offset, ap=[to.ap[0], [S, KC], [1, P]])
            nc.scalar.activation(to, m.bank(2 * (b % 2), D).rearrange("p (c t) -> p c t", c=KC),
                                 ACT.Copy).then_inc(copied, 1)

        for b in range(NB):
            act.wait_ge(added, 2 * b + 2)
            if b >= 2:
                act.wait_ge(squared, b - 1)
            nc.scalar.activation(m.a(sq0 + (b % 2) * D, D), m.a(X0 + b * D, D), ACT.Square,
                                 accum_out=m.a(ST0 + b, 1)).then_inc(squared, 1)
            act.wait_ge(var_ok, b + 1)
            nc.scalar.activation(m.a(var0 + b, 1), m.a(var0 + b, 1), ACT.Sqrt).then_inc(rooted, 1)
            if out is None and b >= 2:
                copy(b - 2)
        if out is None:
            copy(NB - 2)
            copy(NB - 1)

    if out is None:
        @block.tensor
        def _(pe):
            for b in range(NB):
                pe.wait_ge(normed, b + 1)
                if b >= 2:
                    pe.wait_ge(copied, b - 1)
                for c in range(KC):
                    x = nc.tensor.transpose(m.bank(2 * (b % 2), P, at=c * P),
                                            m.a(h0 + (b % 2) * D + c * P, P), m.ident())
                x.then_inc(turned, 1)

    @block.sync
    def _(sp):
        sp.dma_start(m.a(GB0, D), row(gain)).then_inc(g_in, 16)
        if out is not None:
            for b in range(NB):
                sp.wait_ge(normed, b + 1)
                sp.dma_start(out[0, b * P:(b + 1) * P, :], m.a(X0 + b * D, D)).then_inc(stored, 16)
            sp.wait_ge(stored, 16 * NB)


def mixture(nc, m, d, layer, table, h_dram, y_dram, gain, out=None):
    with Phase(nc, f"moe{layer}") as ph:
        routed, tabled, outputs_in = ph.sem("routed"), ph.sem("tabled"), ph.sem("outputs_in")
        with ph.block() as block:
            route(nc, m, d, ph, block, layer, table, routed, tabled)
            experts(nc, m, d, ph, block, layer, table, h_dram, y_dram, routed, tabled, outputs_in)
            combine(nc, m, ph, block, y_dram, gain, out, outputs_in)


def load_memory(nc, m, d):
    with Phase(nc, "memory") as ph:
        loaded = ph.sem("loaded")
        with ph.block() as block:
            @block.sync
            def _(sp):
                sp.dma_start(m.ident(), d["c_ident"]).then_inc(loaded, 16)
                sp.dma_start(m.a(X0, 2 * D).rearrange("p (b n) -> p b n", b=2),
                             d["mem"][0].rearrange("(b p) n -> p b n", p=P)).then_inc(loaded, 16)
                sp.wait_ge(loaded, 32)


def program(nc, d, out, stop=None):
    def scratch(name, shape, dt=F32):
        return nc.dram_tensor(name, shape, dt, kind="Internal").ap()

    spectra = scratch("spectra", (2 * QT_N, P, FQ))
    h_dram = scratch("h_tokens", (S, D))
    y_dram = scratch("y_slots", (NSLOT, D))
    table = scratch("slot_table", (NSLOT, 1), I32)

    def rows(w):
        return lambda c: [(0, P, w[c * P:(c + 1) * P, :])]

    w_o = d["o_w_out"][0].rearrange("(i s j e) n -> i j s e n", i=2, s=2, j=4)
    steps = [
        lambda: load_memory(nc, m, d),
        lambda: norm_transpose(nc, m, "memnorm", d["g_mem"], X0, ME0, 2),
        lambda: load_start(nc, m, d),
        lambda: filter_taps(nc, m, d),
        lambda: filter_spectrum(nc, m, d, 0, spectra),
        lambda: filter_spectrum(nc, m, d, 1, spectra),
        lambda: norm_transpose(nc, m, "enorm", d["e_norm"][0], X0, HT0, NB),
        lambda: diff_attention(nc, m, d, y_dram),
        lambda: hyena_project(nc, m, d),
        lambda: long_conv(nc, m, d, 0, spectra),
        lambda: long_conv(nc, m, d, 1, spectra),
        lambda: project_add(nc, m, "eout", rows(d["e_w_out"][0]), 8, reload=d["x"][0],
                            gain=d["c_norm"][0]),
    ]
    for layer in range(2):
        if layer == 1:
            steps += [
                lambda: window_attention(nc, m, d),
                lambda: project_add(nc, m, "oout", lambda c: [
                    (64 * s, 64 * s + 64, w_o[c // 4, c % 4, s]) for s in range(2)], 8,
                    gain=d["c_norm"][1]),
            ]
        steps += [
            lambda L=layer: cross_attention(nc, m, d, L),
            lambda L=layer: project_add(nc, m, f"cout{L}", rows(d["c_wo"][L]), 4,
                                        gain=d["f_norm"][L], h_dram=h_dram,
                                        router=((d["f_w_grp"][L], 0, NG), (d["f_w_exp"][L], NG, NR))),
            lambda L=layer: mixture(nc, m, d, L, table, h_dram, y_dram,
                                    *((d["o_norm"][0],) if L == 0 else (d["g_final"], out))),
        ]
    with ExitStack() as stack:
        m = Core(nc, stack)
        for step in steps[:stop]:
            step()


def constants():
    f8 = np.float64
    c = {"c_ident": np.eye(P)}
    pos = np.arange(S, dtype=np.float32)
    t = np.linspace(0.0, 1.0, S, dtype=np.float32)
    bands = np.linspace(1e-4, 15, 16, dtype=np.float32)
    ang = bands[None] * (2.0 * np.pi * pos[:, None] / S).astype(np.float32)
    c["c_pos"] = np.concatenate([t[:, None], np.cos(ang), -np.sin(ang)], axis=1).T
    deltas = np.linspace(np.log(1e-2) / 1.5, np.log(1e-2) / 0.3, HW, dtype=np.float32)
    decay = np.exp(-t[:, None] * np.abs(deltas)[None])
    c["c_decay"] = decay.reshape(4, P, 2, HW).transpose(1, 2, 0, 3).reshape(P, 8 * HW)
    c["c_sign"] = np.where(np.arange(P) < 64, 1.0, -1.0)[:, None]
    times = np.arange(S).reshape(4, P, 2)
    freq = (np.arange(S // 2) + 0.5).reshape(4, P)
    ang = np.pi * times[None, None].astype(f8) * freq[:, :, None, None, None] / S
    both = np.stack([np.cos(ang), np.sin(ang)])
    c["c_dft"] = both.transpose(1, 4, 0, 5, 3, 2).reshape(4, P, -1)
    c["c_idft"] = both.transpose(1, 2, 0, 5, 3, 4).reshape(4, P, -1) / S
    p = np.arange(P)[:, None]
    c["c_dist"] = -8.0 * np.abs(p - (np.arange(2 * S - P)[None] - (S - P)))
    rel = np.abs(p + P - np.arange(3 * P)[None])
    heads = np.array([[s * 4 + j for s in range(2)] for j in range(4)]).reshape(8, 1, 1)
    slopes = 2.0 ** (-8.0 * (heads + 1) / 16)
    c["c_window"] = np.where(rel[None] <= P, -8.0 * slopes * rel[None], -1e30).transpose(1, 0, 2).reshape(P, -1)
    c["c_iota"] = np.broadcast_to(np.arange(NBLK), (P, NBLK))
    c["c_tri"] = np.triu(np.ones((P, P)), 1)
    out = {k: np.ascontiguousarray(v, dtype=np.float32) for k, v in c.items()}
    out["c_tok"] = np.ascontiguousarray((np.arange(NB)[None] * P + p).astype(np.int32))
    return out


_INS = ['x', 'mem', 'e_norm', 'e_w_in', 'e_conv_w', 'e_conv_b', 'e_filt_w1', 'e_filt_b1', 'e_filt_w2',
        'e_filt_b2', 'e_filt_w3', 'e_filt_freq', 'e_hy_bias', 'e_lam', 'e_subln', 'e_w_out', 'o_norm',
        'o_w_in', 'o_sink', 'o_w_out', 'c_norm', 'c_wq', 'c_wkv', 'c_wo', 'f_norm', 'f_w_grp', 'f_b_grp',
        'f_w_exp', 'f_b_exp', 'f_w_gate', 'f_w_up', 'f_w_down', 'g_mem', 'g_final']
STOP = None


def kernel(**inputs):
    import concourse.bacc as _bacc
    from concourse.bass_utils import run_bass_kernel_spmd as _run

    nc = _bacc.Bacc("TRN2", target_bir_lowering=False, num_devices=1)
    arrays = {f"in_{n}": np.ascontiguousarray(inputs[n]) for n in _INS}
    arrays.update({f"in_{n}": v for n, v in constants().items()})
    d = {n[3:]: nc.dram_tensor(n, v.shape, mybir.dt.from_np(v.dtype), kind="ExternalInput").ap()
         for n, v in arrays.items()}
    out = nc.dram_tensor("out_0", (1, S, D), F32, kind="ExternalOutput").ap()
    program(nc, d, out, STOP)
    r = _run(nc, [arrays], core_ids=[0])
    return r.results[0]["out_0"]
```

```python
from contextlib import ExitStack

import numpy as np
import concourse.bass as bass
from concourse import mybir
from concourse.alu_op_type import AluOpType as ALU

ACT = mybir.ActivationFunctionType
F32 = mybir.dt.float32
I32 = mybir.dt.int32
U32 = mybir.dt.uint32
AX_X = mybir.AxisListType.X

P = 128
S = 1024
D = 1024
NB = S // P
KC = D // P
BANK = 512
EPS = 1e-6
HW = 512
QT_N = 4
M_LEN = 256
XH = 4
NE = 32
NG = 4
EG = NE // NG
NR = NG + NE
ROUTE_BANK = 5
EH = 512
NBLK = 2 * S // P + NE
NSLOT = NBLK * P

X0 = 0
HT0 = X0 + NB * D
MT0 = HT0 + KC * S
ID0 = MT0 + KC * S
ST0 = ID0 + P
GB0 = ST0 + 256
ME0 = GB0 + D
W0 = ME0 + KC * M_LEN
TOTAL = 53200


RBIAS = ST0 + 160

EO_W = [W0 + (12 + c) * D for c in range(8)]
EO_BUF = W0 + 20 * D
OO_W = [W0 + (18 + c) * D for c in range(6)] + [W0 + (12 + c) * D for c in range(2)]
OO_BUF = W0 + 14 * D
CO_W = [W0 + 15 * D + 256 + c * D for c in range(4)]
CO_BUF = CO_W[3] + D
assert OO_W[5] + D <= TOTAL and EO_BUF + 4 * D <= TOTAL and CO_BUF + 4 * D + KC * NR + S <= TOTAL


class Steps:

    def __init__(self, sem):
        self.sem, self.k, self.i, self.per = sem, 0, None, 0

    def enter(self, i, per):
        self.i, self.per, self.k0 = i, per, self.k

    def leave(self, trips):
        assert self.k - self.k0 == self.per, (self.k - self.k0, self.per)
        self.k, self.i = self.k0 + trips * self.per, None

    def tick(self):
        self.k += 1
        return 1

    @property
    def n(self):
        return self.k if self.i is None else self.i * self.per + self.k


class Core:

    def __init__(self, nc, stack):
        self.nc = nc
        self.A = stack.enter_context(nc.sbuf_tensor("sbuf", [P, TOTAL], F32))
        self.PS = stack.enter_context(nc.psum_tensor("psum", [P, 8 * BANK], F32))
        self.ahead = {n: [stack.enter_context(nc.semaphore(f"ahead_{n}{k}")) for k in range(c)]
                      for n, c in (("spectra", 1), ("diff", 3), ("hyproj", 2), ("eout", 6), ("cross0", 6), ("cout0", 4),
                                   ("gqa", 6), ("oout", 6), ("cross1", 6), ("cout1", 4))}
        self.pool_dma = iter([stack.enter_context(nc.semaphore(f"pool_dma{n}")) for n in range(35)])

    def a(self, at, n, p0=0, p1=P):
        return self.A[p0:p1, at:at + n]

    def dyn(self, at, n, p0=0, p1=P):
        return self.A[p0:p1, bass.ds(at, n)]

    def bank(self, b, n=BANK, p0=0, p1=P, at=0):
        return self.PS[p0:p1, b * BANK + at:b * BANK + at + n]

    def ident(self, n=P):
        return self.A[0:n, ID0:ID0 + n]


class Phase:

    def __init__(self, nc, name):
        self.nc, self.name = nc, name

    def __enter__(self):
        self.stack, self.sems = ExitStack(), []
        return self

    def sem(self, name):
        s = self.stack.enter_context(self.nc.semaphore(f"{self.name}_{name}"))
        self.sems.append(s)
        return s

    def pool_dma(self, m):
        return next(m.pool_dma)

    def block(self):
        return self.nc.Block()

    def __exit__(self, *exc):
        if exc[0] is None:
            for s in self.sems:
                self.nc.sync.sem_clear(s)
            self.nc.all_engine_barrier()
        self.stack.close()


def row(ap):
    n = ap.shape[0]
    return ap.rearrange("(a n) -> a n", a=1).to_broadcast([P, n])


def load_chunks(m, eng, name, w, at):
    for c, sem in enumerate(m.ahead[name]):
        for p0, p1, rows in w(c):
            eng.dma_start(m.a(at[c], D, p0, p1), rows).then_inc(sem, 16)


def project_add(nc, m, name, w, ww, buf, gain, ahead=None, reload=None, h_dram=None, router=None):
    nfc = len(ww)
    sq0 = buf
    h0 = sq0 + 2 * D
    wr0 = h0 + 2 * D
    lt0 = wr0 + KC * NR
    GROUPS = ((0, 4), (4, 6), (6, 8))
    var0, rs0 = ST0 + 8, ST0 + 16
    with Phase(nc, name) as ph:
        w_in = [*m.ahead[name], *(ph.sem(f"w_in{c}") for c in range(len(m.ahead[name]), nfc))]
        x_in, summed, added, squared = ph.sem("x_in"), ph.sem("summed"), ph.sem("added"), ph.sem("squared")
        g_in, var_ok, rooted, dve_s = ph.sem("g_in"), ph.sem("var_ok"), ph.sem("rooted"), ph.sem("dve")
        h_ready, turned, copied, stored = ph.sem("h_ready"), ph.sem("turned"), ph.sem("copied"), ph.sem("stored")
        wr_in, lg_ok, lt_ok = ph.sem("wr_in"), ph.sem("lg_ok"), ph.sem("lt_ok")
        with ph.block() as block:
            @block.sync
            def _(sp):
                for c in range(len(m.ahead[name]), nfc):
                    for p0, p1, rows in w(c):
                        sp.dma_start(m.a(ww[c], D, p0, p1), rows).then_inc(w_in[c], 16)
                if reload is not None:
                    sp.dma_start(m.a(X0, NB * D).rearrange("p (b n) -> p b n", b=NB),
                                 reload.rearrange("(b p) n -> p b n", p=P)).then_inc(x_in, 16)
                sp.dma_start(m.a(GB0, D), row(gain)).then_inc(g_in, 16)
                if router is not None:
                    wr = m.a(wr0, KC * NR).rearrange("p (c n) -> p c n", c=KC)
                    for w_r, b_r, n0, n1 in router:
                        sp.dma_start(wr[:, :, n0:n1],
                                     w_r.rearrange("(c p) n -> p c n", p=P)).then_inc(wr_in, 16)
                        sp.dma_start(m.a(RBIAS + n0, n1 - n0), row(b_r)).then_inc(wr_in, 16)
                if ahead is not None:
                    ahead(sp)
                if h_dram is not None:
                    for b in range(NB):
                        sp.wait_ge(h_ready, b + 1)
                        sp.dma_start(h_dram[b * P:(b + 1) * P, :],
                                     m.a(h0 + (b % 2) * D, D)).then_inc(stored, 16)
                        sp.wait_ge(stored, 16 * (b + 1))

            @block.tensor
            def _(pe):
                def product(c, blk):
                    for h in range(2):
                        t = nc.tensor.matmul(m.bank(2 * (blk % 4) + h), m.a(MT0 + c * S + blk * P, P),
                                             m.a(ww[c] + h * BANK, BANK),
                                             start=(c == 0), stop=(c == nfc - 1))
                    if c == nfc - 1:
                        t.then_inc(summed, 1)

                def turn(blk):
                    pe.wait_ge(h_ready, blk + 1)
                    pe.wait_ge(added, 5 + blk % 2)
                    if blk >= 2:
                        pe.wait_ge(copied, blk - 1)
                    for c in range(KC):
                        t = nc.tensor.transpose(m.bank(2 * (blk % 2), P, at=c * P),
                                                m.a(h0 + (blk % 2) * D + c * P, P), m.ident())
                    t.then_inc(turned, 1)

                def logits(g):
                    u, z = GROUPS[g]
                    if g == 0:
                        pe.wait_ge(wr_in, 32 * len(router))
                        pe.wait_ge(added, NB)
                    if g >= 2:
                        pe.wait_ge(lt_ok, g - 1)
                    pe.wait_ge(copied, z)
                    for c in range(KC):
                        t = nc.tensor.matmul(m.bank(4 + 2 * (g % 2), (z - u) * P, p1=NR),
                                             m.a(wr0 + c * NR, NR), m.a(HT0 + c * S + u * P, (z - u) * P),
                                             start=(c == 0), stop=(c == KC - 1))
                    t.then_inc(lg_ok, 1)

                def turn_logits(g):
                    pe.wait_ge(lt_ok, g + 1)
                    for u in range(*GROUPS[g]):
                        nc.tensor.transpose(m.bank(ROUTE_BANK, NR, at=u * NR), m.a(lt0 + u * P, P, p1=NR),
                                            m.ident(NR))

                for c in range(nfc):
                    pe.wait_ge(w_in[c], 16 * len(w(c)))
                    for blk in range(4):
                        product(c, blk)
                for blk in range(4, NB):
                    pe.wait_ge(added, blk - 3)
                    for c in range(nfc):
                        product(c, blk)
                    if blk >= 6:
                        turn(blk - 6)
                for blk in range(2, NB):
                    turn(blk)
                    if router is not None and blk in (4, 6):
                        logits(blk // 2 - 2)
                    if router is not None and blk in (5, 7):
                        turn_logits(blk // 2 - 2)
                if router is not None:
                    logits(2)
                    turn_logits(2)

            @block.vector
            def _(dve):
                if reload is not None:
                    dve.wait_ge(x_in, 16)
                st = Steps(dve_s)

                def roots(g):
                    dve.wait_ge(squared, 4 * g + 4)
                    nc.vector.tensor_scalar(m.a(var0 + 4 * g, 4), m.a(ST0 + 4 * g, 4), 1.0 / D, EPS,
                                            ALU.mult, ALU.add).then_inc(var_ok, 1)
                    dve.wait_ge(rooted, g + 1)
                    nc.vector.reciprocal(m.a(rs0 + 4 * g, 4), m.a(var0 + 4 * g, 4)).then_inc(dve_s, st.tick())
                    dve.wait_ge(dve_s, st.n)

                def normalise(blk):
                    if blk == 0:
                        dve.wait_ge(g_in, 16)
                    if blk >= 2:
                        dve.wait_ge(turned, blk - 1)
                        if h_dram is not None:
                            dve.wait_ge(stored, 16 * (blk - 1))
                    nc.vector.scalar_tensor_tensor(
                        out=m.a(h0 + (blk % 2) * D, D), in0=m.a(X0 + blk * D, D), scalar=m.a(rs0 + blk, 1),
                        in1=m.a(GB0, D), op0=ALU.mult, op1=ALU.mult).then_inc(h_ready, 1)

                for blk in range(NB):
                    dve.wait_ge(summed, blk + 1)
                    x = m.a(X0 + blk * D, D)
                    nc.vector.tensor_tensor(x, m.bank(2 * (blk % 4), D), x, ALU.add).then_inc(added, 1)
                    if blk in (4, 5):
                        if blk == 4:
                            roots(0)
                        normalise(blk - 4)
                normalise(2)
                roots(1)
                for blk in range(3, NB):
                    normalise(blk)

            @block.scalar
            def _(act):
                def copy_logits(g):
                    u, z = GROUPS[g]
                    act.wait_ge(lg_ok, g + 1)
                    nc.scalar.activation(m.a(lt0 + u * P, (z - u) * P, p1=NR),
                                         m.bank(4 + 2 * (g % 2), (z - u) * P, p1=NR), ACT.Copy).then_inc(lt_ok, 1)

                def root(g):
                    act.wait_ge(var_ok, g + 1)
                    v = m.a(var0 + 4 * g, 4)
                    nc.scalar.activation(v, v, ACT.Sqrt).then_inc(rooted, 1)

                def copy(blk):
                    act.wait_ge(turned, blk + 1)
                    out = m.A[:, HT0 + blk * P:HT0 + blk * P + (KC - 1) * S + P]
                    out = bass.AP(tensor=out.tensor, offset=out.offset, ap=[out.ap[0], [S, KC], [1, P]])
                    nc.scalar.activation(out, m.bank(2 * (blk % 2), D).rearrange("p (c t) -> p c t", c=KC),
                                         ACT.Copy).then_inc(copied, 1)

                for blk in range(NB):
                    act.wait_ge(added, blk + 1)
                    if blk >= 2:
                        act.wait_ge(squared, blk - 1)
                    nc.scalar.activation(m.a(sq0 + (blk % 2) * D, D), m.a(X0 + blk * D, D), ACT.Square,
                                         accum_out=m.a(ST0 + blk, 1)).then_inc(squared, 1)
                    if blk == 4:
                        root(0)
                copy(0)
                copy(1)
                root(1)
                for blk in range(2, NB):
                    copy(blk)
                    if router is not None and blk in (4, 6):
                        copy_logits(blk // 2 - 2)
                if router is not None:
                    copy_logits(2)


FQ = 2 * 2 * 4 * P


SPF0 = W0 + 22 * S


def begin(nc, m, d):
    z0 = W0
    a10, a20 = z0 + S, z0 + 2 * S
    u0, r0 = z0 + 3 * S, z0 + 4 * S
    w10 = z0 + 5 * S
    w20 = w10 + 64
    v0 = w20 + P
    w30 = v0 + 8
    dec0 = w30 + 4 * HW
    mem0 = dec0 + 8 * HW
    h0 = mem0 + 2 * D
    sq0 = h0 + 2 * D
    assert sq0 + 2 * D <= SPF0
    with Phase(nc, "begin") as ph:
        mem_in, x_in, squared, var_ok = ph.sem("mem_in"), ph.sem("x_in"), ph.sem("squared"), ph.sem("var_ok")
        rooted, normed, turned, copied = ph.sem("rooted"), ph.sem("normed"), ph.sem("turned"), ph.sem("copied")
        first_in, loaded = ph.sem("first_in"), ph.sem("loaded")
        dec_in, sign_ok = ph.sem("dec_in"), ph.sem("sign_ok")
        layer, arg, sined = ph.sem("layer"), ph.sem("arg"), ph.sem("sined")
        dve_s, h_sum, h_ok = ph.sem("dve"), ph.sem("h_sum"), ph.sem("h_ok")
        w3 = d["e_filt_w3"][0].rearrange("k (o q c) -> k o q c", o=2, q=2)
        with ph.block() as block:
            @block.sync
            def _(sp):
                def column(name, n, q, sem):
                    sp.dma_start(m.a(v0 + n, 1, 64 * q, 64 * q + 64),
                                 d[name][0].rearrange("(k o) -> k o", o=1)).then_inc(sem, 16)

                sp.dma_start(m.a(z0, S, 0, 33), d["c_pos"]).then_inc(first_in, 16)
                sp.dma_start(m.a(w10, 64, 0, 33), d["e_filt_w1"][0]).then_inc(first_in, 16)
                column("e_filt_b1", 0, 0, first_in)
                column("e_filt_freq", 1, 0, first_in)
                column("e_filt_freq", 1, 1, loaded)
                for q in range(2):
                    column("e_filt_b2", 2, q, loaded)
                    sp.dma_start(m.a(w20 + 64 * q, 64, 0, 64), d["e_filt_w2"][0]).then_inc(loaded, 16)
                sp.dma_start(m.a(v0 + 4, 1), d["c_sign"]).then_inc(loaded, 16)
                for q in range(2):
                    sp.dma_start(m.a(w30, 2 * HW, 64 * q, 64 * q + 64).rearrange("k (o c) -> k o c", o=2),
                                 w3[:, :, q, :]).then_inc(loaded, 16)
                sp.dma_start(m.a(dec0, 8 * HW), d["c_decay"]).then_inc(dec_in, 16)
                sp.dma_start(m.a(SPF0, FQ), d["c_dft"][0]).then_inc(m.ahead["spectra"][0], 16)
                sp.dma_start(m.a(X0, NB * D).rearrange("p (b n) -> p b n", b=NB),
                             d["x"][0].rearrange("(b p) n -> p b n", p=P)).then_inc(x_in, 16)
                sp.wait_ge(x_in, 16)

            @block.tensor
            def _(pe):
                pe.wait_ge(first_in, 64)
                for h in range(2):
                    t = nc.tensor.matmul(m.bank(h, p1=64), m.a(w10, 64, 0, 33),
                                         m.a(z0 + h * BANK, BANK, 0, 33), start=True, stop=True)
                t.then_inc(layer, 1)
                pe.wait_ge(sined, 1)
                pe.wait_ge(loaded, 128)
                for h in range(2):
                    t = nc.tensor.matmul(m.bank(2 + h), m.a(w20, P, 0, 64),
                                         m.a(a10 + h * BANK, BANK, 0, 64), start=True, stop=True)
                t.then_inc(layer, 1)
                for b in range(2):
                    pe.wait_ge(normed, b + 1)
                    for c in range(KC):
                        t = nc.tensor.transpose(m.bank(4 * b, P, at=c * P), m.a(h0 + b * D + c * P, P),
                                                m.ident())
                    t.then_inc(turned, 1)
                pe.wait_ge(copied, 2)
                pe.wait_ge(sign_ok, 2)
                for o in range(2):
                    for j in range(8):
                        for q in range(2):
                            n = 2 * (8 * o + j) + q
                            if n >= 4:
                                pe.wait_ge(h_ok, n - 3)
                            at = a20 + 2 * P * (j % 4) + j // 4
                            nc.tensor.matmul(m.bank(4 + n % 4), m.A[:, at:at + 2 * P - 1:2],
                                             m.a(w30 + (2 * q + o) * HW, HW),
                                             start=True, stop=True).then_inc(h_sum, 1)

            @block.scalar
            def _(act):
                act.dma_start(m.a(mem0, 2 * D).rearrange("p (b n) -> p b n", b=2),
                              d["mem"][0].rearrange("(b p) n -> p b n", p=P)).then_inc(mem_in, 16)
                act.dma_start(m.ident(), d["c_ident"]).then_inc(mem_in, 16)
                act.dma_start(m.a(GB0, D), row(d["g_mem"])).then_inc(mem_in, 16)
                act.wait_ge(mem_in, 48)
                for b in range(2):
                    nc.scalar.activation(m.a(sq0 + b * D, D), m.a(mem0 + b * D, D), ACT.Square,
                                         accum_out=m.a(ST0 + b, 1)).then_inc(squared, 1)
                for n, (to, p1) in enumerate(((a10, 64), (a20, P))):
                    act.wait_ge(arg, n + 1)
                    nc.scalar.activation(m.a(to, S, p1=p1), m.a(r0, S, p1=p1), ACT.Sin).then_inc(sined, 1)
                    if n == 0:
                        act.wait_ge(var_ok, 1)
                        nc.scalar.activation(m.a(ST0 + 8, 2), m.a(ST0 + 8, 2), ACT.Sqrt).then_inc(rooted, 1)
                        for b in range(2):
                            act.wait_ge(turned, b + 1)
                            to = m.a(ME0 + b * P, (KC - 1) * M_LEN + P)
                            to = bass.AP(tensor=to.tensor, offset=to.offset, ap=[to.ap[0], [M_LEN, KC], [1, P]])
                            nc.scalar.activation(to, m.bank(4 * b, D).rearrange("p (c t) -> p c t", c=KC),
                                                 ACT.Copy).then_inc(copied, 1)

            @block.vector
            def _(dve):
                st = Steps(dve_s)
                turn, big, hi = 2.0 * np.pi, 1.5 * 2.0 ** 23, 6.28125
                dve.wait_ge(first_in, 64)
                for n in range(2):
                    p1 = 64 * (n + 1)
                    u, r = m.a(u0, S, p1=p1), m.a(r0, S, p1=p1)
                    dve.wait_ge(layer, n + 1)
                    nc.vector.tensor_scalar(u, m.bank(2 * n, S, p1=p1), m.a(v0 + 2 * n, 1, p1=p1),
                                            m.a(v0 + 1, 1, p1=p1), ALU.add, ALU.mult)\
                        .then_inc(dve_s, st.tick())
                    dve.wait_ge(dve_s, st.n)
                    nc.vector.tensor_scalar(r, u, float(1.0 / turn), big, ALU.mult, ALU.add)\
                        .then_inc(dve_s, st.tick())
                    dve.wait_ge(dve_s, st.n)
                    nc.vector.tensor_scalar(r, r, big, None, ALU.subtract).then_inc(dve_s, st.tick())
                    dve.wait_ge(dve_s, st.n)
                    nc.vector.scalar_tensor_tensor(out=u, in0=r, scalar=-hi, in1=u, op0=ALU.mult,
                                                   op1=ALU.add).then_inc(dve_s, st.tick())
                    dve.wait_ge(dve_s, st.n)
                    nc.vector.scalar_tensor_tensor(out=u, in0=r, scalar=float(hi - turn), in1=u,
                                                   op0=ALU.mult, op1=ALU.add).then_inc(dve_s, st.tick())
                    dve.wait_ge(dve_s, st.n)
                    nc.vector.tensor_scalar(r, u, 3.1415925, -3.1415925, ALU.min, ALU.max).then_inc(arg, 1)
                    if n == 0:
                        dve.wait_ge(loaded, 128)
                        nc.vector.tensor_scalar(m.a(w30 + 2 * HW, 2 * HW), m.a(w30, 2 * HW), m.a(v0 + 4, 1), None,
                                                ALU.mult).then_inc(sign_ok, 1)
                        dve.wait_ge(squared, 2)
                        rstd = m.a(ST0 + 8, 2)
                        nc.vector.tensor_scalar(rstd, m.a(ST0, 2), 1.0 / D, EPS, ALU.mult,
                                                ALU.add).then_inc(var_ok, 1)
                        dve.wait_ge(rooted, 1)
                        nc.vector.reciprocal(rstd, rstd).then_inc(dve_s, st.tick())
                        dve.wait_ge(dve_s, st.n)
                        dve.wait_ge(mem_in, 48)
                        for b in range(2):
                            nc.vector.scalar_tensor_tensor(
                                out=m.a(h0 + b * D, D), in0=m.a(mem0 + b * D, D), scalar=m.a(ST0 + 8 + b, 1),
                                in1=m.a(GB0, D), op0=ALU.mult, op1=ALU.mult).then_inc(normed, 1)
                dve.wait_ge(sined, 2)
                nc.vector.memset(m.a(a20, 1, 64, P), 0.0).then_inc(sign_ok, 1)
                dve.wait_ge(dec_in, 16)
                for o in range(2):
                    for j in range(8):
                        for q in range(2):
                            n = 2 * (8 * o + j) + q
                            dve.wait_ge(h_sum, n + 1)
                            nc.vector.tensor_tensor(m.a((HT0, MT0)[o] + (8 * q + j) * HW, HW),
                                                    m.bank(4 + n % 4), m.a(dec0 + j * HW, HW),
                                                    ALU.mult).then_inc(h_ok, 1)


def filter_spectra(nc, m, d, k_dram):
    f0 = W0 + 3 * KC * P
    f_at = [SPF0, f0, f0 + FQ, f0 + 2 * FQ]
    ko0 = f0 + 3 * FQ
    c0 = ko0 + 2 * FQ
    h0 = c0 + 4 * HW
    sq0 = h0 + 2 * D
    assert sq0 + 2 * D <= SPF0 and SPF0 + FQ <= TOTAL
    rstd = m.a(ST0 + 8, NB)
    with Phase(nc, "spectra") as ph:
        f_in = [*m.ahead["spectra"], *(ph.sem(f"f_in{q}") for q in range(1, QT_N))]
        dft, odd, k_ok, g_in = ph.sem("dft"), ph.sem("odd"), ph.sem("k_ok"), ph.sem("g_in")
        k_out = [ph.sem("k_out0"), ph.sem("k_out1")]
        squared, var_ok, rooted, inverted = ph.sem("squared"), ph.sem("var_ok"), ph.sem("rooted"), ph.sem("inverted")
        normed, turned, copied = ph.sem("normed"), ph.sem("turned"), ph.sem("copied")
        with ph.block() as block:
            @block.sync
            def _(sp):
                for q in range(1, QT_N):
                    sp.dma_start(m.a(f_at[q], FQ), d["c_dft"][q]).then_inc(f_in[q], 16)
                sp.dma_start(m.a(GB0, D), row(d["e_norm"][0])).then_inc(g_in, 16)
                for t in range(3):
                    load_diff_weights(m, sp, d, t, 0)

            @block.tensor
            def _(pe):
                def sums(o, q, s, n, cs):
                    for par in range(2):
                        for j in range(4):
                            t = nc.tensor.matmul(
                                m.bank(4 * s + 2 * cs + par),
                                m.a(f_at[q] + ((2 * cs + par) * 4 + j) * P, P),
                                m.a(HT0 + (16 * o + 8 * cs + 4 * par + j) * HW, HW),
                                start=(j == 0), stop=(j == 3))
                    return t

                for o in range(2):
                    for q in range(QT_N):
                        s, n = q % 2, 4 * o + q
                        if o == 0:
                            pe.wait_ge(f_in[q], 16)
                        if n >= 2:
                            pe.wait_ge(k_ok, n - 1)
                        if o == 1 and q >= 1:
                            pe.wait_ge(copied, 2 * q)
                        sums(o, q, s, n, 0)
                        if o == 1:
                            pe.wait_ge(k_ok, n)
                            for r in range(2):
                                pe.wait_ge(normed, 2 * q + r + 1)
                                for c in range(KC):
                                    t = nc.tensor.transpose(m.bank(4 * (1 - s) + 2 * r, P, at=c * P),
                                                            m.a(h0 + r * D + c * P, P), m.ident())
                                t.then_inc(turned, 1)
                        sums(o, q, s, n, 1).then_inc(dft, 1)

            @block.scalar
            def _(act):
                for b in range(NB):
                    if b >= 2:
                        act.wait_ge(squared, b - 1)
                    nc.scalar.activation(m.a(sq0 + (b % 2) * D, D), m.a(X0 + b * D, D), ACT.Square,
                                         accum_out=m.a(ST0 + b, 1)).then_inc(squared, 1)
                act.wait_ge(var_ok, 1)
                nc.scalar.activation(rstd, rstd, ACT.Sqrt).then_inc(rooted, 1)
                for n in range(2 * QT_N):
                    s = n % 2
                    for b in range(2 * (n - QT_N), 2 * (n - QT_N) + 2) if n >= QT_N else ():
                        act.wait_ge(dft, QT_N)
                        act.wait_ge(turned, b + 1)
                        to = m.a(HT0 + b * P, (KC - 1) * S + P)
                        to = bass.AP(tensor=to.tensor, offset=to.offset, ap=[to.ap[0], [S, KC], [1, P]])
                        nc.scalar.activation(to, m.bank(4 * (1 - s) + 2 * (b % 2), D)
                                             .rearrange("p (c t) -> p c t", c=KC), ACT.Copy).then_inc(copied, 1)
                    act.wait_ge(dft, n + 1)
                    odd_sums = m.bank(4 * s, 4 * BANK).rearrange("p (a b n) -> p a b n", a=2, b=2)
                    nc.scalar.activation(m.a(c0 + s * 2 * HW, 2 * HW).rearrange("p (a n) -> p a n", a=2),
                                         odd_sums[:, :, 1, :], ACT.Copy).then_inc(odd, 1)
                    act.wait_ge(k_ok, n + 1)
                    act.dma_start(k_dram[n], m.a(ko0 + s * FQ, FQ)).then_inc(k_out[s], 16)
                for s in range(2):
                    act.wait_ge(k_out[s], 16 * QT_N)

            @block.vector
            def _(dve):
                dve.wait_ge(squared, NB)
                nc.vector.tensor_scalar(rstd, m.a(ST0, NB), 1.0 / D, EPS, ALU.mult, ALU.add).then_inc(var_ok, 1)
                dve.wait_ge(rooted, 1)
                nc.vector.reciprocal(rstd, rstd).then_inc(inverted, 1)
                dve.wait_ge(inverted, 1)
                dve.wait_ge(g_in, 16)
                for n in range(2 * QT_N):
                    s = n % 2
                    for b in range(2 * (n - QT_N), 2 * (n - QT_N) + 2) if n >= QT_N else ():
                        if b >= 2:
                            dve.wait_ge(turned, b - 1)
                        nc.vector.scalar_tensor_tensor(
                            out=m.a(h0 + (b % 2) * D, D), in0=m.a(X0 + b * D, D), scalar=m.a(ST0 + 8 + b, 1),
                            in1=m.a(GB0, D), op0=ALU.mult, op1=ALU.mult).then_inc(normed, 1)
                    dve.wait_ge(odd, n + 1)
                    if n >= 2:
                        dve.wait_ge(k_out[s], 16 * (n // 2))
                    even = m.bank(4 * s, 4 * BANK).rearrange("p (a b n) -> p a b n", a=2, b=2)[:, :, 0, :]
                    odd_c = m.a(c0 + s * 2 * HW, 2 * HW).rearrange("p (a n) -> p a n", a=2)
                    k = m.a(ko0 + s * FQ, FQ).rearrange("p (a b n) -> p a b n", a=2, b=2)
                    nc.vector.tensor_tensor(k[:, :, 0, :], even, odd_c, ALU.add)
                    nc.vector.tensor_tensor(k[:, :, 1, :], even, odd_c, ALU.subtract).then_inc(k_ok, 1)


U0 = W0


HYW0 = W0 + 18 * S


def load_hyena_weights(m, eng, d, s, i):
    w = d["e_w_in"][0].rearrange("(c p) n -> p c n", p=P)
    eng.dma_start(m.a(HYW0 + s * KC * P, KC * P).rearrange("p (c n) -> p c n", c=KC),
                  w[:, :, bass.ds((2 * i + s) * P, P)]).then_inc(m.ahead["hyproj"][s], 16)


def hyena_project(nc, m, d):
    w0 = HYW0
    raw0 = U0 + 12 * S
    cw0 = raw0 + 2 * S
    assert cw0 + 48 <= w0
    with Phase(nc, "hyproj") as ph:
        cw_in = ph.sem("cw_in")
        w_in = m.ahead["hyproj"]
        summed, copied, conved, dve_s = ph.sem("summed"), ph.sem("copied"), ph.sem("conved"), ph.sem("dve")
        with ph.block() as block:
            @block.sync
            def _(sp):
                with nc.allow_non_contiguous_dma(reason="a few columns of taps and biases"):
                    for t in range(3):
                        sp.dma_start(m.a(cw0 + 12 * t, 12), d["e_conv_w"][0, t, :]
                                     .rearrange("(c p) -> p c", p=P)).then_inc(cw_in, 16)
                    sp.dma_start(m.a(cw0 + 36, 12), d["e_conv_b"][0]
                                 .rearrange("(c p) -> p c", p=P)).then_inc(cw_in, 16)
                with sp.Fori(1, 6) as i:
                    for s in range(2):
                        sp.wait_ge(summed, 2 * i + s + 1)
                        load_hyena_weights(m, sp, d, s, i)

            @block.tensor
            def _(pe):
                pe.sem_inc(summed, 2)
                with pe.Fori(0, 6) as i:
                    for s in range(2):
                        pe.wait_ge(w_in[s], 16 * i + 16)
                        pe.wait_ge(copied, 2 * i + s + 1)
                        for h in range(2):
                            for c in range(KC):
                                t = nc.tensor.matmul(m.bank(2 * s + h), m.a(w0 + (s * KC + c) * P, P),
                                                     m.a(HT0 + c * S + h * BANK, BANK),
                                                     start=(c == 0), stop=(c == KC - 1))
                        t.then_inc(summed, 1)

            @block.scalar
            def _(act):
                act.sem_inc(copied, 2)
                with act.Fori(0, 6) as i:
                    for s in range(2):
                        act.wait_ge(summed, 2 * i + s + 3)
                        act.wait_ge(conved, 2 * i + s + 1)
                        nc.scalar.activation(m.a(raw0 + s * S, S), m.bank(2 * s, S),
                                             ACT.Copy).then_inc(copied, 1)

            @block.vector
            def _(dve):
                dve.sem_inc(conved, 2)
                dve.wait_ge(cw_in, 64)
                st = Steps(dve_s)
                with dve.Fori(0, 6) as i:
                    st.enter(i, 4)
                    for s in range(2):
                        b = 2 * i + s
                        tap = lambda t: m.dyn(cw0 + 12 * t + b, 1)
                        dve.wait_ge(copied, b + 3)
                        nc.vector.tensor_scalar(m.dyn(U0 + b * S, S), m.a(raw0 + s * S, S), tap(1), tap(3),
                                                ALU.mult, ALU.add).then_inc(dve_s, st.tick())
                        dve.wait_ge(dve_s, st.n)
                        left = m.dyn(U0 + b * S + 1, S - 1)
                        nc.vector.scalar_tensor_tensor(out=left, in0=m.a(raw0 + s * S, S - 1),
                                                       scalar=tap(0), in1=left, op0=ALU.mult,
                                                       op1=ALU.add).then_inc(dve_s, st.tick())
                        dve.wait_ge(dve_s, st.n)
                        right = m.dyn(U0 + b * S, S - 1)
                        nc.vector.scalar_tensor_tensor(out=right, in0=m.a(raw0 + s * S + 1, S - 1),
                                                       scalar=tap(2), in1=right, op0=ALU.mult,
                                                       op1=ALU.add).then_inc(conved, 1)
                    st.leave(6)


def long_conv(nc, m, d, o, k_dram, ahead=None):
    zt0 = U0 + 12 * S
    xs0 = zt0 + 8 * HW
    bias0 = xs0 + FQ
    odd0 = bias0 + 8
    t0 = odd0 + 2 * HW
    assert t0 + 4 * HW + FQ <= TOTAL
    pr0 = HT0
    f0, k0 = X0, X0 + 2 * FQ
    gq = [MT0, MT0 + FQ, t0 + 4 * HW, f0]
    with Phase(nc, f"conv{o}") as ph:
        b_in = ph.sem("b_in")
        f_in = [ph.sem("f_in0"), ph.sem("f_in1")]
        k_in = [ph.sem("k_in0"), ph.sem("k_in1")]
        g_in = [ph.pool_dma(m) for q in range(QT_N)]
        turned, time_ok, dft, odd = ph.sem("turned"), ph.sem("time_ok"), ph.sem("dft"), ph.sem("odd")
        xs_ok, y_ok, inv, gated, dve_s = ph.sem("xs_ok"), ph.sem("y_ok"), ph.sem("inv"), ph.sem("gated"), ph.sem("dve")
        with ph.block() as block:
            @block.sync
            def _(sp):
                with nc.allow_non_contiguous_dma(reason="a few columns of biases"):
                    sp.dma_start(m.a(bias0, 4), d["e_hy_bias"][0, o, :]
                                 .rearrange("(c p) -> p c", p=P)).then_inc(b_in, 16)
                with sp.Fori(0, QT_N // 2) as i:
                    for s in range(2):
                        sp.wait_ge(dft, 2 * i + s + 1)
                        sp.dma_start(m.a(f0 + s * FQ, FQ), d["c_dft"][bass.ds(2 * i + s, 1), :, :]
                                     .rearrange("a p n -> (a p) n")).then_inc(f_in[s], 16)
                        sp.wait_ge(y_ok, 2 * i + s + 1)
                        sp.dma_start(m.a(k0 + s * FQ, FQ), k_dram[bass.ds(4 * o + 2 * i + s, 1), :, :]
                                     .rearrange("a p n -> (a p) n")).then_inc(k_in[s], 16)
                if ahead is not None:
                    sp.wait_ge(y_ok, 2 + QT_N)
                    ahead(sp)

            @block.gpsimd
            def _(pool):
                for q in range(QT_N):
                    if q == QT_N - 1:
                        pool.wait_ge(dft, 2 + QT_N - 1)
                    pool.dma_start(m.a(gq[q], FQ), d["c_idft"][q]).then_inc(g_in[q], 16)

            @block.tensor
            def _(pe):
                pe.sem_inc(dft, 2)
                for j in range(8):
                    for c in range(4):
                        at = U0 + c * S + 2 * P * (j % 4) + j // 4
                        t = nc.tensor.transpose(m.bank(j, P, at=c * P), m.A[:, at:at + 2 * P - 1:2],
                                                m.ident())
                    t.then_inc(turned, 1)
                pe.wait_ge(time_ok, 8)
                with pe.Fori(0, QT_N // 2) as i:
                    for s in range(2):
                        pe.wait_ge(f_in[s], 16 * i + 16)
                        pe.wait_ge(xs_ok, 2 * i + s + 1)
                        for cs in range(2):
                            for par in range(2):
                                for j in range(4):
                                    t = nc.tensor.matmul(
                                        m.bank(4 * s + 2 * cs + par),
                                        m.a(f0 + s * FQ + ((2 * cs + par) * 4 + j) * P, P),
                                        m.a(zt0 + (4 * par + j) * HW, HW), start=(j == 0), stop=(j == 3))
                        t.then_inc(dft, 1)

                def inverse(q, c):
                    for par in range(2):
                        for cs in range(2):
                            t = nc.tensor.matmul(
                                m.bank(2 * c + par),
                                m.a(pr0 + q * FQ + (2 * cs + par) * HW + c * P, P),
                                m.a(gq[q] + (2 * cs + par) * HW, HW),
                                start=(q == 0 and cs == 0), stop=(q == QT_N - 1 and cs == 1))
                    return t

                for half in range(2):
                    for q in range(QT_N - 1):
                        pe.wait_ge(y_ok, 2 + QT_N - 1 + half)
                        if half == 0:
                            pe.wait_ge(g_in[q], 16)
                        for c in (2 * half, 2 * half + 1):
                            inverse(q, c)
                q = QT_N - 1
                pe.wait_ge(g_in[q], 16)
                for c in range(4):
                    inverse(q, c).then_inc(inv, 1)

            @block.scalar
            def _(act):
                for j in range(8):
                    act.wait_ge(turned, j + 1)
                    nc.scalar.activation(m.a(zt0 + j * HW, HW), m.bank(j), ACT.Copy).then_inc(time_ok, 1)
                with act.Fori(0, QT_N // 2) as i:
                    for s in range(2):
                        act.wait_ge(dft, 2 * i + s + 3)
                        act.wait_ge(xs_ok, 2 * i + s + 2)
                        odd_sums = m.bank(4 * s, 4 * BANK).rearrange("p (a b n) -> p a b n", a=2, b=2)
                        nc.scalar.activation(m.a(odd0, 2 * HW).rearrange("p (a n) -> p a n", a=2),
                                             odd_sums[:, :, 1, :], ACT.Copy).then_inc(odd, 1)

            @block.vector
            def _(dve):
                dve.sem_inc(xs_ok, 2)
                dve.sem_inc(y_ok, 2)
                st = Steps(dve_s)
                with dve.Fori(0, QT_N // 2) as i:
                    st.enter(i, 14)
                    for s in range(2):
                        dve.wait_ge(odd, 2 * i + s + 1)
                        even = m.bank(4 * s, 4 * BANK).rearrange("p (a b n) -> p a b n", a=2, b=2)[:, :, 0, :]
                        odd_c = m.a(odd0, 2 * HW).rearrange("p (a n) -> p a n", a=2)
                        x = m.a(xs0, FQ).rearrange("p (a b n) -> p a b n", a=2, b=2)
                        nc.vector.tensor_tensor(x[:, :, 0, :], even, odd_c, ALU.add).then_inc(dve_s, st.tick())
                        nc.vector.tensor_tensor(x[:, :, 1, :], even, odd_c, ALU.subtract).then_inc(xs_ok, 1)
                        dve.wait_ge(k_in[s], 16 * i + 16)
                        dve.wait_ge(dve_s, st.n)
                        dve.wait_ge(xs_ok, 2 * i + s + 3)
                        xc, xs = m.a(xs0, 2 * HW), m.a(xs0 + 2 * HW, 2 * HW)
                        kc, ks = m.a(k0 + s * FQ, 2 * HW), m.a(k0 + s * FQ + 2 * HW, 2 * HW)
                        ta, tb = m.a(t0, 2 * HW), m.a(t0 + 2 * HW, 2 * HW)
                        dve.wait_ge(y_ok, 2 * i + s + 2)
                        nc.vector.tensor_tensor(ta, xc, kc, ALU.mult).then_inc(dve_s, st.tick())
                        nc.vector.tensor_tensor(tb, xs, ks, ALU.mult).then_inc(dve_s, st.tick())
                        dve.wait_ge(dve_s, st.n)
                        nc.vector.tensor_tensor(xc, xc, ks, ALU.mult).then_inc(dve_s, st.tick())
                        nc.vector.tensor_tensor(xs, xs, kc, ALU.mult).then_inc(dve_s, st.tick())
                        dve.wait_ge(dve_s, st.n)
                        nc.vector.tensor_tensor(ta, ta, tb, ALU.subtract).then_inc(dve_s, st.tick())
                        dve.wait_ge(dve_s, st.n)
                        nc.vector.tensor_tensor(tb, xc, xs, ALU.add).then_inc(dve_s, st.tick())
                        dve.wait_ge(dve_s, st.n)
                        y = m.a(t0, FQ).rearrange("p (a b n) -> p a b n", a=2, b=2)
                        pr = m.dyn(pr0 + (2 * i + s) * FQ, FQ).rearrange("p (a b n) -> p a b n", a=2, b=2)
                        nc.vector.tensor_tensor(pr[:, :, 0, :], y[:, :, 0, :], y[:, :, 1, :], ALU.add)
                        nc.vector.tensor_tensor(pr[:, :, 1, :], y[:, :, 0, :], y[:, :, 1, :],
                                                ALU.subtract).then_inc(y_ok, 1)
                    st.leave(QT_N // 2)
                dve.wait_ge(b_in, 16)
                for c in range(4):
                    dve.wait_ge(inv, c + 1)
                    for par in range(2):
                        at = c * S + par
                        z = m.A[:, U0 + at:U0 + at + S - 1:2]
                        g = m.A[:, U0 + (4 * o + 4) * S + at:U0 + (4 * o + 4) * S + at + S - 1:2]
                        to = z if o == 0 else m.A[:, MT0 + at:MT0 + at + S - 1:2]
                        tmp = m.a(t0 + (par * 2) * HW, HW)
                        nc.vector.scalar_tensor_tensor(out=tmp, in0=z, scalar=m.a(bias0 + c, 1),
                                                       in1=m.bank(2 * c + par), op0=ALU.mult,
                                                       op1=ALU.add).then_inc(dve_s, st.tick())
                        dve.wait_ge(dve_s, st.n)
                        nc.vector.tensor_tensor(to, tmp, g, ALU.mult).then_inc(gated, 1)
def load_diff_weights(m, eng, d, t, i):
    w = d["e_w_in"][0].rearrange("(c p) n -> p c n", p=P)
    eng.dma_start(m.a(W0 + t * KC * P, KC * P).rearrange("p (c n) -> p c n", c=KC),
                  w[:, :, bass.ds(i * P + (3 + t) * 512, P)]).then_inc(m.ahead["diff"][t], 16)


def diff_attention(nc, m, d, y_dram):
    w0 = W0
    q0 = w0 + 3 * KC * P
    k0, vt0, v0 = q0 + S, q0 + 2 * S, q0 + 3 * S
    mh0 = v0 + S
    MHN = 2 * S - P
    e0 = mh0 + MHN
    at0 = e0 + 4 * S
    oa0 = at0 + 2 * S
    sub0 = oa0 + S
    l0 = sub0 + P
    sm0 = l0 + 384
    sq0 = sm0 + 32
    zero0 = sq0 + P
    assert zero0 + D <= HYW0
    lam_init = 0.8 - 0.6 * float(np.exp(-0.3 * 0))
    SCALE = 64 ** -0.5
    with Phase(nc, "diff") as ph:
        loaded = ph.sem("loaded")
        w_in = m.ahead["diff"]
        proj = [ph.sem(f"proj{t}") for t in range(2)]
        q_ok, k_ok, v_half, vt_ok = ph.sem("q_ok"), ph.sem("k_ok"), ph.sem("v_half"), ph.sem("vt_ok")
        v_turned, v_ok = ph.sem("v_turned"), ph.sem("v_ok")
        dve_s, lam_s, lam_e = ph.sem("dve"), ph.sem("lam_s"), ph.sem("lam_e")
        scored, maxed, neg_ok, exped = ph.sem("scored"), ph.sem("maxed"), ph.sem("neg_ok"), ph.sem("exped")
        a_ok, a_turned, at_ok = ph.sem("a_ok"), ph.sem("a_turned"), ph.sem("at_ok")
        pv, o_ok, var_ok, rooted = ph.sem("pv"), ph.sem("o_ok"), ph.sem("var_ok"), ph.sem("rooted")
        normed, o_turned, mixed = ph.sem("normed"), ph.sem("o_turned"), ph.sem("mixed")
        passed = ph.sem("passed")
        zeroed, cleared = ph.sem("zeroed"), ph.pool_dma(m)
        with ph.block() as block:
            @block.gpsimd
            def _(pool):
                first = 2 * S // P
                nc.gpsimd.memset(m.a(zero0, D), 0.0).then_inc(zeroed, 1)
                pool.wait_ge(zeroed, 1)
                with pool.Fori(first, NBLK) as j:
                    pool.dma_start(y_dram[bass.ds(j * P, P), :], m.a(zero0, D)).then_inc(cleared, 16)
                pool.wait_ge(cleared, 16 * (NBLK - first))

            @block.sync
            def _(sp):
                sp.dma_start(m.a(l0, 256), row(d["e_lam"][0].rearrange("a n -> (a n)"))).then_inc(loaded, 16)
                sp.dma_start(m.a(sub0, P), row(d["e_subln"][0])).then_inc(loaded, 16)
                sp.dma_start(m.a(mh0, MHN), d["c_dist"]).then_inc(loaded, 16)
                with sp.Fori(1, 4) as i:
                    for t in range(3):
                        if t < 2:
                            sp.wait_ge(proj[t], i + 1)
                        else:
                            sp.wait_ge(v_half, 2 * i + 1)
                        load_diff_weights(m, sp, d, t, i)
                for s in range(2):
                    load_hyena_weights(m, sp, d, s, 0)

            @block.tensor
            def _(pe):
                for t in (*proj, v_half):
                    pe.sem_inc(t, 1)

                def project(t, bank, h):
                    for c in range(KC):
                        x = nc.tensor.matmul(m.bank(bank + h), m.a(w0 + (t * KC + c) * P, P),
                                             m.a(HT0 + c * S + h * BANK, BANK),
                                             start=(c == 0), stop=(c == KC - 1))
                    return x

                def queries(i):
                    pe.wait_ge(w_in[0], 16 * i + 16)
                    project(0, 4, 0)
                    project(0, 4, 1).then_inc(proj[0], 1)

                def scores(i, u, s):
                    pe.wait_ge(maxed, 16 * i + 2 * u + s + 1)
                    for h in range(2):
                        x = nc.tensor.matmul(m.bank(2 * s + h), m.a(q0 + u * P, P, 64 * s, 64 * s + 64),
                                             m.a(k0 + h * BANK, BANK, 64 * s, 64 * s + 64),
                                             start=True, stop=True)
                    x.then_inc(scored, 1)

                def pair(i):
                    pe.wait_ge(w_in[1], 16 * i + 16)
                    pe.wait_ge(o_ok, 8 * i + 1)
                    project(1, 6, 0)
                    project(1, 6, 1).then_inc(proj[1], 1)
                    pe.wait_ge(w_in[2], 16 * i + 16)
                    pe.wait_ge(q_ok, i + 1)
                    project(2, 4, 0).then_inc(v_half, 1)
                    pe.wait_ge(k_ok, i + 1)
                    pe.wait_ge(mixed, i + 1)
                    scores(i, 0, 0)
                    scores(i, 0, 1)
                    x = project(2, 4, 1)
                    x.then_inc(v_half, 1)
                    scores(i, 1, 0)
                    scores(i, 1, 1)
                    pe.wait_ge(vt_ok, 2 * i + 2)
                    for j in range(NB):
                        x = nc.tensor.transpose(m.bank(6, P, at=j * P), m.a(vt0 + j * P, P), m.ident())
                    x.then_inc(v_turned, 1)
                    for u in range(1, NB + 1):
                        if u < NB - 1:
                            scores(i, u + 1, 0)
                        pe.wait_ge(a_ok, 8 * i + u)
                        for j in range(NB):
                            x = nc.tensor.transpose(m.bank(4, P, at=j * P),
                                                    m.a(e0 + ((u - 1) % 2) * 2 * S + j * P, P), m.ident())
                        x.then_inc(a_turned, 1)
                        if u < NB - 1:
                            scores(i, u + 1, 1)
                        if u == 1:
                            pe.wait_ge(v_ok, i + 1)
                        pe.wait_ge(at_ok, 8 * i + u)
                        pe.wait_ge(o_ok, 8 * i + u)
                        for j in range(NB):
                            x = nc.tensor.matmul(m.bank(6, P),
                                                 m.a(at0 + ((u - 1) % 2) * S + j * P, P),
                                                 m.a(v0 + j * P, P), start=(j == 0), stop=(j == NB - 1))
                        x.then_inc(pv, 1)

                def turn_outputs(i):
                    pe.wait_ge(normed, i + 1)
                    pe.wait_ge(maxed, 16 * i + 18)
                    for u in range(NB):
                        x = nc.tensor.transpose(m.bank(2, P, at=u * P), m.a(oa0 + u * P, P), m.ident())
                    x.then_inc(o_turned, 1)

                queries(0)
                with pe.Fori(0, 3) as i:
                    pair(i)
                    queries(i + 1)
                    turn_outputs(i)
                pair(3)
                turn_outputs(3)

            @block.scalar
            def _(act):
                act.wait_ge(lam_s, 1)
                nc.scalar.activation(m.a(l0 + 370, 2), m.a(l0 + 368, 2), ACT.Exp).then_inc(lam_e, 1)
                act.sem_inc(mixed, 1)
                act.sem_inc(o_ok, 1)

                def queries(i):
                    act.wait_ge(proj[0], i + 2)
                    nc.scalar.activation(m.a(q0, S), m.bank(4, S), ACT.Copy).then_inc(q_ok, 1)

                def values(i, h):
                    act.wait_ge(v_half, 2 * i + h + 2)
                    nc.scalar.activation(m.a(vt0 + h * BANK, BANK), m.bank(4 + h), ACT.Copy).then_inc(vt_ok, 1)

                def exps(i, u):
                    for s in range(2):
                        e = m.a(e0 + (2 * (u % 2) + s) * S, S)
                        c = sm0 + 16 * (u % 2) + s
                        act.wait_ge(neg_ok, 16 * i + 2 * u + s + 1)
                        nc.scalar.activation(e, e, ACT.Exp, bias=m.a(c + 2, 1), scale=SCALE,
                                             accum_out=m.a(c + 4, 1)).then_inc(exped, 1)

                def pair(i):
                    act.wait_ge(proj[1], i + 2)
                    nc.scalar.activation(m.a(k0, S), m.bank(6, S), ACT.Copy).then_inc(k_ok, 1)
                    values(i, 0)
                    exps(i, 0)
                    values(i, 1)
                    act.wait_ge(v_turned, i + 1)
                    nc.scalar.activation(m.a(v0, S), m.bank(6, S), ACT.Copy).then_inc(v_ok, 1)
                    for u in range(1, NB + 1):
                        if u < NB:
                            exps(i, u)
                        act.wait_ge(a_turned, 8 * i + u)
                        nc.scalar.activation(m.a(at0 + ((u - 1) % 2) * S, S), m.bank(4, S),
                                             ACT.Copy).then_inc(at_ok, 1)
                        act.wait_ge(pv, 8 * i + u)
                        act.wait_ge(o_ok, 8 * i + u)
                        inv = m.a(sm0 + 16 * ((u - 1) % 2) + 6, 1)
                        nc.scalar.activation(m.a(sq0, P), m.bank(6, P), ACT.Square, scale=inv,
                                             accum_out=m.a(ST0 + 16 + u - 1, 1))
                        nc.scalar.activation(m.a(oa0 + (u - 1) * P, P), m.bank(6, P),
                                             ACT.Copy, scale=inv).then_inc(o_ok, 1)
                    act.wait_ge(var_ok, i + 1)
                    nc.scalar.activation(m.a(ST0 + 24, NB), m.a(ST0 + 24, NB), ACT.Sqrt).then_inc(rooted, 1)

                def turned_outputs(i):
                    act.wait_ge(o_turned, i + 1)
                    nc.scalar.activation(m.dyn(MT0 + 4 * S + i * S, S), m.bank(2, S),
                                         ACT.Copy).then_inc(mixed, 1)

                queries(0)
                with act.Fori(0, 3) as i:
                    pair(i)
                    queries(i + 1)
                    turned_outputs(i)
                pair(3)
                turned_outputs(3)

            @block.vector
            def _(dve):
                st = Steps(dve_s)

                def tick(x):
                    x.then_inc(dve_s, st.tick())
                    dve.wait_ge(dve_s, st.n)

                dve.sem_inc(maxed, 2)
                dve.wait_ge(loaded, 48)
                nc.vector.tensor_tensor(m.a(l0, 64), m.a(l0, 64), m.a(l0 + 64, 64), ALU.mult)
                tick(nc.vector.tensor_tensor(m.a(l0 + 128, 64), m.a(l0 + 128, 64), m.a(l0 + 192, 64), ALU.mult))
                nc.vector.reduce_sum(m.a(l0 + 368, 1), m.a(l0, 64), AX_X)
                nc.vector.reduce_sum(m.a(l0 + 369, 1), m.a(l0 + 128, 64), AX_X).then_inc(lam_s, 1)
                dve.wait_ge(lam_e, 1)
                neg_lam = m.a(l0 + 372, 1)
                nc.vector.tensor_scalar(m.a(sub0, P), m.a(sub0, P), 1.0 - lam_init, None, ALU.mult)
                tick(nc.vector.tensor_tensor(neg_lam, m.a(l0 + 371, 1), m.a(l0 + 370, 1), ALU.subtract))
                tick(nc.vector.tensor_scalar(neg_lam, neg_lam, -lam_init, None, ALU.add))

                def scores(i, u):
                    for s in range(2):
                        c = sm0 + 16 * (u % 2) + s
                        dve.wait_ge(scored, 16 * i + 2 * u + s + 1)
                        if s == 0 and u >= 2:
                            dve.wait_ge(a_turned, 8 * i + u - 1)
                        dve.sem_inc(passed, 1)
                        nc.vector.tensor_tensor_reduce(
                            m.a(e0 + (2 * (u % 2) + s) * S, S), m.a(mh0 + (NB - 1 - u) * P, S),
                            m.bank(2 * s, S), 1.0, -3.0e38, ALU.add, ALU.max,
                            m.a(c, 1)).then_inc(maxed, 1)
                        dve.wait_ge(maxed, 16 * i + 2 * u + s + 3)
                        nc.vector.tensor_scalar(m.a(c + 2, 1), m.a(c, 1), -SCALE, None,
                                                ALU.mult).then_inc(neg_ok, 1)

                def difference(i, u):
                    c = sm0 + 16 * (u % 2)
                    ea = e0 + 2 * (u % 2) * S
                    dve.wait_ge(exped, 16 * i + 2 * u + 2)
                    if u >= 2:
                        dve.wait_ge(o_ok, 8 * i + u)
                    tick(nc.vector.reciprocal(m.a(c + 6, 2), m.a(c + 4, 2)))
                    tick(nc.vector.tensor_scalar(m.a(c + 8, 1), m.a(c + 7, 1), m.a(c + 4, 1), neg_lam,
                                                 ALU.mult, ALU.mult))
                    nc.vector.scalar_tensor_tensor(out=m.a(ea, S), in0=m.a(ea + S, S),
                                                   scalar=m.a(c + 8, 1), in1=m.a(ea, S),
                                                   op0=ALU.mult, op1=ALU.add).then_inc(a_ok, 1)

                def pair(i):
                    tick(nc.vector.tensor_scalar(m.a(mh0, MHN), m.a(mh0, MHN), 0.25, None, ALU.mult))
                    scores(i, 0)
                    for u in range(1, NB + 1):
                        if u < NB:
                            scores(i, u)
                        difference(i, u - 1)
                    dve.wait_ge(o_ok, 8 * i + 9)
                    nc.vector.tensor_scalar(m.a(ST0 + 24, NB), m.a(ST0 + 16, NB), 1.0 / P, EPS,
                                            ALU.mult, ALU.add).then_inc(var_ok, 1)
                    dve.wait_ge(rooted, i + 1)
                    tick(nc.vector.reciprocal(m.a(ST0 + 24, NB), m.a(ST0 + 24, NB)))
                    for u in range(NB):
                        o = m.a(oa0 + u * P, P)
                        x = nc.vector.scalar_tensor_tensor(out=o, in0=o, scalar=m.a(ST0 + 24 + u, 1),
                                                           in1=m.a(sub0, P), op0=ALU.mult, op1=ALU.mult)
                    x.then_inc(normed, 1)
                    tick(nc.vector.memset(m.a(sm0 + 31, 1), 0.0))

                with dve.Fori(0, 3) as i:
                    st.enter(i, 1 + NB * 2 + 1 + 1)
                    pair(i)
                    st.leave(3)
                pair(3)


GQW0 = W0 + 18 * S


def load_window_weights(m, eng, d, t, i):
    w = d["o_w_in"][0].rearrange("(c p) n -> p c n", p=P)
    to = m.a(GQW0 + t * KC * P, KC * P).rearrange("p (c n) -> p c n", c=KC)
    if t < 4:
        for g in range(2):
            n = i * 512 + g * 256 + t * 64
            eng.dma_start(to[:, :, 64 * g:64 * g + 64], w[:, :, n:n + 64]).then_inc(m.ahead["gqa"][t], 16)
    else:
        n = i * P + 1024 + (t - 4) * 256
        eng.dma_start(to, w[:, :, n:n + P]).then_inc(m.ahead["gqa"][t], 16)


def window_attention(nc, m, d, ahead):
    HD, HG, WINW = 64, 4, 3 * P
    NT = HG + 2
    w0 = GQW0
    q0 = W0
    k0 = q0 + HG * S
    v0 = k0 + S
    mh0 = v0 + S
    e0 = mh0 + 2 * HG * WINW
    pt0 = e0 + 2 * 8 * WINW
    oa0 = pt0 + 2 * 2 * WINW
    sk0 = oa0 + 2 * 4 * P
    sm0 = sk0 + 32
    assert sm0 + 128 <= w0 and w0 + NT * KC * P <= TOTAL
    SCALE = HD ** -0.5
    STEPS = 2 * HG

    def keys(u):
        return max(u - 1, 0), min(u + 1, NB - 1)

    with Phase(nc, "gqa") as ph:
        loaded = ph.sem("loaded")
        w_in = m.ahead["gqa"]
        proj = [ph.sem(f"proj{t}") for t in range(NT)]
        qkv_ok, v_turned, v_ok = ph.sem("qkv_ok"), ph.sem("v_turned"), ph.sem("v_ok")
        dve_s, scored, maxed, neg_ok = ph.sem("dve"), ph.sem("scored"), ph.sem("maxed"), ph.sem("neg_ok")
        exped, p_turned, pt_ok, pv = ph.sem("exped"), ph.sem("p_turned"), [ph.sem("pt_ok0"), ph.sem("pt_ok1")], ph.sem("pv")
        o_ok, o_turned, mixed, sink_e = ph.sem("o_ok"), ph.sem("o_turned"), ph.sem("mixed"), ph.sem("sink_e")
        passed = ph.sem("passed")
        vt = q0
        with ph.block() as block:
            @block.sync
            def _(sp):
                sp.dma_start(m.a(sk0, 16), row(d["o_sink"][0])).then_inc(loaded, 16)
                sp.dma_start(m.a(mh0, 2 * HG * WINW), d["c_window"]).then_inc(loaded, 16)
                for t in (5, 4, 0, 2, 3, 1):
                    sp.wait_ge(proj[t], 2)
                    load_window_weights(m, sp, d, t, 1)
                for t in range(NT):
                    sp.wait_ge(proj[t], 3)
                ahead(sp)

            @block.tensor
            def _(pe):
                for t in range(NT):
                    pe.sem_inc(proj[t], 1)
                with pe.Fori(0, 2) as i:
                    def project(t, b):
                        pe.wait_ge(w_in[t], (32 if t < HG else 16) * (i + 1))
                        for h in range(2):
                            for c in range(KC):
                                x = nc.tensor.matmul(m.bank(b + h), m.a(w0 + (t * KC + c) * P, P),
                                                     m.a(HT0 + c * S + h * BANK, BANK),
                                                     start=(c == 0), stop=(c == KC - 1))
                        x.then_inc(proj[t], 1)

                    pe.wait_ge(mixed, 8 * i + 1)
                    project(5, 0)
                    project(4, 2)
                    project(0, 4)
                    pe.wait_ge(qkv_ok, 6 * i + 1)
                    for j in range(NB):
                        x = nc.tensor.transpose(m.bank(0, P, at=j * P), m.a(vt + j * P, P), m.ident())
                    x.then_inc(v_turned, 1)
                    pe.wait_ge(qkv_ok, 6 * i + 2)
                    project(2, 2)
                    pe.wait_ge(qkv_ok, 6 * i + 3)
                    project(3, 4)
                    pe.wait_ge(v_ok, i + 1)
                    pe.wait_ge(qkv_ok, 6 * i + 4)

                    def scores(n):
                        j, u0 = n // 2, 4 * (n % 2)
                        for u in range(u0, u0 + 4):
                            a, z = keys(u)
                            for s in range(2):
                                pe.wait_ge(maxed, 64 * i + 8 * n + 2 * (u - u0) + s + 1)
                                nc.tensor.matmul(m.bank(2 * (u % 2) + s, (z - a + 1) * P),
                                                 m.a(q0 + j * S + u * P, P, 64 * s, 64 * s + 64),
                                                 m.a(k0 + a * P, (z - a + 1) * P, 64 * s, 64 * s + 64),
                                                 start=True, stop=True).then_inc(scored, 1)

                    def turn_probs(n, u, s):
                        a, z = keys(u)
                        k = 8 * n + 2 * (u % 4) + s
                        pe.wait_ge(exped, 64 * i + k + 1)
                        pe.wait_ge(pt_ok[s], 32 * i + k // 2 + 1)
                        for b in range(z - a + 1):
                            x = nc.tensor.transpose(
                                m.bank(4 + s, P, at=b * P),
                                m.a(e0 + (n % 2) * 8 * WINW + (2 * (u % 4) + s) * WINW + b * P, P),
                                m.ident())
                        x.then_inc(p_turned, 1)

                    def weigh(n, u, s):
                        a, z = keys(u)
                        k = 8 * n + 2 * (u % 4) + s
                        pe.wait_ge(pt_ok[s], 32 * i + k // 2 + 2)
                        if k % 8 == 0:
                            pe.wait_ge(o_ok, 8 * i + n + 1)
                        for b in range(z - a + 1):
                            x = nc.tensor.matmul(
                                m.bank(6, HD, at=(u % 4) * P + s * HD),
                                m.a(pt0 + ((u % 2) * 2 + s) * WINW + b * P, P),
                                m.a(v0 + (a + b) * P + s * HD, HD),
                                start=(b == 0), stop=(b == z - a))
                        x.then_inc(pv, 1)

                    def outputs(n):
                        u0 = 4 * (n % 2)
                        for u in range(u0, u0 + 5):
                            for s in range(2):
                                if u < u0 + 4:
                                    turn_probs(n, u, s)
                                if u > u0:
                                    weigh(n, u - 1, s)

                    def turn_outputs(n):
                        pe.wait_ge(o_ok, 8 * i + n + 2)
                        pe.wait_ge(mixed, 8 * i + n + 1)
                        for u in range(4):
                            x = nc.tensor.transpose(m.bank(7, P, at=u * P),
                                                    m.a(oa0 + (n % 2) * 4 * P + u * P, P), m.ident())
                        x.then_inc(o_turned, 1)

                    scores(0)
                    project(1, 6)
                    scores(1)
                    pe.wait_ge(qkv_ok, 6 * i + 6)
                    for n in range(STEPS):
                        if 1 < n + 1 < STEPS:
                            scores(n + 1)
                        outputs(n)
                        if n >= 1:
                            turn_outputs(n - 1)
                    turn_outputs(STEPS - 1)

            @block.scalar
            def _(act):
                act.sem_inc(mixed, 1)
                act.sem_inc(pt_ok[0], 1)
                with act.Fori(0, 2) as i:
                    act.wait_ge(proj[5], i + 2)
                    nc.scalar.activation(m.a(vt, S), m.bank(0, S), ACT.Copy).then_inc(qkv_ok, 1)
                    act.wait_ge(proj[4], i + 2)
                    nc.scalar.activation(m.a(k0, S), m.bank(2, S), ACT.Copy).then_inc(qkv_ok, 1)
                    act.wait_ge(v_turned, i + 1)
                    nc.scalar.activation(m.a(v0, S), m.bank(0, S), ACT.Copy).then_inc(v_ok, 1)

                    def queries(t, b):
                        act.wait_ge(proj[t], i + 2)
                        nc.scalar.activation(m.a(q0 + t * S, S), m.bank(b, S), ACT.Copy).then_inc(qkv_ok, 1)

                    queries(0, 4)
                    queries(2, 2)
                    queries(3, 4)

                    def sink(n):
                        act.wait_ge(neg_ok, 8 * i + n + 1)
                        c = sm0 + 64 * (n % 2)
                        nc.scalar.activation(m.a(c + 24, 8), m.a(c + 24, 8), ACT.Exp).then_inc(sink_e, 1)

                    def exp(n, k):
                        u = 4 * (n % 2) + k // 2
                        a, z = keys(u)
                        c = sm0 + 64 * (n % 2)
                        e = m.a(e0 + (n % 2) * 8 * WINW + k * WINW, (z - a + 1) * P)
                        nc.scalar.activation(e, e, ACT.Exp, bias=m.a(c + 8 + k, 1), scale=SCALE,
                                             accum_out=m.a(c + 16 + k, 1)).then_inc(exped, 1)

                    def move(n, k):
                        u = 4 * (n % 2) + k // 2
                        a, z = keys(u)
                        act.wait_ge(p_turned, 64 * i + 8 * n + k + 1)
                        nc.scalar.activation(m.a(pt0 + (u % 2) * 2 * WINW, (z - a + 1) * P),
                                             m.bank(4, (z - a + 1) * P), ACT.Copy).then_inc(pt_ok[0], 1)

                    def mix(n):
                        act.wait_ge(o_turned, 8 * i + n + 1)
                        nc.scalar.activation(m.dyn(MT0 + i * 4 * S + (n // 2) * S + (n % 2) * BANK, BANK),
                                             m.bank(7), ACT.Copy).then_inc(mixed, 1)

                    sink(0)
                    for k in range(8):
                        exp(0, k)
                    queries(1, 6)
                    for n in range(STEPS):
                        for k in range(8):
                            if k % 2 == 0:
                                move(n, k)
                            if n + 1 < STEPS and k >= 1:
                                if k == 1:
                                    sink(n + 1)
                                exp(n + 1, k - 1)
                        if n + 1 < STEPS:
                            exp(n + 1, 7)
                        if n >= 1:
                            mix(n - 1)
                    mix(STEPS - 1)

            @block.vector
            def _(dve):
                st = Steps(dve_s)

                def tick(x):
                    x.then_inc(dve_s, st.tick())
                    dve.wait_ge(dve_s, st.n)

                dve.sem_inc(maxed, 4)
                dve.sem_inc(pt_ok[1], 1)
                dve.sem_inc(o_ok, 1)
                dve.wait_ge(loaded, 32)
                with dve.Fori(0, 2) as i:
                    st.enter(i, 2 + STEPS * 3)
                    tick(nc.vector.tensor_scalar(m.a(sk0 + 16, 8), m.dyn(sk0 + i * 8, 8), 1.0 / SCALE, None,
                                                 ALU.mult))

                    def head(n):
                        j, u0 = n // 2, 4 * (n % 2)
                        c = sm0 + 64 * (n % 2)
                        if n >= 2:
                            dve.wait_ge(p_turned, 64 * i + 8 * (n - 1))
                        for u in range(u0, u0 + 4):
                            a, z = keys(u)
                            for s in range(2):
                                k = 2 * (u - u0) + s
                                w = (z - a + 1) * P
                                dve.wait_ge(scored, 64 * i + 8 * n + k + 1)
                                dve.sem_inc(passed, 1)
                                nc.vector.tensor_tensor_reduce(
                                    m.a(e0 + (n % 2) * 8 * WINW + k * WINW, w),
                                    m.a(mh0 + (2 * j + s) * WINW + (a - u + 1) * P, w),
                                    m.bank(2 * (u % 2) + s, w), 1.0, -3.0e38, ALU.add, ALU.max,
                                    m.a(c + k, 1)).then_inc(maxed, 1)
                        dve.wait_ge(maxed, 64 * i + 8 * n + 8 + 4)
                        mx = m.a(c, 8).rearrange("p (u s) -> p u s", s=2)
                        for s in range(2):
                            x = nc.vector.tensor_scalar(mx[:, :, s], mx[:, :, s], m.a(sk0 + 16 + 4 * s + j, 1),
                                                        None, ALU.max)
                        tick(x)
                        for s in range(2):
                            x = nc.vector.tensor_scalar(m.a(c + 24, 8).rearrange("p (u s) -> p u s", s=2)[:, :, s],
                                                        mx[:, :, s], m.a(sk0 + 16 + 4 * s + j, 1), -SCALE,
                                                        ALU.subtract, ALU.mult)
                        nc.vector.tensor_scalar(m.a(c + 8, 8), m.a(c, 8), -SCALE, None,
                                                ALU.mult).then_inc(neg_ok, 1)

                    def moves(n):
                        for k in range(1, 8, 2):
                            u = 4 * (n % 2) + k // 2
                            a, z = keys(u)
                            dve.wait_ge(p_turned, 64 * i + 8 * n + k + 1)
                            nc.vector.tensor_copy(m.a(pt0 + ((u % 2) * 2 + 1) * WINW, (z - a + 1) * P),
                                                  m.bank(5, (z - a + 1) * P)).then_inc(pt_ok[1], 1)

                    def tail(n):
                        c = sm0 + 64 * (n % 2)
                        dve.wait_ge(exped, 64 * i + 8 * n + 8)
                        dve.wait_ge(sink_e, 8 * i + n + 1)
                        tick(nc.vector.tensor_tensor(m.a(c + 16, 8), m.a(c + 16, 8), m.a(c + 24, 8), ALU.add))
                        tick(nc.vector.reciprocal(m.a(c + 16, 8), m.a(c + 16, 8)))
                        dve.wait_ge(pv, 64 * i + 8 * n + 8)
                        nc.vector.tensor_tensor(
                            m.a(oa0 + (n % 2) * 4 * P, 4 * P).rearrange("p (k e) -> p k e", k=8),
                            m.bank(6, 4 * P).rearrange("p (k e) -> p k e", k=8),
                            m.a(c + 16, 8).rearrange("p (k o) -> p k o", o=1).to_broadcast([P, 8, HD]),
                            ALU.mult).then_inc(o_ok, 1)

                    head(0)
                    for n in range(STEPS):
                        if n + 1 < STEPS:
                            head(n + 1)
                        moves(n)
                        tail(n)
                    tick(nc.vector.tensor_scalar(m.a(mh0, 2 * HG * WINW), m.a(mh0, 2 * HG * WINW), 0.0625, None,
                                                 ALU.mult))
                    st.leave(2)
def load_cross_weights(m, eng, d, layer, h, t):
    w, n = ((d["c_wq"][layer], h), (d["c_wkv"][layer], h), (d["c_wkv"][layer], XH + h))[t]
    eng.dma_start(m.a(W0 + (3 * (h % 2) + t) * KC * P, KC * P).rearrange("p (c n) -> p c n", c=KC),
                  w.rearrange("(c p) n -> p c n", p=P)[:, :, n * P:(n + 1) * P])\
        .then_inc(m.ahead[f"cross{layer}"][3 * (h % 2) + t], 16)


def cross_attention(nc, m, d, layer, ahead):
    w0 = W0
    q0 = w0 + 6 * KC * P
    k0 = q0 + 2 * S
    v0 = k0 + 2 * M_LEN
    e0 = v0 + 2 * M_LEN
    pt0 = e0 + 2 * NB * M_LEN
    sm0 = pt0 + 2 * S
    assert sm0 + 48 <= CO_W[0]
    SCALE = 128 ** -0.5
    with Phase(nc, f"cross{layer}") as ph:
        w_in = [[m.ahead[f"cross{layer}"][3 * s + t] for s in range(2)] for t in range(3)]
        qp, kp, vp, kv_ok, q_ok = ph.sem("qp"), ph.sem("kp"), ph.sem("vp"), ph.sem("kv_ok"), ph.sem("q_ok")
        scored, neg_ok, exped, p_ok = ph.sem("scored"), ph.sem("neg_ok"), ph.sem("exped"), ph.sem("p_ok")
        p_turned, pt_ok, pv, mixed, dve_s = ph.sem("p_turned"), ph.sem("pt_ok"), ph.sem("pv"), ph.sem("mixed"), ph.sem("dve")
        with ph.block() as block:
            @block.sync
            def _(sp):
                for h in range(2, XH):
                    for t in range(3):
                        sp.wait_ge((qp, kp, vp)[t], h - 1)
                        load_cross_weights(m, sp, d, layer, h, t)
                ahead(sp)

            @block.tensor
            def _(pe):
                def project(h):
                    s = h % 2
                    w = lambda t, c: w0 + ((3 * s + t) * KC + c) * P
                    for t in range(3):
                        pe.wait_ge(w_in[t][s], 16 * (h // 2 + 1))
                        if h >= 1 and t == 0:
                            pe.wait_ge(kv_ok, 2 * h)
                        if h >= 2 and t == 0:
                            pe.wait_ge(pt_ok, 2 * (h - 1))
                            pe.wait_ge(mixed, h - 1)
                        if t == 0:
                            for b in range(2):
                                for c in range(KC):
                                    x = nc.tensor.matmul(m.bank(b), m.a(w(0, c), P),
                                                         m.a(HT0 + c * S + b * BANK, BANK),
                                                         start=(c == 0), stop=(c == KC - 1))
                            x.then_inc(qp, 1)
                        elif t == 1:
                            for c in range(KC):
                                x = nc.tensor.matmul(m.bank(6, M_LEN), m.a(w(1, c), P),
                                                     m.a(ME0 + c * M_LEN, M_LEN),
                                                     start=(c == 0), stop=(c == KC - 1))
                            x.then_inc(kp, 1)
                        else:
                            for b in range(2):
                                for c in range(KC):
                                    x = nc.tensor.matmul(m.bank(7, P, at=b * P),
                                                         m.a(ME0 + c * M_LEN + b * P, P), m.a(w(2, c), P),
                                                         start=(c == 0), stop=(c == KC - 1))
                            x.then_inc(vp, 1)

                def scores(h):
                    s = h % 2
                    pe.wait_ge(q_ok, h + 1)
                    pe.wait_ge(kv_ok, 2 * h + 1)
                    if h >= 1:
                        pe.wait_ge(exped, h)
                    for u in range(NB):
                        x = nc.tensor.matmul(m.bank(2 + u // 2, M_LEN, at=(u % 2) * M_LEN),
                                             m.a(q0 + s * S + u * P, P), m.a(k0 + s * M_LEN, M_LEN),
                                             start=True, stop=True)
                    x.then_inc(scored, 1)

                def outputs(h):
                    s = h % 2
                    pe.wait_ge(p_ok, h + 1)
                    pe.wait_ge(kv_ok, 2 * min(h + 2, XH))
                    pe.wait_ge(q_ok, min(h + 2, XH))
                    if h >= 1:
                        pe.wait_ge(mixed, h)
                    for b in range(2):
                        for u in range(NB):
                            x = nc.tensor.transpose(m.bank(6 * b, P, at=u * P),
                                                    m.a(e0 + (s * NB + u) * M_LEN + b * P, P), m.ident())
                        x.then_inc(p_turned, 1)
                    pe.wait_ge(pt_ok, 2 * h + 2)
                    for half in range(2):
                        for b in range(2):
                            x = nc.tensor.matmul(m.bank(half), m.a(v0 + s * M_LEN + b * P, P),
                                                 m.a(pt0 + b * S + half * BANK, BANK),
                                                 start=(b == 0), stop=(b == 1))
                    x.then_inc(pv, 1)

                project(0)
                scores(0)
                for h in range(XH):
                    if h + 1 < XH:
                        project(h + 1)
                        scores(h + 1)
                    outputs(h)

            @block.scalar
            def _(act):
                def copies(h):
                    s = h % 2
                    act.wait_ge(qp, h + 1)
                    nc.scalar.activation(m.a(q0 + s * S, S), m.bank(0, S), ACT.Copy).then_inc(q_ok, 1)
                    act.wait_ge(kp, h + 1)
                    nc.scalar.activation(m.a(k0 + s * M_LEN, M_LEN), m.bank(6, M_LEN),
                                         ACT.Copy).then_inc(kv_ok, 1)
                    act.wait_ge(vp, h + 1)
                    nc.scalar.activation(m.a(v0 + s * M_LEN, M_LEN), m.bank(7, M_LEN),
                                         ACT.Copy).then_inc(kv_ok, 1)

                def exps(h):
                    s = h % 2
                    c = sm0 + 24 * s
                    act.wait_ge(neg_ok, h + 1)
                    for u in range(NB):
                        x = nc.scalar.activation(m.a(e0 + (s * NB + u) * M_LEN, M_LEN),
                                                 m.bank(2 + u // 2, M_LEN, at=(u % 2) * M_LEN), ACT.Exp,
                                                 bias=m.a(c + 8 + u, 1), scale=SCALE,
                                                 accum_out=m.a(c + 16 + u, 1))
                    x.then_inc(exped, 1)

                copies(0)
                exps(0)
                for h in range(XH):
                    if h + 1 < XH:
                        copies(h + 1)
                    for b in range(2):
                        act.wait_ge(p_turned, 2 * h + b + 1)
                        nc.scalar.activation(m.a(pt0 + b * S, S), m.bank(6 * b, S), ACT.Copy).then_inc(pt_ok, 1)
                    act.wait_ge(pv, h + 1)
                    nc.scalar.activation(m.a(MT0 + h * S, S), m.bank(0, S), ACT.Copy).then_inc(mixed, 1)
                    if h + 1 < XH:
                        exps(h + 1)

            @block.vector
            def _(dve):
                st = Steps(dve_s)

                def tick(x):
                    x.then_inc(dve_s, st.tick())
                    dve.wait_ge(dve_s, st.n)

                for h in range(XH):
                    s = h % 2
                    c = sm0 + 24 * s
                    dve.wait_ge(scored, h + 1)
                    tick(nc.vector.tensor_reduce(m.a(c, NB), m.bank(2, 4 * BANK)
                                                 .rearrange("p (u n) -> p u n", u=NB), AX_X, ALU.max))
                    nc.vector.tensor_scalar(m.a(c + 8, NB), m.a(c, NB), -SCALE, None, ALU.mult).then_inc(neg_ok, 1)
                    dve.wait_ge(exped, h + 1)
                    tick(nc.vector.reciprocal(m.a(c + 16, NB), m.a(c + 16, NB)))
                    e = m.a(e0 + s * NB * M_LEN, NB * M_LEN).rearrange("p (u n) -> p u n", u=NB)
                    r = m.a(c + 16, NB).rearrange("p (u o) -> p u o", o=1).to_broadcast([P, NB, M_LEN])
                    nc.vector.tensor_tensor(e, e, r, ALU.mult).then_inc(p_ok, 1)


MOE_W = W0
MOE_X = MOE_W + 2 * KC * EH
MOE_XT = MOE_X + 2 * D
MOE_HM = MOE_XT + 2 * D
MOE_HT = MOE_HM + 2 * EH
MOE_Y = MOE_HT + 2 * EH
MOE_IX = MOE_Y + 2 * D
MOE_END = MOE_IX + 2

SLOT0 = ST0 + 64
WT0 = ST0 + 80
TRIPS = ST0 + 100
BE0 = ST0 + 104


def route(nc, m, d, ph, block, layer, table, first_routed, routed, tabled, h_dram, x_in):
    at = MOE_END

    def room(n):
        nonlocal at
        at += n
        return at - n

    lg0 = room(NB * NR)
    iota0, tri0, tok0, one0, zero0 = room(2 * P), room(P), room(NB), room(P), room(NBLK)
    g80, gm0, gi0, gf0, goh0 = room(64), room(64), room(64), room(NB), room(NB * NG)
    es0, em0, ei0, tmp0 = room(64), room(64), room(64), room(64)
    ef0, gx0, gs0, ed0, den0 = room(2 * NB), room(NB * NG), room(NB), room(NB), room(NB)
    mk0, ms0, tot0, pre0, sl0, pick0 = room(512), room(256), room(256), room(256), room(256), room(512)
    cnt0, i1280, cmp0, nb0, pend0, pst0 = room(NE), room(NB), room(NE * NB), room(NE), room(NE), room(NE)
    ones0, le0, be0, tr0, slf0 = room(NE), room(NBLK * NE), room(NBLK), room(NBLK), room(2 * NB)
    tf0 = room(NB)
    assert at <= TOTAL
    hot0 = MOE_XT
    assert hot0 + 2 * 2 * NB * P <= MOE_Y

    def b3(ap, a, b):
        return ap.rearrange("p (a o) -> p a o", o=1).to_broadcast([P, a, b])

    def b2(ap, a, b):
        return ap.rearrange("p (o b) -> p o b", o=1).to_broadcast([P, a, b])

    def t3(ap, a):
        return ap.rearrange("p (a b) -> p a b", a=a)

    loaded, zeroed, cleared = ph.sem("loaded"), ph.sem("zeroed"), ph.sem("cleared")
    ex_in, ex_out, marked, counted = ph.sem("ex_in"), ph.sem("ex_out"), ph.sem("marked"), ph.sem("counted")
    hot_ok, found, first_ok = ph.sem("hot_ok"), ph.sem("found"), ph.sem("first_ok")
    slots_ok, scattered, dve_s = ph.sem("slots_ok"), ph.pool_dma(m), ph.sem("dve")
    @block.sync
    def _(sp):
        sp.dma_start(m.a(iota0, 2 * P), d["c_iota"]).then_inc(loaded, 16)
        sp.dma_start(m.a(tri0, P), d["c_tri"]).then_inc(loaded, 16)
        sp.dma_start(m.a(tok0, NB).bitcast(I32), d["c_tok"]).then_inc(loaded, 16)
        sp.wait_ge(zeroed, 1)
        sp.dma_start(table.rearrange("(p n) o -> p (n o)", p=P),
                     m.a(zero0, NBLK).bitcast(I32)).then_inc(cleared, 16)
        sp.wait_ge(cleared, 16)

    @block.gpsimd
    def _(pool):
        nc.gpsimd.memset(m.a(one0, P), 1.0)
        nc.gpsimd.memset(m.a(zero0, NBLK), 0.0).then_inc(zeroed, 1)
        pool.wait_ge(cleared, 16)
        pool.wait_ge(slots_ok, 1)
        pool.wait_ge(loaded, 48)
        for k in range(2):
            for b in range(NB):
                pool.indirect_dma_start(
                    table, bass.IndirectOffsetOnAxis(ap=m.a(SLOT0 + 8 * k + b, 1).bitcast(U32), axis=0),
                    m.a(tok0 + b, 1).bitcast(I32), None).then_inc(scattered, 16)
            pool.wait_ge(first_ok, k + 1)
            pool.indirect_dma_start(
                m.a(MOE_X + k * D, D), None, h_dram,
                bass.IndirectOffsetOnAxis(ap=m.a(MOE_IX + k, 1).bitcast(U32), axis=0)).then_inc(x_in[k], 16)
        pool.wait_ge(scattered, 16 * 2 * NB)
        pool.sem_inc(tabled, 1)

    @block.tensor
    def _(pe):
        pe.wait_ge(loaded, 48)
        pe.wait_ge(marked, 1)
        pe.wait_ge(zeroed, 1)
        nc.tensor.matmul(m.bank(1, 256), m.a(tri0, P), m.a(ms0, 256), start=True, stop=True)
        nc.tensor.matmul(m.bank(2, 256), m.a(one0, P), m.a(ms0, 256), start=True,
                         stop=True).then_inc(counted, 1)
        for j in range(2):
            pe.wait_ge(hot_ok, j + 1)
            for n in range(2 * NB):
                x = nc.tensor.matmul(m.bank(7 - j, 1), m.a(hot0 + (j * 2 * NB + n) * P, P),
                                     m.a(tf0 + n % NB, 1), start=(n == 0), stop=(n == 2 * NB - 1))
            x.then_inc(found, 1)

    @block.scalar
    def _(act):
        act.wait_ge(ex_in, 1)
        nc.scalar.activation(m.a(gx0, NB * NG), m.a(gx0, NB * NG), ACT.Exp)
        nc.scalar.activation(m.a(ed0, NB), m.a(ed0, NB), ACT.Exp).then_inc(ex_out, 1)

    @block.vector
    def _(dve):
        st = Steps(dve_s)
        v = nc.vector

        def tick(x):
            x.then_inc(dve_s, st.tick())
            dve.wait_ge(dve_s, st.n)

        v.memset(m.a(g80, 64), -3.0e38)
        lg = t3(m.a(lg0, NB * NR), NB)
        tick(v.tensor_tensor(lg, t3(m.bank(ROUTE_BANK, NB * NR), NB), b2(m.a(RBIAS, NR), NB, NR), ALU.add))
        tick(v.tensor_copy(t3(m.a(g80, 64), NB)[:, :, 0:NG], lg[:, :, 0:NG]))
        for b in range(NB):
            x = v.max(m.a(gm0 + 8 * b, 8), m.a(g80 + 8 * b, 8))
        tick(x)
        for b in range(NB):
            x = v.max_index(m.a(gi0 + 8 * b, 8).bitcast(U32), m.a(gm0 + 8 * b, 8), m.a(g80 + 8 * b, 8))
        tick(x)
        gm = t3(m.a(gm0, 64), NB)[:, :, 0:1]
        dve.wait_ge(loaded, 48)
        v.tensor_copy(m.a(tf0, NB), m.a(tok0, NB).bitcast(I32))
        tick(v.tensor_copy(m.a(gf0, NB), t3(m.a(gi0, 64), NB)[:, :, 0].bitcast(U32)))
        v.tensor_tensor(t3(m.a(gx0, NB * NG), NB), lg[:, :, 0:NG], gm.to_broadcast([P, NB, NG]),
                        ALU.subtract)
        tick(v.tensor_tensor(t3(m.a(goh0, NB * NG), NB), b3(m.a(gf0, NB), NB, NG),
                             b2(m.a(iota0, NG), NB, NG), ALU.is_equal))
        goh = t3(m.a(goh0, NB * NG), NB)
        es, tmp = t3(m.a(es0, 64), NB), t3(m.a(tmp0, 64), NB)
        for g in range(NG):
            part = lg[:, :, NG + EG * g:NG + EG * (g + 1)]
            tick(v.tensor_tensor(es if g == 0 else tmp, part,
                                 goh[:, :, g:g + 1].to_broadcast([P, NB, EG]), ALU.mult))
            if g:
                tick(v.tensor_tensor(es, es, tmp, ALU.add))
        for b in range(NB):
            x = v.max(m.a(em0 + 8 * b, 8), m.a(es0 + 8 * b, 8))
        tick(x)
        for b in range(NB):
            x = v.max_index(m.a(ei0 + 8 * b, 8).bitcast(U32), m.a(em0 + 8 * b, 8), m.a(es0 + 8 * b, 8))
        em = t3(m.a(em0, 64), NB)
        tick(x)
        v.tensor_tensor(m.a(ed0, NB), em[:, :, 1], em[:, :, 0], ALU.subtract).then_inc(ex_in, 1)
        for k in range(2):
            tick(v.tensor_copy(m.a(ef0 + k * NB, NB), t3(m.a(ei0, 64), NB)[:, :, k].bitcast(U32)))
            tick(v.scalar_tensor_tensor(out=m.a(ef0 + k * NB, NB), in0=m.a(gf0, NB), scalar=float(EG),
                                        in1=m.a(ef0 + k * NB, NB), op0=ALU.mult, op1=ALU.add))
            tick(v.tensor_tensor(t3(m.a(mk0 + 256 * k, 256), NB), b3(m.a(ef0 + k * NB, NB), NB, NE),
                                 b2(m.a(iota0, NE), NB, NE), ALU.is_equal))
        v.tensor_tensor(m.a(ms0, 256), m.a(mk0, 256), m.a(mk0 + 256, 256), ALU.add).then_inc(marked, 1)
        dve.wait_ge(ex_out, 1)
        tick(v.tensor_reduce(m.a(gs0, NB), t3(m.a(gx0, NB * NG), NB), AX_X, ALU.add))
        tick(v.scalar_tensor_tensor(out=m.a(den0, NB), in0=m.a(ed0, NB), scalar=1.0, in1=m.a(gs0, NB),
                                    op0=ALU.add, op1=ALU.mult))
        tick(v.reciprocal(m.a(WT0, NB), m.a(den0, NB)))
        v.tensor_tensor(m.a(WT0 + NB, NB), m.a(WT0, NB), m.a(ed0, NB), ALU.mult)
        dve.wait_ge(counted, 1)
        v.memset(m.a(pre0, NE), 0.0)
        tick(v.tensor_copy(m.a(tot0, 256), m.bank(2, 256)))
        for b in range(1, NB + 1):
            to = cnt0 if b == NB else pre0 + b * NE
            tick(v.tensor_tensor(m.a(to, NE), m.a(pre0 + (b - 1) * NE, NE),
                                 m.a(tot0 + (b - 1) * NE, NE), ALU.add))
        v.tensor_tensor(m.a(sl0, 256), m.a(pre0, 256), m.bank(1, 256), ALU.add)
        tick(v.tensor_scalar(m.a(i1280, NB), m.a(iota0, NB), float(P), None, ALU.mult))
        tick(v.tensor_tensor(t3(m.a(cmp0, NE * NB), NE), b3(m.a(cnt0, NE), NE, NB),
                             b2(m.a(i1280, NB), NE, NB), ALU.is_gt))
        v.memset(m.a(ones0, NE), 1.0)
        tick(v.tensor_reduce(m.a(nb0, NE), t3(m.a(cmp0, NE * NB), NE), AX_X, ALU.add))
        tick(v.tensor_tensor_scan(m.a(pend0, NE), m.a(ones0, NE), m.a(nb0, NE), 0.0, ALU.mult, ALU.add))

        def block_experts(j, z):
            n = z - j
            tick(v.tensor_tensor(t3(m.a(le0, n * NE), n), b2(m.a(pend0, NE), n, NE),
                                 b3(m.a(iota0 + j, n), n, NE), ALU.is_le))
            tick(v.tensor_reduce(m.a(be0, n), t3(m.a(le0, n * NE), n), AX_X, ALU.add))
            tick(v.tensor_scalar(m.a(be0, n), m.a(be0, n), float(NE - 1), None, ALU.min))
            return v.tensor_copy(m.a(BE0 + j, n).bitcast(I32), m.a(be0, n))

        block_experts(0, 2).then_inc(first_routed, 1)
        tick(v.tensor_tensor(m.a(pst0, NE), m.a(pend0, NE), m.a(nb0, NE), ALU.subtract))
        tick(v.tensor_scalar(m.a(pst0, NE), m.a(pst0, NE), float(P), None, ALU.mult))
        tick(v.tensor_tensor(t3(m.a(sl0, 256), NB), t3(m.a(sl0, 256), NB), b2(m.a(pst0, NE), NB, NE),
                             ALU.add))
        for k in range(2):
            tick(v.tensor_tensor(m.a(pick0 + 256 * k, 256), m.a(mk0 + 256 * k, 256), m.a(sl0, 256),
                                 ALU.mult))
        tick(v.tensor_reduce(m.a(slf0, 2 * NB), t3(m.a(pick0, 512), 2 * NB), AX_X, ALU.add))
        v.tensor_copy(m.a(SLOT0, 2 * NB).bitcast(U32), m.a(slf0, 2 * NB)).then_inc(slots_ok, 1)
        def hot(j):
            v.tensor_tensor(t3(m.a(hot0 + j * 2 * NB * P, 2 * NB * P), 2 * NB), b3(m.a(slf0, 2 * NB), 2 * NB, P),
                            b2(m.a(iota0 + j * P, P), 2 * NB, P), ALU.is_equal).then_inc(hot_ok, 1)

        def first(j):
            dve.wait_ge(found, j + 1)
            v.tensor_copy(m.a(MOE_IX + j, 1).bitcast(U32), m.bank(7 - j, 1)).then_inc(first_ok, 1)

        hot(0)
        block_experts(2, NBLK)
        tick(v.tensor_tensor(m.a(tr0, NBLK // 2), m.a(pend0 + NE - 1, 1).to_broadcast([P, NBLK // 2]),
                             m.a(iota0, NBLK).rearrange("p (a b) -> p a b", b=2)[:, :, 0], ALU.is_gt))
        tick(v.tensor_reduce(m.a(cnt0, 1), m.a(tr0, NBLK // 2), AX_X, ALU.add))
        v.tensor_copy(m.a(TRIPS, 1).bitcast(I32), m.a(cnt0, 1)).then_inc(routed, 1)
        first(0)
        hot(1)
        first(1)


def experts(nc, m, d, ph, block, layer, table, h_dram, y_dram, first_routed, routed, tabled, outputs_in, ahead, x_in):
    WE = KC * EH
    w0 = HT0
    assert w0 + 4 * WE <= ID0
    w2 = MOE_W
    wat = [[w0, w0 + WE, w0 + 2 * WE], [w0 + 3 * WE, w2, w2 + WE]]
    x0, xt0, hm0, ht0, y0, ix0 = MOE_X, MOE_XT, MOE_HM, MOE_HT, MOE_Y, MOE_IX
    HC = EH // P
    w_aps = (d["f_w_gate"].rearrange("l e (p c) n -> (l e) p (c n)", p=P),
             d["f_w_up"].rearrange("l e (p c) n -> (l e) p (c n)", p=P),
             d["f_w_down"].rearrange("l e (p c) n -> (l e) p (c n)", p=P))
    trips_ap = m.a(TRIPS, 1, 0, 1).bitcast(I32)
    w_in = [[ph.sem(f"w{t}_in{s}") for s in range(2)] for t in range(3)]
    gated, upped, downed = ph.sem("gated"), ph.sem("upped"), ph.sem("downed")
    ix_in = [ph.pool_dma(m), ph.pool_dma(m)]
    x_turned, xt_ok, silu, hm_ok = ph.sem("x_turned"), ph.sem("xt_ok"), ph.sem("silu"), ph.sem("hm_ok")
    h_turned, ht_ok, y_ok = ph.sem("h_turned"), ph.sem("ht_ok"), ph.sem("y_ok")
    y_out, passed = [ph.sem("y_out0"), ph.sem("y_out1")], ph.sem("passed")
    @block.sync
    def _(sp):
        sp.wait_ge(first_routed, 1)

        def load(i, s, first=False):
            e = sp.value_load(m.dyn(BE0 + 2 * i + s, 1, 0, 1).bitcast(I32), min_val=0, max_val=NE - 1)
            for t, used in enumerate((gated, upped, downed)):
                if not first:
                    sp.wait_ge(used, 2 * i + s + 1)
                sp.dma_start(m.a(wat[s][t], WE), w_aps[t][bass.ds(e + layer * NE, 1), :, :]
                             .rearrange("a p n -> (a p) n")).then_inc(w_in[t][s], 16)
                if first and s == 0 and t == 1:
                    sp.wait_ge(x_in[0], 16)

        load(0, 0, first=True)
        load(0, 1, first=True)
        sp.wait_ge(routed, 1)
        trips = sp.value_load(trips_ap, min_val=8, max_val=NBLK // 2)
        with sp.Fori(1, trips) as i:
            for s in range(2):
                load(i, s)
        if ahead is not None:
            ahead(sp)

    @block.gpsimd
    def _(pool):
        pool.wait_ge(routed, 1)
        pool.wait_ge(tabled, 1)
        trips = pool.value_load(trips_ap, min_val=8, max_val=NBLK // 2)
        with pool.Fori(1, trips) as i:
            for s in range(2):
                pool.wait_ge(x_turned, 2 * i + s + 1)
                pool.dma_start(m.a(ix0 + s, 1).bitcast(I32),
                               table[bass.ds((2 * i + s) * P, P), :]).then_inc(ix_in[s], 16)
                pool.wait_ge(ix_in[s], 16 * i)
                pool.sem_inc(passed, 1)
                pool.indirect_dma_start(
                    m.a(x0 + s * D, D), None, h_dram,
                    bass.IndirectOffsetOnAxis(ap=m.a(ix0 + s, 1).bitcast(U32), axis=0))\
                    .then_inc(x_in[s], 16)

    @block.tensor
    def _(pe):
        pe.wait_ge(routed, 1)
        trips = pe.value_load(trips_ap, min_val=8, max_val=NBLK // 2)
        for q in (gated, upped, downed, x_turned):
            pe.sem_inc(q, 2)

        def turn_x(n, s, i):
            pe.wait_ge(x_in[s], 16 * i + 16)
            pe.wait_ge(xt_ok, n + 1)
            for c in range(KC):
                x = nc.tensor.transpose(m.bank(0, P, at=c * P),
                                        m.A[:, x0 + s * D + c:x0 + (s + 1) * D:KC], m.ident())
            x.then_inc(x_turned, 1)

        def gate_up(n, s, i):
            pe.wait_ge(xt_ok, n + 2)
            for t, b, done in ((0, 2, gated), (1, 3, upped)):
                pe.wait_ge(w_in[t][s], 16 * i + 16)
                pe.wait_ge((silu, hm_ok)[t], n + 1)
                for c in range(KC):
                    x = nc.tensor.matmul(m.bank(b), m.a(xt0 + s * D + c * P, P),
                                         m.a(wat[s][t] + c * EH, EH),
                                         start=(c == 0), stop=(c == KC - 1))
                x.then_inc(done, 1)

        def turn_h(n, s):
            pe.wait_ge(hm_ok, n + 2)
            pe.wait_ge(ht_ok, n + 1)
            for c in range(HC):
                x = nc.tensor.transpose(m.bank(4, P, at=c * P),
                                        m.A[:, hm0 + s * EH + c:hm0 + (s + 1) * EH:HC], m.ident())
            x.then_inc(h_turned, 1)

        def down(n, s, i):
            pe.wait_ge(ht_ok, n + 2)
            pe.wait_ge(w_in[2][s], 16 * i + 16)
            pe.wait_ge(y_ok, n + 2)
            for h in range(2):
                for c in range(HC):
                    x = nc.tensor.matmul(m.bank(5 + h), m.a(ht0 + s * EH + c * P, P),
                                         m.a(wat[s][2] + c * D + h * BANK, BANK),
                                         start=(c == 0), stop=(c == HC - 1))
            x.then_inc(downed, 1)

        turn_x(0, 0, 0)
        gate_up(0, 0, 0)
        turn_x(1, 1, 0)
        turn_h(0, 0)
        with pe.Fori(0, trips - 1) as i:
            gate_up(2 * i + 1, 1, i)
            turn_x(2 * i + 2, 0, i + 1)
            down(2 * i, 0, i)
            turn_h(2 * i + 1, 1)
            gate_up(2 * i + 2, 0, i + 1)
            turn_x(2 * i + 3, 1, i + 1)
            down(2 * i + 1, 1, i)
            turn_h(2 * i + 2, 0)
        last = trips * 2 - 1
        gate_up(last, 1, trips - 1)
        down(last - 1, 0, trips - 1)
        turn_h(last, 1)
        down(last, 1, trips - 1)

    @block.scalar
    def _(act):
        act.wait_ge(routed, 1)
        trips = act.value_load(trips_ap, min_val=8, max_val=NBLK // 2)
        for q in (xt_ok, silu, ht_ok):
            act.sem_inc(q, 1)
        act.sem_inc(y_ok, 2)
        for s in range(2):
            act.sem_inc(y_out[s], 16)

        def copy_x(n, s):
            act.wait_ge(x_turned, n + 3)
            nc.scalar.activation(m.a(xt0 + s * D, D), m.bank(0, D), ACT.Copy).then_inc(xt_ok, 1)

        def gate(n, s):
            act.wait_ge(gated, n + 3)
            act.wait_ge(h_turned, n + 1)
            nc.scalar.activation(m.a(hm0 + s * EH, EH), m.bank(2), ACT.Silu).then_inc(silu, 1)

        def copy_h(n, s):
            act.wait_ge(h_turned, n + 2)
            nc.scalar.activation(m.a(ht0 + s * EH, EH), m.bank(4), ACT.Copy).then_inc(ht_ok, 1)

        def store_y(n, s, i):
            act.wait_ge(downed, n + 3)
            act.wait_ge(y_out[s], 16 * i + 16)
            nc.scalar.activation(m.a(y0 + s * D, D), m.bank(5, D), ACT.Copy).then_inc(y_ok, 1)
            act.wait_ge(y_ok, n + 3)
            act.dma_start(y_dram[bass.ds(n * P, P), :], m.a(y0 + s * D, D)).then_inc(y_out[s], 16)

        copy_x(0, 0)
        gate(0, 0)
        copy_x(1, 1)
        copy_h(0, 0)
        with act.Fori(0, trips - 1) as i:
            gate(2 * i + 1, 1)
            copy_x(2 * i + 2, 0)
            store_y(2 * i, 0, i)
            copy_h(2 * i + 1, 1)
            gate(2 * i + 2, 0)
            copy_x(2 * i + 3, 1)
            store_y(2 * i + 1, 1, i)
            copy_h(2 * i + 2, 0)
        last = trips * 2 - 1
        gate(last, 1)
        store_y(last - 1, 0, trips - 1)
        copy_h(last, 1)
        store_y(last, 1, trips - 1)
        for s in range(2):
            act.wait_ge(y_out[s], trips * 16 + 16)
            act.sem_inc(outputs_in, 1)

    @block.vector
    def _(dve):
        dve.wait_ge(routed, 1)
        trips = dve.value_load(trips_ap, min_val=8, max_val=NBLK // 2)
        dve.sem_inc(hm_ok, 1)
        dve.sem_inc(h_turned, 1)
        with dve.Fori(0, trips) as i:
            for s in range(2):
                n = 2 * i + s
                dve.wait_ge(silu, n + 2)
                dve.wait_ge(upped, n + 3)
                h = m.a(hm0 + s * EH, EH)
                nc.vector.tensor_tensor(h, h, m.bank(3), ALU.mult).then_inc(hm_ok, 1)


def combine(nc, m, ph, block, y_dram, gain, out, outputs_in):
    NS = 8
    y0, sq0, h0 = MOE_W, MOE_XT, MOE_Y
    var0, rs0 = ST0 + 8, ST0 + 16
    y_in = [ph.pool_dma(m) for s in range(NS)]
    added, squared, g_in, var_ok = ph.sem("added"), ph.sem("squared"), ph.sem("g_in"), ph.sem("var_ok")
    rooted, inverted, normed = ph.sem("rooted"), ph.sem("inverted"), ph.sem("normed")
    turned, copied, stored = ph.sem("turned"), ph.sem("copied"), ph.sem("stored")

    @block.gpsimd
    def _(pool):
        pool.wait_ge(outputs_in, 2)
        for n in range(2 * NB):
            b, k = n // 2, n % 2
            if n >= NS:
                pool.wait_ge(added, n - NS + 1)
            pool.indirect_dma_start(
                m.a(y0 + (n % NS) * D, D), None, y_dram,
                bass.IndirectOffsetOnAxis(ap=m.a(SLOT0 + 8 * k + b, 1).bitcast(U32), axis=0))\
                .then_inc(y_in[n % NS], 16)

    @block.vector
    def _(dve):
        def mean_square(b):
            dve.wait_ge(squared, b + 1)
            nc.vector.tensor_scalar(m.a(var0 + b, 1), m.a(ST0 + b, 1), 1.0 / D, EPS,
                                    ALU.mult, ALU.add).then_inc(var_ok, 1)

        def normalise(b):
            dve.wait_ge(rooted, b + 1)
            nc.vector.reciprocal(m.a(rs0 + b, 1), m.a(var0 + b, 1)).then_inc(inverted, 1)
            dve.wait_ge(inverted, b + 1)
            if b == 0:
                dve.wait_ge(g_in, 16)
            to = X0 + b * D if out is not None else h0 + (b % 2) * D
            if out is None and b >= 2:
                dve.wait_ge(turned, b - 1)
            nc.vector.scalar_tensor_tensor(out=m.a(to, D), in0=m.a(X0 + b * D, D), scalar=m.a(rs0 + b, 1),
                                           in1=m.a(GB0, D), op0=ALU.mult, op1=ALU.mult).then_inc(normed, 1)

        for n in range(2 * NB):
            b, k = n // 2, n % 2
            dve.wait_ge(y_in[n % NS], 16 * (n // NS + 1))
            if k:
                dve.wait_ge(added, n)
            x = m.a(X0 + b * D, D)
            nc.vector.scalar_tensor_tensor(out=x, in0=m.a(y0 + (n % NS) * D, D),
                                           scalar=m.a(WT0 + 8 * k + b, 1), in1=x,
                                           op0=ALU.mult, op1=ALU.add).then_inc(added, 1)
            if b >= 1:
                (normalise if k else mean_square)(b - 1)
        mean_square(NB - 1)
        normalise(NB - 1)

    @block.scalar
    def _(act):
        def copy(b):
            act.wait_ge(turned, b + 1)
            to = m.A[:, HT0 + b * P:HT0 + b * P + (KC - 1) * S + P]
            to = bass.AP(tensor=to.tensor, offset=to.offset, ap=[to.ap[0], [S, KC], [1, P]])
            nc.scalar.activation(to, m.bank(2 * (b % 2), D).rearrange("p (c t) -> p c t", c=KC),
                                 ACT.Copy).then_inc(copied, 1)

        for b in range(NB):
            act.wait_ge(added, 2 * b + 2)
            if b >= 2:
                act.wait_ge(squared, b - 1)
            nc.scalar.activation(m.a(sq0 + (b % 2) * D, D), m.a(X0 + b * D, D), ACT.Square,
                                 accum_out=m.a(ST0 + b, 1)).then_inc(squared, 1)
            act.wait_ge(var_ok, b + 1)
            nc.scalar.activation(m.a(var0 + b, 1), m.a(var0 + b, 1), ACT.Sqrt).then_inc(rooted, 1)
            if out is None and b >= 2:
                copy(b - 2)
        if out is None:
            copy(NB - 2)
            copy(NB - 1)

    if out is None:
        @block.tensor
        def _(pe):
            for b in range(NB):
                pe.wait_ge(normed, b + 1)
                if b >= 2:
                    pe.wait_ge(copied, b - 1)
                for c in range(KC):
                    x = nc.tensor.transpose(m.bank(2 * (b % 2), P, at=c * P),
                                            m.a(h0 + (b % 2) * D + c * P, P), m.ident())
                x.then_inc(turned, 1)

    @block.sync
    def _(sp):
        sp.dma_start(m.a(GB0, D), row(gain)).then_inc(g_in, 16)
        if out is not None:
            for b in range(NB):
                sp.wait_ge(normed, b + 1)
                sp.dma_start(out[0, b * P:(b + 1) * P, :], m.a(X0 + b * D, D)).then_inc(stored, 16)
            sp.wait_ge(stored, 16 * NB)


def mixture(nc, m, d, layer, table, h_dram, y_dram, gain, out=None, ahead=None):
    with Phase(nc, f"moe{layer}") as ph:
        first_routed = ph.sem("first_routed")
        routed, tabled, outputs_in = ph.sem("routed"), ph.sem("tabled"), ph.sem("outputs_in")
        x_in = [ph.pool_dma(m), ph.pool_dma(m)]
        with ph.block() as block:
            route(nc, m, d, ph, block, layer, table, first_routed, routed, tabled, h_dram, x_in)
            experts(nc, m, d, ph, block, layer, table, h_dram, y_dram, first_routed, routed, tabled, outputs_in, ahead,
                    x_in)
            combine(nc, m, ph, block, y_dram, gain, out, outputs_in)


def program(nc, d, out, stop=None):
    def scratch(name, shape, dt=F32):
        return nc.dram_tensor(name, shape, dt, kind="Internal").ap()

    spectra = scratch("spectra", (2 * QT_N, P, FQ))
    h_dram = scratch("h_tokens", (S, D))
    y_dram = scratch("y_slots", (NSLOT, D))
    table = scratch("slot_table", (NSLOT, 1), I32)

    def rows(w):
        return lambda c: [(0, P, w[c * P:(c + 1) * P, :])]

    w_o = d["o_w_out"][0].rearrange("(i s j e) n -> i j s e n", i=2, s=2, j=4)
    w_eout = rows(d["e_w_out"][0])

    def w_oout(c):
        return [(64 * s, 64 * s + 64, w_o[c // 4, c % 4, s]) for s in range(2)]

    def cross_ahead(layer):
        def load(eng):
            for h in range(2):
                for t in range(3):
                    load_cross_weights(m, eng, d, layer, h, t)
        return load

    def window_ahead(eng):
        for t in (5, 4, 0, 2, 3, 1):
            load_window_weights(m, eng, d, t, 0)

    steps = [
        lambda: begin(nc, m, d),
        lambda: filter_spectra(nc, m, d, spectra),
        lambda: diff_attention(nc, m, d, y_dram),
        lambda: hyena_project(nc, m, d),
        lambda: long_conv(nc, m, d, 0, spectra),
        lambda: long_conv(nc, m, d, 1, spectra, lambda eng: load_chunks(m, eng, "eout", w_eout, EO_W)),
        lambda: project_add(nc, m, "eout", w_eout, EO_W, EO_BUF, d["c_norm"][0], cross_ahead(0),
                            reload=d["x"][0]),
    ]
    for layer in range(2):
        if layer == 1:
            steps += [
                lambda: window_attention(nc, m, d, lambda eng: load_chunks(m, eng, "oout", w_oout, OO_W)),
                lambda: project_add(nc, m, "oout", w_oout, OO_W, OO_BUF, d["c_norm"][1], cross_ahead(1)),
            ]
        steps += [
            lambda L=layer: cross_attention(nc, m, d, L, lambda eng: load_chunks(
                m, eng, f"cout{L}", rows(d["c_wo"][L]), CO_W)),
            lambda L=layer: project_add(nc, m, f"cout{L}", rows(d["c_wo"][L]), CO_W, CO_BUF, d["f_norm"][L],
                                        h_dram=h_dram,
                                        router=((d["f_w_grp"][L], d["f_b_grp"][L], 0, NG),
                                                (d["f_w_exp"][L], d["f_b_exp"][L], NG, NR))),
            lambda L=layer: mixture(nc, m, d, L, table, h_dram, y_dram,
                                    *((d["o_norm"][0], None, window_ahead) if L == 0
                                      else (d["g_final"], out))),
        ]
    with ExitStack() as stack:
        m = Core(nc, stack)
        for step in steps[:stop]:
            step()


def constants():
    f8 = np.float64
    c = {"c_ident": np.eye(P)}
    pos = np.arange(S, dtype=np.float32)
    t = np.linspace(0.0, 1.0, S, dtype=np.float32)
    bands = np.linspace(1e-4, 15, 16, dtype=np.float32)
    ang = bands[None] * (2.0 * np.pi * pos[:, None] / S).astype(np.float32)
    c["c_pos"] = np.concatenate([t[:, None], np.cos(ang), -np.sin(ang)], axis=1).T
    deltas = np.linspace(np.log(1e-2) / 1.5, np.log(1e-2) / 0.3, HW, dtype=np.float32)
    decay = np.exp(-t[:, None] * np.abs(deltas)[None])
    c["c_decay"] = decay.reshape(4, P, 2, HW).transpose(1, 2, 0, 3).reshape(P, 8 * HW)
    c["c_sign"] = np.where(np.arange(P) < 64, 1.0, -1.0)[:, None]
    times = np.arange(S).reshape(4, P, 2)
    freq = (np.arange(S // 2) + 0.5).reshape(4, P)
    ang = np.pi * times[None, None].astype(f8) * freq[:, :, None, None, None] / S
    both = np.stack([np.cos(ang), np.sin(ang)])
    c["c_dft"] = both.transpose(1, 4, 0, 5, 3, 2).reshape(4, P, -1)
    c["c_idft"] = both.transpose(1, 2, 0, 5, 3, 4).reshape(4, P, -1) / S
    p = np.arange(P)[:, None]
    c["c_dist"] = -8.0 * np.abs(p - (np.arange(2 * S - P)[None] - (S - P)))
    rel = np.abs(p + P - np.arange(3 * P)[None])
    heads = np.array([[s * 4 + j for s in range(2)] for j in range(4)]).reshape(8, 1, 1)
    slopes = 2.0 ** (-8.0 * (heads + 1) / 16)
    c["c_window"] = np.where(rel[None] <= P, -8.0 * slopes * rel[None], -1e30).transpose(1, 0, 2).reshape(P, -1)
    c["c_iota"] = np.broadcast_to(np.arange(2 * P), (P, 2 * P))
    c["c_tri"] = np.triu(np.ones((P, P)), 1)
    out = {k: np.ascontiguousarray(v, dtype=np.float32) for k, v in c.items()}
    out["c_tok"] = np.ascontiguousarray((np.arange(NB)[None] * P + p).astype(np.int32))
    return out


_INS = ['x', 'mem', 'e_norm', 'e_w_in', 'e_conv_w', 'e_conv_b', 'e_filt_w1', 'e_filt_b1', 'e_filt_w2',
        'e_filt_b2', 'e_filt_w3', 'e_filt_freq', 'e_hy_bias', 'e_lam', 'e_subln', 'e_w_out', 'o_norm',
        'o_w_in', 'o_sink', 'o_w_out', 'c_norm', 'c_wq', 'c_wkv', 'c_wo', 'f_norm', 'f_w_grp', 'f_b_grp',
        'f_w_exp', 'f_b_exp', 'f_w_gate', 'f_w_up', 'f_w_down', 'g_mem', 'g_final']
STOP = None


def kernel(**inputs):
    import concourse.bacc as _bacc
    from concourse.bass_utils import run_bass_kernel_spmd as _run

    nc = _bacc.Bacc("TRN2", target_bir_lowering=False, num_devices=1)
    arrays = {f"in_{n}": np.ascontiguousarray(inputs[n]) for n in _INS}
    arrays.update({f"in_{n}": v for n, v in constants().items()})
    d = {n[3:]: nc.dram_tensor(n, v.shape, mybir.dt.from_np(v.dtype), kind="ExternalInput").ap()
         for n, v in arrays.items()}
    out = nc.dram_tensor("out_0", (1, S, D), F32, kind="ExternalOutput").ap()
    program(nc, d, out, STOP)
    r = _run(nc, [arrays], core_ids=[0])
    return r.results[0]["out_0"]
```
